# Optimizing a Trainium2 kernel written in Bass

```python
import math
import jax
import jax.numpy as jnp
from jax import lax
import numpy as np
import jax, jax.numpy as jnp

D_MODEL = 1024
BATCH = 1
SEQ = 256
DEPTH = 2

N_EVEN = (DEPTH + 1) // 2
N_ODD = DEPTH // 2
EPS = 1e-6
ROPE_THETA = 10000.0
Q_BLOCK = 128

GDN_HEADS = 4
GDN_DK = 128
GDN_DV = 128
GDN_CONV = 4
GDN_CHUNK = 64
GDN_QK = GDN_HEADS * GDN_DK
GDN_V = GDN_HEADS * GDN_DV
GDN_CONV_CH = 2 * GDN_QK + GDN_V
MOBA_HEADS = 4
MOBA_DH = 128
MOBA_BLOCK = 256
MOBA_TOPK = 3
MOBA_W = MOBA_HEADS * MOBA_DH
HY_SIZES = (GDN_CONV_CH, GDN_V, GDN_HEADS, GDN_HEADS, MOBA_W, MOBA_W, MOBA_W)
HY_IN = sum(HY_SIZES)
HY_SPLITS = tuple(int(i) for i in np.cumsum(HY_SIZES)[:-1])
HY_OUT = GDN_V + MOBA_W
MLA_HEADS = 8
MLA_Q_RANK = 512
MLA_KV_RANK = 256
MLA_NOPE = 128
MLA_ROPE = 64
MLA_V = 128
MLA_IN = MLA_Q_RANK + MLA_KV_RANK + MLA_ROPE
PEER_HEADS = 8
PEER_NKEYS = 128
PEER_EXPERTS = PEER_NKEYS * PEER_NKEYS
PEER_DKEY = 256
PEER_TOPK = 16
PEER_TOK_CHUNK = 128


def rmsnorm(x, w):
    xf = x.astype(jnp.float32)
    y = xf * lax.rsqrt(jnp.mean(xf * xf, axis=-1, keepdims=True) + EPS)
    return (y * w.astype(jnp.float32)).astype(x.dtype)

def l2norm(x):
    xf = x.astype(jnp.float32)
    return xf * lax.rsqrt(jnp.sum(xf * xf, axis=-1, keepdims=True) + EPS)

def rope_tables(positions, dim):
    inv_freq = ROPE_THETA ** (-jnp.arange(0, dim, 2, dtype=jnp.float32) / dim)
    ang = positions.astype(jnp.float32)[..., None] * inv_freq
    return jnp.cos(ang), jnp.sin(ang)

def apply_rope(x, cos, sin):
    x1, x2 = jnp.split(x.astype(jnp.float32), 2, axis=-1)
    c = cos[:, :, None, :]
    s = sin[:, :, None, :]
    return jnp.concatenate([x1 * c - x2 * s, x2 * c + x1 * s], axis=-1)

def causal_conv_silu(x, w):
    k_w = w.shape[0]
    s = x.shape[1]
    xp = jnp.pad(x, ((0, 0), (k_w - 1, 0), (0, 0)))
    y = xp[:, 0:s] * w[0]
    for j in range(1, k_w):
        y = y + xp[:, j:j + s] * w[j]
    return jax.nn.silu(y)

def unit_lower_inverse(l_strict):
    n = l_strict.shape[-1]
    eye = jnp.eye(n, dtype=l_strict.dtype)
    neg = -l_strict
    inv = eye + neg
    power = neg
    p = 2
    while p < n:
        power = power @ power
        inv = inv @ (eye + power)
        p *= 2
    return inv

def gated_delta_rule(q, k, v, g, beta):
    bsz, s, nh, dk = q.shape
    dv = v.shape[-1]
    cs = GDN_CHUNK
    nc = s // cs

    def to_chunks(t):
        t = t.reshape((bsz, nc, cs, nh) + t.shape[3:])
        return jnp.moveaxis(t, 3, 1)

    q = to_chunks(q * dk ** -0.5)
    k = to_chunks(k)
    v = to_chunks(v)
    beta = to_chunks(beta)
    g = jnp.cumsum(to_chunks(g), axis=-1)
    causal = jnp.tril(jnp.ones((cs, cs), dtype=bool))
    strict = jnp.tril(jnp.ones((cs, cs), dtype=bool), -1)
    decay = jnp.exp(jnp.where(causal, g[..., :, None] - g[..., None, :], -jnp.inf))
    k_beta = k * beta[..., None]
    l_strict = jnp.where(strict, jnp.einsum('bhncd,bhnmd->bhncm', k_beta, k) * decay, 0.0)
    t_inv = unit_lower_inverse(l_strict)
    u = t_inv @ (v * beta[..., None])
    w = t_inv @ (k_beta * jnp.exp(g)[..., None])
    qk = jnp.einsum('bhncd,bhnmd->bhncm', q, k) * decay
    q_dec = q * jnp.exp(g)[..., None]
    g_last = g[..., -1]
    k_dec = k * jnp.exp(g_last[..., None] - g)[..., None]

    def step(state, inp):
        qd, kd, uc, wc, qkc, gl = inp
        v_new = uc - jnp.einsum('bhck,bhkv->bhcv', wc, state)
        out = jnp.einsum('bhck,bhkv->bhcv', qd, state) + jnp.einsum('bhcm,bhmv->bhcv', qkc, v_new)
        state = state * jnp.exp(gl)[..., None, None] + jnp.einsum('bhck,bhcv->bhkv', kd, v_new)
        return state, out

    xs = tuple(jnp.moveaxis(t, 2, 0) for t in (q_dec, k_dec, u, w, qk, g_last))
    state0 = jnp.zeros((bsz, nh, dk, dv), jnp.float32)
    _, o = lax.scan(step, state0, xs)
    return jnp.transpose(o, (1, 0, 3, 2, 4)).reshape(bsz, s, nh, dv)

def moba_attention(q, k, v):
    bsz, s, nh, d = q.shape
    nb = -(-s // MOBA_BLOCK)
    pad = nb * MOBA_BLOCK - s
    topk = min(MOBA_TOPK, nb)
    qh = jnp.moveaxis(q, 2, 1) * d ** -0.5

    def to_blocks(t):
        t = jnp.pad(jnp.moveaxis(t, 2, 1), ((0, 0), (0, 0), (0, pad), (0, 0)))
        return t.reshape(bsz, nh, nb, MOBA_BLOCK, d)

    k_blk = to_blocks(k)
    v_blk = to_blocks(v)
    k_mean = jnp.mean(k_blk, axis=3)
    b_idx = jnp.arange(bsz)[:, None, None, None]
    h_idx = jnp.arange(nh)[None, :, None, None]
    blk_ids = jnp.arange(nb)

    def one_block(ci):
        start = ci * Q_BLOCK
        own = start // MOBA_BLOCK
        qc = lax.dynamic_slice_in_dim(qh, start, Q_BLOCK, axis=2)
        qpos = start + jnp.arange(Q_BLOCK)
        gate = jnp.einsum('bhqd,bhnd->bhqn', qc, k_mean)
        gate = jnp.where(blk_ids < own, gate, -jnp.inf)
        _, sel = lax.top_k(gate, topk)
        valid = sel < own
        k_sel = k_blk[b_idx, h_idx, sel]
        v_sel = v_blk[b_idx, h_idx, sel]
        s_sel = jnp.einsum('bhqd,bhqtkd->bhqtk', qc, k_sel)
        s_sel = jnp.where(valid[..., None], s_sel, -jnp.inf).reshape(bsz, nh, Q_BLOCK, topk * MOBA_BLOCK)
        k_own = lax.dynamic_index_in_dim(k_blk, own, axis=2, keepdims=False)
        v_own = lax.dynamic_index_in_dim(v_blk, own, axis=2, keepdims=False)
        kpos = own * MOBA_BLOCK + jnp.arange(MOBA_BLOCK)
        s_own = jnp.einsum('bhqd,bhkd->bhqk', qc, k_own)
        s_own = jnp.where(kpos[None, :] <= qpos[:, None], s_own, -jnp.inf)
        p = jax.nn.softmax(jnp.concatenate([s_sel, s_own], axis=-1), axis=-1)
        p_sel = p[..., :topk * MOBA_BLOCK].reshape(bsz, nh, Q_BLOCK, topk, MOBA_BLOCK)
        p_own = p[..., topk * MOBA_BLOCK:]
        return (jnp.einsum('bhqtk,bhqtkd->bhqd', p_sel, v_sel)
                + jnp.einsum('bhqk,bhkd->bhqd', p_own, v_own))

    o = lax.map(one_block, jnp.arange(s // Q_BLOCK))
    return jnp.transpose(o, (1, 0, 3, 2, 4)).reshape(bsz, s, nh, d)

def hybrid_mixer(h, cos, sin, w_in, conv_w, a_log, dt_bias, o_norm, w_out):
    bsz, s, _ = h.shape
    f32 = jnp.float32
    qkv_a, z_a, b_a, a_a, q_b, k_b, v_b = jnp.split(h @ w_in, HY_SPLITS, axis=-1)
    qkv_a = causal_conv_silu(qkv_a, conv_w)
    q_a, k_a, v_a = jnp.split(qkv_a, [GDN_QK, 2 * GDN_QK], axis=-1)
    q_a = l2norm(q_a.reshape(bsz, s, GDN_HEADS, GDN_DK))
    k_a = l2norm(k_a.reshape(bsz, s, GDN_HEADS, GDN_DK))
    v_a = v_a.reshape(bsz, s, GDN_HEADS, GDN_DV).astype(f32)
    beta = jax.nn.sigmoid(b_a.astype(f32))
    g = -jnp.exp(a_log.astype(f32)) * jax.nn.softplus(a_a.astype(f32) + dt_bias.astype(f32))
    o_a = gated_delta_rule(q_a, k_a, v_a, g, beta)
    o_a = rmsnorm(o_a, o_norm) * jax.nn.silu(z_a.reshape(bsz, s, GDN_HEADS, GDN_DV).astype(f32))
    q_b = apply_rope(q_b.reshape(bsz, s, MOBA_HEADS, MOBA_DH), cos, sin)
    k_b = apply_rope(k_b.reshape(bsz, s, MOBA_HEADS, MOBA_DH), cos, sin)
    v_b = v_b.reshape(bsz, s, MOBA_HEADS, MOBA_DH).astype(f32)
    o_b = moba_attention(q_b, k_b, v_b)
    o = jnp.concatenate([o_a.reshape(bsz, s, GDN_V), o_b.reshape(bsz, s, MOBA_W)], axis=-1)
    return o.astype(h.dtype) @ w_out

def mla_mixer(h, cos, sin, w_in, q_norm, kv_norm, w_uq, w_ukv, w_out):
    bsz, s, _ = h.shape
    f32 = jnp.float32
    cq, ckv, k_rope = jnp.split(h @ w_in, [MLA_Q_RANK, MLA_Q_RANK + MLA_KV_RANK], axis=-1)
    q = (rmsnorm(cq, q_norm) @ w_uq).reshape(bsz, s, MLA_HEADS, MLA_NOPE + MLA_ROPE)
    kv = (rmsnorm(ckv, kv_norm) @ w_ukv).reshape(bsz, s, MLA_HEADS, MLA_NOPE + MLA_V)
    q_nope, q_rope = jnp.split(q.astype(f32), [MLA_NOPE], axis=-1)
    k_nope, val = jnp.split(kv.astype(f32), [MLA_NOPE], axis=-1)
    q_rope = apply_rope(q_rope, cos, sin)
    k_rope = apply_rope(k_rope[:, :, None, :], cos, sin)[:, :, 0, :]
    scale = (MLA_NOPE + MLA_ROPE) ** -0.5
    qn = jnp.moveaxis(q_nope, 2, 1) * scale
    qr = jnp.moveaxis(q_rope, 2, 1) * scale
    kn = jnp.moveaxis(k_nope, 2, 1)
    vh = jnp.moveaxis(val, 2, 1)
    kpos = jnp.arange(s)

    def one_block(bi):
        start = bi * Q_BLOCK
        qn_b = lax.dynamic_slice_in_dim(qn, start, Q_BLOCK, axis=2)
        qr_b = lax.dynamic_slice_in_dim(qr, start, Q_BLOCK, axis=2)
        scores = (jnp.einsum('bhqd,bhkd->bhqk', qn_b, kn)
                  + jnp.einsum('bhqr,bkr->bhqk', qr_b, k_rope))
        qpos = start + jnp.arange(Q_BLOCK)
        scores = jnp.where(kpos[None, :] <= qpos[:, None], scores, -jnp.inf)
        return jnp.einsum('bhqk,bhkd->bhqd', jax.nn.softmax(scores, axis=-1), vh)

    o = lax.map(one_block, jnp.arange(s // Q_BLOCK))
    o = jnp.transpose(o, (1, 0, 3, 2, 4)).reshape(bsz, s, MLA_HEADS * MLA_V)
    return o.astype(h.dtype) @ w_out

def peer_ffn(h, w_q, sub_keys, u, v):
    bsz, s, d = h.shape
    f32 = jnp.float32
    q = (h @ w_q).astype(f32).reshape(bsz, s, PEER_HEADS, 2, PEER_DKEY // 2)
    scores = jnp.einsum('bshpd,hpnd->bshpn', q, sub_keys.astype(f32))
    s1, i1 = lax.top_k(scores[..., 0, :], PEER_TOPK)
    s2, i2 = lax.top_k(scores[..., 1, :], PEER_TOPK)
    n_cand = PEER_TOPK * PEER_TOPK
    cand = (s1[..., :, None] + s2[..., None, :]).reshape(bsz, s, PEER_HEADS, n_cand)
    cand_idx = (i1[..., :, None] * PEER_NKEYS + i2[..., None, :]).reshape(bsz, s, PEER_HEADS, n_cand)
    top, pos = lax.top_k(cand, PEER_TOPK)
    expert = jnp.take_along_axis(cand_idx, pos, axis=-1)
    gates = jax.nn.softmax(top, axis=-1)
    n_tok = bsz * s
    n_sel = PEER_HEADS * PEER_TOPK
    n_chunk = n_tok // PEER_TOK_CHUNK
    h_c = h.reshape(n_chunk, PEER_TOK_CHUNK, d)
    e_c = expert.reshape(n_chunk, PEER_TOK_CHUNK, n_sel)
    g_c = gates.reshape(n_chunk, PEER_TOK_CHUNK, n_sel)

    def one_chunk(args):
        hc, ec, gc = args
        act = jax.nn.gelu(jnp.einsum('td,ted->te', hc, u[ec]).astype(f32), approximate=False)
        return jnp.einsum('te,ted->td', (gc * act).astype(v.dtype), v[ec])

    out = lax.map(one_chunk, (h_c, e_c, g_c))
    return out.reshape(bsz, s, d).astype(h.dtype)

def first_inputs(seed: int = 0) -> dict:
    key = jax.random.key(seed)
    ks = jax.random.split(key, 24)
    f32 = jnp.float32
    D = D_MODEL

    def nrm(k, shape, scale):
        return jax.random.normal(k, shape, f32) * scale

    def gain(k, shape):
        return 1.0 + 0.02 * jax.random.normal(k, shape, f32)

    dt = jnp.exp(jax.random.uniform(ks[9], (N_EVEN, GDN_HEADS), f32, math.log(1e-3), math.log(1e-1)))
    return {
        'x': nrm(ks[0], (BATCH, SEQ, D), 1.0),
        'c': nrm(ks[1], (BATCH, D), 1.0),
        'positions': jnp.broadcast_to(jnp.arange(SEQ, dtype=jnp.int32), (BATCH, SEQ)),
        'mod_w': nrm(ks[2], (DEPTH, D, 6 * D), 0.5 * D ** -0.5),
        'mod_b': nrm(ks[3], (DEPTH, 6 * D), 0.02),
        'norm_mix': gain(ks[4], (DEPTH, D)),
        'norm_ffn': gain(ks[5], (DEPTH, D)),
        'hy_w_in': nrm(ks[6], (N_EVEN, D, HY_IN), D ** -0.5),
        'gdn_conv': nrm(ks[7], (N_EVEN, GDN_CONV, GDN_CONV_CH), GDN_CONV ** -0.5),
        'gdn_a_log': jnp.log(jax.random.uniform(ks[8], (N_EVEN, GDN_HEADS), f32, 1.0, 16.0)),
        'gdn_dt_bias': dt + jnp.log(-jnp.expm1(-dt)),
        'gdn_o_norm': gain(ks[10], (N_EVEN, GDN_DV)),
        'hy_w_out': nrm(ks[11], (N_EVEN, HY_OUT, D), HY_OUT ** -0.5),
        'mla_w_in': nrm(ks[12], (N_ODD, D, MLA_IN), D ** -0.5),
        'mla_q_norm': gain(ks[13], (N_ODD, MLA_Q_RANK)),
        'mla_kv_norm': gain(ks[14], (N_ODD, MLA_KV_RANK)),
        'mla_w_uq': nrm(ks[15], (N_ODD, MLA_Q_RANK, MLA_HEADS * (MLA_NOPE + MLA_ROPE)), MLA_Q_RANK ** -0.5),
        'mla_w_ukv': nrm(ks[16], (N_ODD, MLA_KV_RANK, MLA_HEADS * (MLA_NOPE + MLA_V)), MLA_KV_RANK ** -0.5),
        'mla_w_out': nrm(ks[17], (N_ODD, MLA_HEADS * MLA_V, D), (MLA_HEADS * MLA_V) ** -0.5),
        'peer_w_q': nrm(ks[18], (DEPTH, D, PEER_HEADS * PEER_DKEY), D ** -0.5),
        'peer_sub_keys': nrm(ks[19], (DEPTH, PEER_HEADS, 2, PEER_NKEYS, PEER_DKEY // 2), (PEER_DKEY // 2) ** -0.5),
        'peer_u': nrm(ks[20], (DEPTH, PEER_EXPERTS, D), D ** -0.5),
        'peer_v': nrm(ks[21], (DEPTH, PEER_EXPERTS, D), PEER_HEADS ** -0.5),
        'final_norm': gain(ks[22], (D,)),
    }

def first_block(x, c, positions, mod_w, mod_b, norm_mix, norm_ffn, hy_w_in, gdn_conv, gdn_a_log,
              gdn_dt_bias, gdn_o_norm, hy_w_out, mla_w_in, mla_q_norm, mla_kv_norm, mla_w_uq,
              mla_w_ukv, mla_w_out, peer_w_q, peer_sub_keys, peer_u, peer_v, final_norm):
    cond = jax.nn.silu(c)
    cos_b, sin_b = rope_tables(positions, MOBA_DH)
    cos_c, sin_c = rope_tables(positions, MLA_ROPE)
    for layer in range(DEPTH):
        mod = cond @ mod_w[layer] + mod_b[layer]
        sh1, sc1, g1, sh2, sc2, g2 = jnp.split(mod[:, None, :], 6, axis=-1)
        h = rmsnorm(x, norm_mix[layer]) * (1.0 + sc1) + sh1
        i = layer // 2
        if layer % 2 == 0:
            y = hybrid_mixer(h, cos_b, sin_b, hy_w_in[i], gdn_conv[i], gdn_a_log[i], gdn_dt_bias[i],
                             gdn_o_norm[i], hy_w_out[i])
        else:
            y = mla_mixer(h, cos_c, sin_c, mla_w_in[i], mla_q_norm[i], mla_kv_norm[i], mla_w_uq[i],
                          mla_w_ukv[i], mla_w_out[i])
        x = x + g1 * y
        h = rmsnorm(x, norm_ffn[layer]) * (1.0 + sc2) + sh2
        x = x + g2 * peer_ffn(h, peer_w_q[layer], peer_sub_keys[layer], peer_u[layer], peer_v[layer])
    return rmsnorm(x, final_norm)


GRID_W = 64
HEAD_DIM = 64
ATT_Q_HEADS = 8
ATT_KV_HEADS = 2
ATT_Q_W = ATT_Q_HEADS * HEAD_DIM
ATT_KV_W = ATT_KV_HEADS * HEAD_DIM
HY_WIDTH = 512
HY_ORDER = 2
HY_BANDS = 16
HY_EMB = 1 + 2 * HY_BANDS
HY_FFN = 64
HY_FAST_DECAY = 0.3
HY_SLOW_DECAY = 1.5
HY_TARGET = 1e-2
GLA_HEADS = 4
GLA_DK = 64
GLA_DV = 128
GLA_RANK = 16
GLA_NORMALIZER = 16.0
GLA_CHUNK = 64
GLA_K_W = GLA_HEADS * GLA_DK
GLA_V_W = GLA_HEADS * GLA_DV
MEM_LEN = 256
X_HEADS = 4
X_HEAD_DIM = D_MODEL // X_HEADS
D_FF = 4 * D_MODEL
N_BRANCH = 3
IN_SPLITS = (ATT_Q_W, ATT_KV_W, ATT_KV_W, 3 * HY_WIDTH, GLA_K_W, GLA_K_W, GLA_V_W, GLA_V_W,
             2 * GLA_RANK, N_BRANCH * D_MODEL)
N_IN = ATT_Q_W + 2 * ATT_KV_W + 3 * HY_WIDTH + 2 * GLA_K_W + 2 * GLA_V_W + 2 * GLA_RANK + N_BRANCH * D_MODEL


F32 = jnp.float32

def rmsnorm_2(x, g):
    xf = x.astype(F32)
    y = xf * lax.rsqrt(jnp.mean(xf * xf, axis=-1, keepdims=True) + EPS)
    return (y * g.astype(F32)).astype(x.dtype)

def split_cols(u, sizes):
    idx = [int(i) for i in np.cumsum(sizes)[:-1]]
    return jnp.split(u, idx, axis=-1)

def axial_rope_angles(L):
    rows = L // GRID_W
    r, c = jnp.meshgrid(jnp.arange(rows), jnp.arange(GRID_W), indexing="ij")
    n_freq = HEAD_DIM // 4
    inv = ROPE_THETA ** (-jnp.arange(n_freq, dtype=F32) / n_freq)
    pos = jnp.stack([r.reshape(-1), c.reshape(-1)], axis=1).astype(F32)
    ang = pos[:, :, None] * inv
    return jnp.cos(ang), jnp.sin(ang)

def apply_rope_2(x, cos, sin):
    xs = x.reshape(x.shape[:-1] + (2, 2, HEAD_DIM // 4)).astype(F32)
    x1, x2 = xs[..., 0, :], xs[..., 1, :]
    out = jnp.stack([x1 * cos - x2 * sin, x1 * sin + x2 * cos], axis=-2)
    return out.reshape(x.shape).astype(x.dtype)

def attention_mixer(q, k, v, qn, kn, cos, sin):
    B, L, _ = q.shape
    G = ATT_Q_HEADS // ATT_KV_HEADS
    q = rmsnorm_2(q.reshape(B, L, ATT_Q_HEADS, HEAD_DIM), qn).transpose(0, 2, 1, 3)
    k = rmsnorm_2(k.reshape(B, L, ATT_KV_HEADS, HEAD_DIM), kn).transpose(0, 2, 1, 3)
    v = v.reshape(B, L, ATT_KV_HEADS, HEAD_DIM).transpose(0, 2, 1, 3)
    q = apply_rope_2(q, cos, sin).reshape(B, ATT_KV_HEADS, G, L, HEAD_DIM)
    k = apply_rope_2(k, cos, sin)
    nb = L // Q_BLOCK
    qb = jnp.moveaxis(q.reshape(B, ATT_KV_HEADS, G, nb, Q_BLOCK, HEAD_DIM), 3, 0)
    scale = HEAD_DIM ** -0.5

    def block(qblk):
        s = jnp.einsum("bkgqd,bktd->bkgqt", qblk, k).astype(F32) * scale
        p = jax.nn.softmax(s, axis=-1).astype(v.dtype)
        return jnp.einsum("bkgqt,bktd->bkgqd", p, v)

    o = lax.map(block, qb)
    o = jnp.moveaxis(o, 0, 3).reshape(B, ATT_Q_HEADS, L, HEAD_DIM)
    return o.transpose(0, 2, 1, 3).reshape(B, L, ATT_Q_W)

def short_conv(u, w):
    up = jnp.pad(u, ((0, 0), (1, 1), (0, 0)))
    return up[:, :-2] * w[0] + up[:, 1:-1] * w[1] + up[:, 2:] * w[2]

def hyena_pos_features(L):
    t = jnp.arange(L, dtype=F32)
    t_norm = t / max(L - 1, 1)
    w = 2.0 * math.pi * t / L
    f = jnp.linspace(1e-4, HY_BANDS - 1, HY_BANDS, dtype=F32)
    fw = w[:, None] * f
    z = jnp.concatenate([t_norm[:, None], jnp.cos(fw), -jnp.sin(fw)], axis=-1)
    deltas = jnp.abs(jnp.linspace(math.log(HY_TARGET) / HY_FAST_DECAY,
                                  math.log(HY_TARGET) / HY_SLOW_DECAY, HY_WIDTH, dtype=F32))
    window = jnp.exp(-t_norm[:, None] * deltas)
    return z, window

def hyena_filter_spectra(z, window, w1, b1, w2, b2, w3, b3, freq):
    L = z.shape[0]
    c = lambda a: a.astype(F32)
    h = jnp.sin(c(freq[0]) * (z @ c(w1) + c(b1)))
    h = jnp.sin(c(freq[1]) * (h @ c(w2) + c(b2)))
    h = (h @ c(w3) + c(b3)).reshape(L, HY_ORDER, 2, HY_WIDTH) * window[:, None, None, :]
    fwd, bwd = h[:, :, 0], h[:, :, 1]
    f = jnp.concatenate([fwd, jnp.zeros((1, HY_ORDER, HY_WIDTH), F32), bwd[1:][::-1]], axis=0)
    f = f / (jnp.sum(jnp.abs(f), axis=0, keepdims=True) + EPS)
    return jnp.fft.rfft(f, axis=0)

def long_conv(u, spec, skip):
    L = u.shape[1]
    uf = u.astype(F32)
    y = jnp.fft.irfft(jnp.fft.rfft(uf, n=2 * L, axis=1) * spec, n=2 * L, axis=1)[:, :L]
    return (y + uf * skip.astype(F32)).astype(u.dtype)

def hyena_mixer(u, conv_w, spec, skip):
    u = short_conv(u, conv_w)
    v, x1, x2 = jnp.split(u, 3, axis=-1)
    z = x1 * long_conv(v, spec[:, 0], skip[0])
    return x2 * long_conv(z, spec[:, 1], skip[1])

def gla_scan(q, k, v, g, include_diag):
    B, H, L, dk = q.shape
    dv = v.shape[-1]
    C = GLA_CHUNK
    N = L // C
    q, k, g = (a.reshape(B, H, N, C, dk) for a in (q, k, g))
    v = v.reshape(B, H, N, C, dv)
    b = jnp.cumsum(g, axis=3)
    b_last = b[:, :, :, -1:, :]
    q_dec = q * jnp.exp(b)
    a = jnp.einsum("bhncd,bhnsd->bhncs", q_dec, k * jnp.exp(-b))
    mask = jnp.tril(jnp.ones((C, C), dtype=bool), k=0 if include_diag else -1)
    o = jnp.einsum("bhncs,bhnse->bhnce", jnp.where(mask, a, 0.0), v)
    d_state = jnp.einsum("bhncd,bhnce->bhnde", k * jnp.exp(b_last - b), v)
    decay = jnp.exp(b_last[:, :, :, 0, :])

    def step(S, inp):
        dec, ds = inp
        return dec[..., None] * S + ds, S

    _, s_prev = lax.scan(step, jnp.zeros((B, H, dk, dv), F32),
                         (jnp.moveaxis(decay, 2, 0), jnp.moveaxis(d_state, 2, 0)))
    s_prev = jnp.moveaxis(s_prev, 0, 2)
    o = o + jnp.einsum("bhncd,bhnde->bhnce", q_dec, s_prev)
    return o.reshape(B, H, L, dv)

def gla_mixer(q, k, v, og, lr, w_lr, b_lr, onorm):
    B, L, _ = q.shape
    heads = lambda a, d: a.astype(F32).reshape(B, L, GLA_HEADS, d).transpose(0, 2, 1, 3)
    q = heads(q, GLA_DK) * (GLA_DK ** -0.5)
    k = heads(k, GLA_DK)
    v = heads(v, GLA_DV)
    logit = jnp.einsum("btsr,srd->btsd", lr.astype(F32).reshape(B, L, 2, GLA_RANK),
                       w_lr.astype(F32)) + b_lr.astype(F32)
    g = jax.nn.log_sigmoid(logit) / GLA_NORMALIZER
    g_f = heads(g[:, :, 0], GLA_DK)
    g_b = heads(g[:, :, 1], GLA_DK)
    fl = lambda a: jnp.flip(a, axis=2)
    o_f = gla_scan(q, k, v, g_f, True)
    o_b = fl(gla_scan(fl(q), fl(k), fl(v), fl(g_b), False))
    o = (o_f + o_b).transpose(0, 2, 1, 3)
    o = rmsnorm_2(o, onorm) * jax.nn.silu(og.astype(F32).reshape(B, L, GLA_HEADS, GLA_DV))
    return o.reshape(B, L, GLA_V_W).astype(og.dtype)

def memory_cross_attention(hn, mn, wq, wk, wv, wo, qn, kn):
    B, L, _ = hn.shape
    M = mn.shape[1]
    q = rmsnorm_2((hn @ wq).reshape(B, L, X_HEADS, X_HEAD_DIM), qn)
    k = rmsnorm_2((mn @ wk).reshape(B, M, X_HEADS, X_HEAD_DIM), kn)
    v = (mn @ wv).reshape(B, M, X_HEADS, X_HEAD_DIM)
    s = jnp.einsum("blhd,bmhd->bhlm", q, k).astype(F32) * (X_HEAD_DIM ** -0.5)
    p = jax.nn.softmax(s, axis=-1).astype(v.dtype)
    o = jnp.einsum("bhlm,bmhd->blhd", p, v).reshape(B, L, D_MODEL)
    return o @ wo

def second_inputs(seed: int = 0) -> dict:
    key = jax.random.key(seed)
    ks = iter(jax.random.split(key, 40))

    def nrm(shape, s):
        return jax.random.normal(next(ks), shape, F32) * s

    def gain(shape):
        return 1.0 + nrm(shape, 0.02)

    Ld = DEPTH
    return {
        "x": nrm((BATCH, SEQ, D_MODEL), 1.0),
        "mem": nrm((BATCH, MEM_LEN, D_MODEL), 1.0),
        "ln_mix": gain((Ld, D_MODEL)),
        "w_in": nrm((Ld, D_MODEL, N_IN), D_MODEL ** -0.5),
        "attn_qnorm": gain((Ld, HEAD_DIM)),
        "attn_knorm": gain((Ld, HEAD_DIM)),
        "hy_conv": nrm((Ld, 3, 3 * HY_WIDTH), 3 ** -0.5),
        "hy_w1": nrm((Ld, HY_EMB, HY_FFN), HY_EMB ** -0.5),
        "hy_b1": nrm((Ld, HY_FFN), 0.1),
        "hy_w2": nrm((Ld, HY_FFN, HY_FFN), HY_FFN ** -0.5),
        "hy_b2": nrm((Ld, HY_FFN), 0.1),
        "hy_w3": nrm((Ld, HY_FFN, HY_ORDER * 2 * HY_WIDTH), HY_FFN ** -0.5),
        "hy_b3": nrm((Ld, HY_ORDER * 2 * HY_WIDTH), 0.1),
        "hy_freq": 1.0 + nrm((Ld, 2, HY_FFN), 0.1),
        "hy_skip": nrm((Ld, HY_ORDER, HY_WIDTH), 0.5),
        "gla_w_lr": nrm((Ld, 2, GLA_RANK, GLA_K_W), GLA_RANK ** -0.5),
        "gla_b_lr": nrm((Ld, 2, GLA_K_W), 0.1),
        "gla_onorm": gain((Ld, GLA_DV)),
        "w_br_attn": nrm((Ld, ATT_Q_W, D_MODEL), ATT_Q_W ** -0.5),
        "w_br_hyena": nrm((Ld, HY_WIDTH, D_MODEL), HY_WIDTH ** -0.5),
        "w_br_gla": nrm((Ld, GLA_V_W, D_MODEL), GLA_V_W ** -0.5),
        "w_out": nrm((Ld, D_MODEL, D_MODEL), D_MODEL ** -0.5),
        "ln_x": gain((Ld, D_MODEL)),
        "ln_mem": gain((Ld, D_MODEL)),
        "x_wq": nrm((Ld, D_MODEL, D_MODEL), D_MODEL ** -0.5),
        "x_wk": nrm((Ld, D_MODEL, D_MODEL), D_MODEL ** -0.5),
        "x_wv": nrm((Ld, D_MODEL, D_MODEL), D_MODEL ** -0.5),
        "x_wo": nrm((Ld, D_MODEL, D_MODEL), D_MODEL ** -0.5),
        "x_qnorm": gain((Ld, X_HEAD_DIM)),
        "x_knorm": gain((Ld, X_HEAD_DIM)),
        "ln_mlp": gain((Ld, D_MODEL)),
        "mlp_w1": nrm((Ld, D_MODEL, D_FF), D_MODEL ** -0.5),
        "mlp_w2": nrm((Ld, D_FF, D_MODEL), D_FF ** -0.5),
    }

def second_block(x, mem, ln_mix, w_in, attn_qnorm, attn_knorm, hy_conv, hy_w1, hy_b1, hy_w2, hy_b2,
              hy_w3, hy_b3, hy_freq, hy_skip, gla_w_lr, gla_b_lr, gla_onorm, w_br_attn, w_br_hyena,
              w_br_gla, w_out, ln_x, ln_mem, x_wq, x_wk, x_wv, x_wo, x_qnorm, x_knorm, ln_mlp,
              mlp_w1, mlp_w2):
    B, L, _ = x.shape
    cos, sin = axial_rope_angles(L)
    z_pos, window = hyena_pos_features(L)
    h = x
    for i in range(DEPTH):
        hn = rmsnorm_2(h, ln_mix[i])
        (aq, ak, av, hy, gq, gk, gv, go, glr, gates) = split_cols(hn @ w_in[i], IN_SPLITS)
        y_a = attention_mixer(aq, ak, av, attn_qnorm[i], attn_knorm[i], cos, sin) @ w_br_attn[i]
        spec = hyena_filter_spectra(z_pos, window, hy_w1[i], hy_b1[i], hy_w2[i], hy_b2[i],
                                    hy_w3[i], hy_b3[i], hy_freq[i])
        y_b = hyena_mixer(hy, hy_conv[i], spec, hy_skip[i]) @ w_br_hyena[i]
        y_c = gla_mixer(gq, gk, gv, go, glr, gla_w_lr[i], gla_b_lr[i], gla_onorm[i]) @ w_br_gla[i]
        gate = jax.nn.sigmoid(gates.reshape(B, L, N_BRANCH, D_MODEL))
        mixed = gate[:, :, 0] * y_a + gate[:, :, 1] * y_b + gate[:, :, 2] * y_c
        h = h + mixed @ w_out[i]
        h = h + memory_cross_attention(rmsnorm_2(h, ln_x[i]), rmsnorm_2(mem, ln_mem[i]),
                                       x_wq[i], x_wk[i], x_wv[i], x_wo[i], x_qnorm[i], x_knorm[i])
        hn = rmsnorm_2(h, ln_mlp[i])
        h = h + jnp.square(jax.nn.relu(hn @ mlp_w1[i])) @ mlp_w2[i]
    return h


def setup_inputs(seed=0):
    out = dict(first_inputs(seed))
    for name, value in second_inputs(seed + 1).items():
        if name != "x":
            out[name + "_2"] = value
    return out


def reference(
    x, c, positions, mod_w, mod_b, norm_mix, norm_ffn, hy_w_in, gdn_conv, gdn_a_log,
    gdn_dt_bias, gdn_o_norm, hy_w_out, mla_w_in, mla_q_norm, mla_kv_norm, mla_w_uq, mla_w_ukv,
    mla_w_out, peer_w_q, peer_sub_keys, peer_u, peer_v, final_norm, mem_2, ln_mix_2, w_in_2,
    attn_qnorm_2, attn_knorm_2, hy_conv_2, hy_w1_2, hy_b1_2, hy_w2_2, hy_b2_2, hy_w3_2, hy_b3_2,
    hy_freq_2, hy_skip_2, gla_w_lr_2, gla_b_lr_2, gla_onorm_2, w_br_attn_2, w_br_hyena_2,
    w_br_gla_2, w_out_2, ln_x_2, ln_mem_2, x_wq_2, x_wk_2, x_wv_2, x_wo_2, x_qnorm_2, x_knorm_2,
    ln_mlp_2, mlp_w1_2, mlp_w2_2,
):
    x = first_block(
        x, c, positions, mod_w, mod_b, norm_mix, norm_ffn, hy_w_in, gdn_conv, gdn_a_log,
        gdn_dt_bias, gdn_o_norm, hy_w_out, mla_w_in, mla_q_norm, mla_kv_norm, mla_w_uq,
        mla_w_ukv, mla_w_out, peer_w_q, peer_sub_keys, peer_u, peer_v, final_norm,
    )
    return second_block(
        x, mem_2, ln_mix_2, w_in_2, attn_qnorm_2, attn_knorm_2, hy_conv_2, hy_w1_2, hy_b1_2,
        hy_w2_2, hy_b2_2, hy_w3_2, hy_b3_2, hy_freq_2, hy_skip_2, gla_w_lr_2, gla_b_lr_2,
        gla_onorm_2, w_br_attn_2, w_br_hyena_2, w_br_gla_2, w_out_2, ln_x_2, ln_mem_2, x_wq_2,
        x_wk_2, x_wv_2, x_wo_2, x_qnorm_2, x_knorm_2, ln_mlp_2, mlp_w1_2, mlp_w2_2,
    )


_drawn_inputs = setup_inputs


def setup_inputs(seed=0):
    import zlib

    import numpy as np

    out = dict(_drawn_inputs(seed))
    spreads = {}
    factors = {'norm_mix': 4.912,
     'norm_ffn': 3.372,
     'gdn_o_norm': 6.533,
     'mla_q_norm': 8.0,
     'mla_kv_norm': 8.0,
     'ln_mix_2': 3.016,
     'attn_qnorm_2': 8.0,
     'attn_knorm_2': 8.0,
     'hy_b1_2': 5.589,
     'hy_b2_2': 4.136,
     'hy_b3_2': 3.303,
     'hy_freq_2': 8.0,
     'gla_b_lr_2': 2.879,
     'gla_onorm_2': 6.891,
     'ln_x_2': 8.0,
     'ln_mem_2': 8.0,
     'x_qnorm_2': 8.0,
     'x_knorm_2': 8.0,
     'ln_mlp_2': 3.728}
    for name, (base, spread) in spreads.items():
        noise = np.random.default_rng([zlib.crc32(name.encode()), seed]).standard_normal(out[name].shape)
        drawn = base * np.exp(spread * noise) if base else spread * noise
        out[name] = jnp.asarray(drawn.astype(out[name].dtype))
    for name, factor in factors.items():
        out[name] = (out[name] * factor).astype(out[name].dtype)
    return out
```

```python
from contextlib import ExitStack

import concourse.bass as bass
from concourse import mybir
import numpy as np

F32 = mybir.dt.float32
I32 = mybir.dt.int32
U32 = mybir.dt.uint32
ALU = mybir.AluOpType
ACT = mybir.ActivationFunctionType
AX = mybir.AxisListType.X

P = 128
T = 256
TM = T // P
D = 1024
DC = D // P
EPS = 1e-6
DEPTH = 2
NEG = -1e30
LOW = -3.0e38

GH, GC = 4, 64
NCH = T // GC
MLA_H = 8
PEER_H, PEER_K, NKEY = 8, 16, 128
HP = 2 * PEER_H
HYW, FT = 512, 2048
D_FF = 4096

RING, RING_W = 3, 4096
UV_RING, UV_W = 4, 2048
GRP = 4


def constant_tables():
    i = np.arange(P)
    s, t = i[:, None], i[None, :]
    same = (s // GC) == (t // GC)
    c = {}
    c["ident"] = np.eye(P)
    c["ones"] = np.ones((P, P))
    c["blk"] = same * 1.0
    c["upto"] = (same & (s <= t)) * 1.0
    c["since"] = (same & (s >= t)) * 1.0
    c["later"] = (same & (s > t)) * 1.0
    c["before"] = (same & (s < t)) * 1.0
    c["mlow"] = np.where(same & (t <= s), 0.0, NEG)
    c["mup"] = np.where(same & (s <= t), 0.0, NEG)

    def rotation(width):
        r = np.zeros((P, P))
        h = width // 2
        for m in range(P):
            if m % width < h:
                r[m + h, m] = -1.0
            else:
                r[m - h, m] = 1.0
        return r
    c["rot128"], c["rot64"], c["rot32"] = rotation(128), rotation(64), rotation(32)
    kv = np.arange(T)[None, None, :]
    q = np.arange(TM)[None, :, None] * P + i[:, None, None]
    c["causal"] = np.where(kv <= q, 0.0, NEG).reshape(P, TM * T)
    f16 = (np.float32(10000.0) ** (-np.arange(16, dtype=np.float32) / 16)).astype(np.float32)
    tok = np.arange(T)
    where = np.stack([tok // 64, tok % 64], 0).astype(np.float32)
    row = i % 64
    ang = (where[row // 32] * f16[row % 16][:, None]).astype(np.float32)
    c["axcos"], c["axsin"] = np.cos(ang), np.sin(ang)
    c["iota"] = np.broadcast_to(np.arange(P, dtype=np.float32), (P, P))
    inv = lambda n: (np.float32(10000.0) ** (-np.arange(0, n, 2, dtype=np.float32) / n)).astype(np.float32)
    c["invf"] = np.stack([inv(128)[i % 64], inv(64)[i % 32]], 1)
    th = 2 * np.pi * (np.arange(T)[None, :] + 0.5) * np.arange(T)[:, None] / (2 * T)
    fwd = np.concatenate([np.cos(th), np.sin(th)], 1).reshape(TM, P, 2 * T)
    inv_ = (np.concatenate([np.cos(th), np.sin(th)], 1).T / T).reshape(4, P, T)
    tn = np.arange(T, dtype=np.float32) / (T - 1)
    import math
    deltas = np.abs(np.linspace(math.log(1e-2) / 0.3, math.log(1e-2) / 1.5, HYW, dtype=np.float32))
    win = np.exp(-tn[:, None] * deltas).astype(np.float32)
    winb = win.copy()
    winb[0] = 0.0
    hy = [fwd.transpose(1, 0, 2).reshape(P, -1), inv_.transpose(1, 0, 2).reshape(P, -1),
          win.reshape(TM, P, HYW).transpose(1, 0, 2).reshape(P, -1),
          winb.reshape(TM, P, HYW).transpose(1, 0, 2).reshape(P, -1)]
    w = (2.0 * math.pi * np.arange(T, dtype=np.float32) / T).astype(np.float32)
    fr = np.linspace(1e-4, 15, 16, dtype=np.float32)
    fw = w[:, None] * fr
    z = np.concatenate([tn[:, None], np.cos(fw), -np.sin(fw)], -1).T
    zp = np.zeros((P, T))
    zp[:33] = z
    c["zpos"] = zp
    return ({k: np.ascontiguousarray(v, dtype=np.float32) for k, v in c.items()},
            np.ascontiguousarray(np.concatenate(hy, 1), dtype=np.float32))


CONST_COLS = dict(ident=P, ones=P, blk=P, upto=P, since=P, later=P, before=P, mlow=P, mup=P, rot128=P,
                  rot64=P, rot32=P, causal=TM * T, axcos=T, axsin=T, iota=P, invf=2, zpos=T)

VEC_COLS = dict(cond=8, norm_mix=16, norm_ffn=16, mod_b=96, gdn_conv=48, gdn_o_norm=1, q_norm=4, kv_norm=2,
                final_norm=8, ln_mix=16, ln_x=16, ln_mem=16, ln_mlp=16, att_qn=2, att_kn=2, x_qn=4, x_kn=4,
                hy_conv=72, hy_skip=16, gla_on=2, hy_b1=2, hy_b2=2, hy_freq=4)


class Signals:

    def __init__(self, nc, ctx):
        self.nc, self.ctx, self.sems, self.seen, self.sent = nc, ctx, {}, {}, {}

    def __getitem__(self, name):
        if name not in self.sems:
            self.sems[name] = self.ctx.enter_context(self.nc.semaphore(name))
        return self.sems[name]

    def nth(self, eng, name, n=1):
        k = (str(eng.engine), name)
        self.seen[k] = self.seen.get(k, 0) + n
        return self.seen[k]


def two_blocks(nc, a, upto=99):
    ctx = ExitStack()
    with ctx:
        S = Signals(nc, ctx)

        def sb(name, n, dt=F32):
            return ctx.enter_context(nc.sbuf_tensor(name, [P, n], dt))

        ps = ctx.enter_context(nc.psum_tensor("ps", [P, 8, 512], F32))
        big = sb("big", NKEY * T)
        uvr = sb("uvr", UV_RING * UV_W)
        xt = sb("xt", DC * T)
        ht = sb("ht", DC * T)
        sel = sb("sel", 3 * T)
        hot = sb("hot", 2 * 2 * GRP * P)
        consts = sb("consts_sb", sum(CONST_COLS.values()))
        vecs = sb("vecs_sb", sum(VEC_COLS.values()))
        modv = sb("modv", 2 * 48)
        small = sb("small", 256)
        pos_in = sb("pos_in", T, I32)[:]

        x = xt[:].rearrange("p (c t) -> p c t", t=T)
        h = ht[:].rearrange("p (c t) -> p c t", t=T)

        def named(tensor, cols):
            out, o = {}, 0
            for k, n in cols.items():
                out[k] = tensor[:, o:o + n]
                o += n
            return out
        C = named(consts, CONST_COLS)
        V = named(vecs, VEC_COLS)
        causal = C["causal"].rearrange("p (m k) -> p m k", m=TM)

        def ring_slot(i):
            return big[:, (i % RING) * RING_W:(i % RING + 1) * RING_W]
        SCR = RING * RING_W
        SCR_N = NKEY * T - SCR

        class Scratch:

            def __init__(self, expert_ring):
                self.at, self.more, self.end = 0, 0, UV_RING * UV_W if expert_ring else 0

            def get(self, n, dt=None):
                if self.at + n <= SCR_N:
                    v = big[:, SCR + self.at:SCR + self.at + n]
                    self.at += n
                else:
                    assert self.more + n <= self.end, (self.at, self.more, n)
                    v = uvr[:, self.more:self.more + n]
                    self.more += n
                return v

            def mat(self, c, n=T):
                return self.get(c * n).rearrange("p (c n) -> p c n", n=n)

        TE, VE, SE, GE, SP = nc.tensor, nc.vector, nc.scalar, nc.gpsimd, nc.sync

        banks = {"act": [0, None], "dve": [4, None]}
        filled = {"act": "tile_for_act", "dve": "tile_for_dve"}
        acquired = {"act": 0, "dve": 0}
        taken = {"act": 0, "dve": 0}
        freed_by = {}
        expected = {}

        def acquire(pool):
            b = banks[pool][0] + acquired[pool] % 4
            acquired[pool] += 1
            if b in freed_by:
                name, n = freed_by[b]
                TE.wait_ge(S[name], n)
            return b

        def frees(b, name):
            expected[name] = expected.get(name, 0) + 1
            freed_by[b] = (name, expected[name])

        def take(pool):
            b = banks[pool][0] + taken[pool] % 4
            taken[pool] += 1
            (SE if pool == "act" else VE).wait_ge(S[filled[pool]], taken[pool])
            return ps[:, b, :]

        mm = TE.matmul

        before = {}
        weights = []
        use = [0]
        weight_done = {}

        def plan(name, src, kc, n, rows=P, pieces=None):
            weights.append((name, src, kc, n, rows, pieces))

        def weights_in(i):
            return 16 * sum(len(w[5] or [0]) for w in weights[i % RING:i + 1:RING])

        def next_weight(name):
            i = use[0]
            assert weights[i][0] == name, (weights[i][0], name)
            use[0] += 1
            TE.wait_ge(S[f"weights_in_{i % RING}"], weights_in(i))
            kc, n = weights[i][2:4]
            return i, ring_slot(i)[:, 0:kc * n].rearrange("p (c n) -> p c n", c=kc)

        def last_use(i, ins_freed):
            weight_done[i] = ins_freed

        def fm_linear(name, xin, kc, ncols, pool, reader, part=2):
            c, b, left = 0, None, ncols // P
            while c < left:
                i, w = next_weight(name)
                for n0 in range(0, weights[i][3], P):
                    if c % part == 0:
                        b = acquire(pool)
                    for k in range(kc):
                        m = mm(ps[:, b, (c % part) * T:(c % part + 1) * T], w[:, k, n0:n0 + P], xin[:, k, :],
                               start=(k == 0), stop=(k == kc - 1))
                    c += 1
                    if c % part == 0 or c == left:
                        m.then_inc(S[filled[pool]], 1)
                        frees(b, reader)
                last_use(i, (reader, expected[reader]) if c % part == 0 or c == left else None)
            for i in list(weight_done):
                if weight_done[i] is None:
                    weight_done[i] = next(weight_done[j] for j in range(i + 1, use[0]) if weight_done[j])

        def tm_linear(name, xin, kc, ncols, pool, reader):
            c = 0
            while c < ncols:
                i, w = next_weight(name)
                n = weights[i][3]
                for n0 in range(0, n, 512):
                    nn = min(512, n - n0)
                    for t in range(TM):
                        b = acquire(pool)
                        for k in range(kc):
                            m = mm(ps[:, b, 0:nn], xin[:, k, t * P:(t + 1) * P], w[:, k, n0:n0 + nn],
                                   start=(k == 0), stop=(k == kc - 1))
                        m.then_inc(S[filled[pool]], 1)
                        frees(b, reader)
                c += n
                last_use(i, (reader, expected[reader]))

        def evict_act(dst, func=ACT.Copy, frees="act_freed", scale=1.0, n=1):
            for i in range(n):
                t = take("act")
                d = dst[i]
                t = t[:, 0:d.free_size()]
                if len(d.shape) == 3:
                    t = t.rearrange("p (c n) -> p c n", n=d.shape[2])
                SE.activation(d, t, func, scale=scale).then_inc(S[frees], 1)
                SE.wait_ge(S[frees], S.nth(SE, frees))

        def pairs(m, lo=0, hi=None):
            hi = hi or m.shape[1]
            return [m[:, c:min(c + 2, hi), :] for c in range(lo, hi, 2)]

        def norm_pe(groups, nchunk, lhs, sq):
            TE.wait_ge(S["squares"], S.nth(TE, "squares"))
            for g0 in range(0, len(groups), 2):
                b = acquire("act")
                for u, g in enumerate(groups[g0:g0 + 2]):
                    for j, c in enumerate(g):
                        m = mm(ps[:, b, u * T:(u + 1) * T], lhs, sq[:, c, :], start=(j == 0), stop=(j == len(g) - 1))
                m.then_inc(S["tile_for_act"], 1)
                frees(b, "roots")

        def norm_act(src, sq, rs, ngroups, mean, flat=None):
            SE.activation(flat or sq, src, ACT.Square).then_inc(S["squares"], 1)
            SE.wait_ge(S["squares"], S.nth(SE, "squares"))
            for g0 in range(0, ngroups, 2):
                n = min(2, ngroups - g0)
                t = take("act")
                SE.activation(rs[:, g0:g0 + n, :], t[:, 0:n * T].rearrange("p (c n) -> p c n", n=T), ACT.Sqrt,
                    scale=1.0 / mean, bias=eps_col).then_inc(S["roots"], 1)
                SE.wait_ge(S["roots"], S.nth(SE, "roots"))

        def norm_dve(rs, ngroups):
            VE.wait_ge(S["roots"], S.nth(VE, "roots", (ngroups + 1) // 2))
            VE.reciprocal(rs[:, 0:ngroups, :], rs[:, 0:ngroups, :]).then_inc(S["dve_step"], 1)
            VE.wait_ge(S["dve_step"], S.nth(VE, "dve_step"))

        eps_col = small[:, 0:1]

        all_groups = [list(range(DC))]

        def block_norm_pe(sq):
            norm_pe(all_groups, DC, C["ones"], sq)

        def block_norm_act(sq, rs):
            SE.wait_ge(S["x_new"], S.nth(SE, "x_new"))
            norm_act(x, sq, rs, 1, D)

        def block_norm_dve(rs, scale, shift=None, out=None, name="h_ready"):
            out = h if out is None else out
            norm_dve(rs, 1)
            for c in range(DC):
                last = c == DC - 1
                signal = name if last and shift is None else "dve_step"
                VE.scalar_tensor_tensor(out=out[:, c, :], in0=x[:, c, :], scalar=scale[:, c:c + 1], in1=rs[:, 0, :],
                    op0=ALU.mult, op1=ALU.mult).then_inc(S[signal], 1)
                VE.wait_ge(S[signal], S.nth(VE, signal))
            if shift is not None:
                for c in range(DC):
                    signal = name if c == DC - 1 else "dve_step"
                    VE.tensor_scalar(out[:, c, :], out[:, c, :], shift[:, c:c + 1], None,
                        ALU.add).then_inc(S[signal], 1)
                    VE.wait_ge(S[signal], S.nth(VE, signal))

        def residual_dve(gate, nbanks=DC // 2, name="x_new"):
            for b in range(nbanks):
                t = take("dve")
                for u in range(2):
                    c = 2 * b + u
                    last = "residual_in" if u else "dve_step"
                    if gate is None:
                        VE.tensor_tensor(x[:, c, :], t[:, u * T:(u + 1) * T], x[:, c, :], ALU.add).then_inc(S[last],
                            1)
                        VE.wait_ge(S[last], S.nth(VE, last))
                    else:
                        VE.scalar_tensor_tensor(out=x[:, c, :], in0=t[:, u * T:(u + 1) * T], scalar=gate[:, c:c + 1],
                            in1=x[:, c, :], op0=ALU.mult, op1=ALU.add).then_inc(S[last], 1)
                        VE.wait_ge(S[last], S.nth(VE, last))
            VE.tensor_copy(small[:, 1:2], small[:, 0:1]).then_inc(S[name], 1)
            VE.wait_ge(S[name], S.nth(VE, name))

        def attention_pe(H, scores, values, p, pt, dv_rows=P):
            for i in range(H + 2):
                if i >= 2:
                    TE.wait_ge(S["probs_turned"], expected["probs_turned"])
                    values(i - 2, pt[i % 2])
                if i < H:
                    b = acquire("dve")
                    m = scores(i, b)
                    m.then_inc(S["tile_for_dve"], 1)
                    frees(b, "scores_taken")
                if 1 <= i <= H:
                    TE.wait_ge(S["probs_ready"], S.nth(TE, "probs_ready"))
                    for j in range(TM):
                        b = acquire("act") if j == 0 else b
                        for t in range(TM):
                            m = TE.transpose(ps[:, b, j * T + t * P:j * T + (t + 1) * P],
                                             p[(i - 1) % 2][:, t, j * P:(j + 1) * P], C["ident"])
                    m.then_inc(S["tile_for_act"], 1)
                    frees(b, "probs_turned")

        def attention_act(H, p, pt, scale, st):
            for i in range(H + 1):
                if i < H:
                    SE.wait_ge(S["row_max"], S.nth(SE, "row_max"))
                    for t in range(TM):
                        signal = "exps" if t else "act_step"
                        SE.activation(p[i % 2][:, t, :], p[i % 2][:, t, :], ACT.Exp, scale=scale,
                            bias=st[:, 4 * (i % 2) + t:4 * (i % 2) + t + 1], accum_out=st[:,
                            4 * (i % 2) + 2 + t:4 * (i % 2) + 3 + t]).then_inc(S[signal], 1)
                        SE.wait_ge(S[signal], S.nth(SE, signal))
                if i >= 1:
                    evict_act([pt[(i + 1) % 2]], frees="probs_turned")

        def attention_dve(H, p, mask, scale, st, out):
            for i in range(H + 2):
                if i >= 2:
                    out(i - 2)
                if i < H:
                    t = take("dve").rearrange("p (m k) -> p m k", m=TM)
                    if mask is None:
                        VE.tensor_copy(p[i % 2], t).then_inc(S["scores_taken"], 1)
                        VE.wait_ge(S["scores_taken"], S.nth(VE, "scores_taken"))
                    else:
                        VE.tensor_tensor(p[i % 2], t, mask, ALU.add).then_inc(S["scores_taken"], 1)
                        VE.wait_ge(S["scores_taken"], S.nth(VE, "scores_taken"))
                    o = 4 * (i % 2)
                    VE.tensor_reduce(st[:, o:o + 2], p[i % 2], AX, ALU.max).then_inc(S["dve_step"], 1)
                    VE.wait_ge(S["dve_step"], S.nth(VE, "dve_step"))
                    VE.tensor_scalar(st[:, o:o + 2], st[:, o:o + 2], -scale, None, ALU.mult).then_inc(S["row_max"], 1)
                    VE.wait_ge(S["row_max"], S.nth(VE, "row_max"))
                if 1 <= i <= H:
                    k = (i - 1) % 2
                    VE.wait_ge(S["exps"], S.nth(VE, "exps"))
                    VE.reciprocal(st[:, 4 * k + 2:4 * k + 4], st[:, 4 * k + 2:4 * k + 4]).then_inc(S["dve_step"], 1)
                    VE.wait_ge(S["dve_step"], S.nth(VE, "dve_step"))
                    for t in range(TM):
                        signal = "probs_ready" if t else "dve_step"
                        VE.tensor_scalar(p[k][:, t, :], p[k][:, t, :], st[:, 4 * k + 2 + t:4 * k + 3 + t], None,
                            ALU.mult).then_inc(S[signal], 1)
                        VE.wait_ge(S[signal], S.nth(VE, signal))

        def value_product(v, cols, b, half, pt):
            for j in range(TM):
                m = mm(ps[0:cols.stop - cols.start, b, half * T:(half + 1) * T], v[:, j, cols], pt[:, j, :],
                       start=(j == 0), stop=(j == TM - 1))
            return m

        def plan_cols(name, w, lo, hi):
            K = w.shape[0]
            kc = K // P
            per = RING_W // kc
            v = w.rearrange("(c p) n -> p c n", p=P)
            for n0 in range(lo, hi, per):
                n = min(per, hi - n0)
                plan(name, v[:, :, n0:n0 + n], kc, n)

        def plan_mod(L):
            plan_cols(f"mod{L}", a["mod_w"][L], 0, 6 * D)

        def plan_hybrid():
            w = a["hy_w_in"][0]
            plan_cols("gdn_qkv", w, 0, 1536)
            plan_cols("gdn_z", w, 1536, 2048)
            plan("gdn_ba", w.rearrange("(c p) n -> p c n", p=P)[:, :, 2048:2056], DC, 8)
            plan_cols("moba_q", w, 2056, 2568)
            plan_cols("moba_k", w, 2568, 3080)
            plan_cols("moba_v", w, 3080, 3592)
            plan_cols("hy_out", a["hy_w_out"][0], 0, D)

        def plan_mla():
            plan_cols("mla_cq", a["mla_w_in"][0], 0, 512)
            plan_cols("mla_ckv", a["mla_w_in"][0], 512, 768)
            plan_cols("mla_kr", a["mla_kr"], 0, P)
            plan_cols("mla_qn", a["mla_uqn"], 0, 1024)
            plan_cols("mla_qr", a["mla_uqr"], 0, 512)
            plan_cols("mla_kn", a["mla_ukn"], 0, 1024)
            plan_cols("mla_v", a["mla_uv"], 0, 1024)
            plan_cols("mla_out", a["mla_w_out"][0], 0, D)

        def plan_peer(L):
            plan_cols("peer_q", a["peer_w_q"][L], 0, HP * P)
            plan("sub_keys", a["sub_keys"][L].rearrange("(c p) n -> p c n", p=P), HP, NKEY)
            before.setdefault(len(weights), []).append(lambda: peer_sp(L))

        def plan_second(L):
            w = a["w_in_2"][L]
            plan("hyena_net", None, 1, FT + 128, P, hyena_pieces(L))
            plan_cols("att_q", w, 0, 512)
            plan_cols("att_k", a["att_kdup"][L], 0, 256)
            plan_cols("att_v", w, 640, 768)
            plan_cols("hyena_in", w, 768, 2304)
            plan_cols("gla_qk", w, 2304, 2816)
            plan_cols("gla_v", w, 2816, 3328)
            plan_cols("gla_o", w, 3328, 3840)
            plan_cols("gla_lr", a["gla_lrdup"][L], 0, 64)
            plan("gla_net", None, 1, 256, P, gla_pieces(L))
            for i, br in enumerate(("w_br_attn_2", "w_br_hyena_2", "w_br_gla_2")):
                plan_cols("gate", w, 3872 + i * D, 3872 + (i + 1) * D)
                plan_cols("branch", a[br][L], 0, D)
            plan_cols("mix_out", a["w_out_2"][L], 0, D)
            plan("mem", a["memT"].rearrange("(c p) n -> p c n", p=P), DC, T)
            plan_cols("x_k", a["x_wk_2"][L], 0, D)
            plan_cols("x_v", a["x_wv_2"][L], 0, D)
            plan_cols("x_q", a["x_wq_2"][L], 0, D)
            plan_cols("x_o", a["x_wo_2"][L], 0, D)
            plan_cols("mlp1", a["mlp_w1_2"][L], 0, D_FF)
            plan_cols("mlp2", a["mlp_w2_2"][L], 0, D)

        def hyena_pieces(L):
            row = lambda v: v.rearrange("(a n) -> a n", a=1)
            return [(0, 64, 0, FT, a["hy_w3_2"][L]), (64, 1, 0, FT, row(a["hy_b3_2"][L])),
                    (0, 33, FT, 64, a["hy_w1_2"][L]), (0, 64, FT + 64, 64, a["hy_w2_2"][L])]

        def gla_pieces(L):
            row = lambda v: v.rearrange("(a n) -> a n", a=1)
            return [(0, 16, 0, 256, a["gla_w_lr_2"][L, 0]), (16, 1, 0, 256, row(a["gla_b_lr_2"][L, 0])),
                    (32, 16, 0, 256, a["gla_w_lr_2"][L, 1]), (48, 1, 0, 256, row(a["gla_b_lr_2"][L, 1]))]

        def mod_pe(L):
            if L == 0:
                TE.wait_ge(S["cond_ready"], S.nth(TE, "cond_ready"))
            for i in range(12):
                w_i, w = next_weight(f"mod{L}")
                b = acquire("dve")
                for j in range(4):
                    for k in range(DC):
                        m = mm(ps[:, b, j:j + 1], w[:, k, j * P:(j + 1) * P], condv[:, k:k + 1],
                               start=(k == 0), stop=(k == DC - 1))
                m.then_inc(S["tile_for_dve"], 1)
                frees(b, "mod_part")
                last_use(w_i, ("mod_part", expected["mod_part"]))

        condv = small[:, 8:16]

        def mod_act(L):
            if L == 0:
                SE.wait_ge(S["inputs_ready"], S.nth(SE, "inputs_ready"))
                SE.activation(condv, V["cond"], ACT.Silu).then_inc(S["cond_ready"], 1)
                SE.wait_ge(S["cond_ready"], S.nth(SE, "cond_ready"))

        def mod_dve(L):
            m = modv[:, 48 * L:48 * L + 48]
            bias = V["mod_b"][:, 48 * L:48 * L + 48]
            for i in range(12):
                VE.tensor_tensor(m[:, 4 * i:4 * i + 4], take("dve")[:, 0:4], bias[:, 4 * i:4 * i + 4],
                    ALU.add).then_inc(S["mod_part"], 1)
                VE.wait_ge(S["mod_part"], S.nth(VE, "mod_part"))
            for which, norm in ((1, "norm_mix"), (4, "norm_ffn")):
                col = m[:, 8 * which:8 * which + 8]
                VE.scalar_tensor_tensor(out=col, in0=col, scalar=1.0, in1=V[norm][:, 8 * L:8 * L + 8], op0=ALU.add,
                    op1=ALU.mult).then_inc(S["dve_step"], 1)
                VE.wait_ge(S["dve_step"], S.nth(VE, "dve_step"))

        def mod_cols(L, which):
            return modv[:, 48 * L + 8 * which:48 * L + 8 * which + 8]

        TWO_PI = 2 * np.pi
        C1 = 6.28125
        C2 = float(np.float32(np.round((TWO_PI - C1) * 2 ** 21) / 2 ** 21))
        C3 = float(TWO_PI - C1 - C2)
        MAGIC = 1.5 * 2 ** 23
        PI_IN = 3.1415925

        def reduced_dve(dst, ang, shift, turns, name):
            VE.tensor_scalar(turns, ang, 1 / TWO_PI, shift / TWO_PI, ALU.mult, ALU.add).then_inc(S["dve_step"], 1)
            VE.wait_ge(S["dve_step"], S.nth(VE, "dve_step"))
            VE.tensor_scalar(turns, turns, MAGIC, MAGIC, ALU.add, ALU.subtract).then_inc(S["dve_step"], 1)
            VE.wait_ge(S["dve_step"], S.nth(VE, "dve_step"))
            VE.scalar_tensor_tensor(out=dst, in0=turns, scalar=-C1, in1=ang, op0=ALU.mult,
                op1=ALU.add).then_inc(S["dve_step"], 1)
            VE.wait_ge(S["dve_step"], S.nth(VE, "dve_step"))
            VE.scalar_tensor_tensor(out=dst, in0=turns, scalar=-C2, in1=dst, op0=ALU.mult,
                op1=ALU.add).then_inc(S["dve_step"], 1)
            VE.wait_ge(S["dve_step"], S.nth(VE, "dve_step"))
            VE.scalar_tensor_tensor(out=dst, in0=turns, scalar=-C3, in1=dst, op0=ALU.mult,
                op1=ALU.add).then_inc(S["dve_step"], 1)
            VE.wait_ge(S["dve_step"], S.nth(VE, "dve_step"))
            if shift:
                VE.tensor_scalar(dst, dst, shift, None, ALU.add).then_inc(S["dve_step"], 1)
                VE.wait_ge(S["dve_step"], S.nth(VE, "dve_step"))
            VE.tensor_scalar(dst, dst, -PI_IN, PI_IN, ALU.max, ALU.min).then_inc(S[name], 1)
            VE.wait_ge(S[name], S.nth(VE, name))

        def rope_dve(which, cosv, sinv, posf, tmp, turns):
            VE.tensor_copy(posf, pos_in).then_inc(S["dve_step"], 1)
            VE.wait_ge(S["dve_step"], S.nth(VE, "dve_step"))
            VE.tensor_scalar(tmp, posf, C["invf"][:, which:which + 1], None, ALU.mult).then_inc(S["dve_step"], 1)
            VE.wait_ge(S["dve_step"], S.nth(VE, "dve_step"))
            reduced_dve(sinv, tmp, 0.0, turns, "angles")
            reduced_dve(cosv, tmp, float(np.pi / 2), turns, "angles")
            VE.wait_ge(S["tables"], S.nth(VE, "tables", 2))

        def rope_act(cosv, sinv):
            for v in (sinv, cosv):
                SE.wait_ge(S["angles"], S.nth(SE, "angles"))
                SE.activation(v, v, ACT.Sin).then_inc(S["tables"], 1)
                SE.wait_ge(S["tables"], S.nth(SE, "tables"))

        def rotate_pe(name, q, nchunk, rot, rows=P):
            TE.wait_ge(S[name], expected[name])
            for c0 in range(0, nchunk, 2):
                b = acquire("dve")
                for c in range(c0, min(c0 + 2, nchunk)):
                    m = mm(ps[:, b, (c - c0) * T:(c - c0 + 1) * T], rot, q[:, c, :], start=True, stop=True)
                m.then_inc(S["tile_for_dve"], 1)
                frees(b, "rotated")

        def rotate_dve(q, nchunk, cosv, sinv, tmp, name):
            for c0 in range(0, nchunk, 2):
                n = min(2, nchunk - c0)
                t = take("dve")[:, 0:n * T].rearrange("p (c n) -> p c n", n=T)
                bc = lambda v: v.unsqueeze(1).to_broadcast([P, n, T])
                VE.tensor_tensor(tmp[:, 0:n, :], t, bc(sinv), ALU.mult).then_inc(S["rotated"], 1)
                VE.wait_ge(S["rotated"], S.nth(VE, "rotated"))
                VE.tensor_tensor(q[:, c0:c0 + n, :], q[:, c0:c0 + n, :], bc(cosv), ALU.mult).then_inc(S["dve_step"],
                    1)
                VE.wait_ge(S["dve_step"], S.nth(VE, "dve_step"))
                signal = name if c0 + 2 >= nchunk else "dve_step"
                VE.tensor_tensor(q[:, c0:c0 + n, :], q[:, c0:c0 + n, :], tmp[:, 0:n, :], ALU.add).then_inc(S[signal],
                    1)
                VE.wait_ge(S[signal], S.nth(VE, signal))

        class Z:
            pass

        def hybrid_places():
            z, r = Z(), Scratch(True)
            z.pad = r.get(12 * 260).rearrange("p (c n) -> p c n", n=260)
            z.conv = r.mat(12)
            z.q, z.k, z.v = z.conv[:, 0:4, :], z.conv[:, 4:8, :], z.conv[:, 8:12, :]
            z.z = r.mat(4)
            z.sq = r.mat(8)
            z.rs = r.mat(8)
            z.ba = r.get(16).rearrange("p (m n) -> p m n", m=TM)
            z.bb = r.get(16).rearrange("p (m n) -> p m n", m=TM)
            z.g = r.get(8).rearrange("p (m n) -> p m n", m=TM)
            z.beta = r.get(8).rearrange("p (m n) -> p m n", m=TM)
            z.nbeta = r.get(8).rearrange("p (m n) -> p m n", m=TM)
            z.al = r.get(8)
            z.cum = r.get(32)
            z.ncum = r.get(8).rearrange("p (m n) -> p m n", m=TM)
            z.ktm = r.get(1024).rearrange("p (m h d) -> p m h d", m=TM, h=GH)
            z.kbeg = r.get(1024).rearrange("p (m h d) -> p m h d", m=TM, h=GH)
            z.kdec = z.ktm
            z.vb = r.get(1024).rearrange("p (m h d) -> p m h d", m=TM, h=GH)
            pairs8 = lambda: r.get(1024).rearrange("p (g n) -> p g n", g=8)
            z.dec, z.decT, z.R, z.N, z.NT, z.inv, z.qk = (pairs8() for _ in range(7))
            z.u = pairs8()
            z.wT = z.dec
            z.state = r.get(512).rearrange("p (h d) -> p h d", h=GH)
            z.vnew = r.get(512).rearrange("p (h d) -> p h d", h=GH)
            z.o = r.mat(4)
            z.keep = z.sq[:, 0:4, :]
            r2 = Scratch(True)
            z.aq, z.ak = r2.mat(4), r2.mat(4)
            z.av = r2.get(1024).rearrange("p (m n) -> p m n", m=TM)
            z.p = [r2.mat(2) for _ in range(2)]
            z.pt = [r2.mat(2) for _ in range(2)]
            z.st = r2.get(8)
            z.cos, z.sin, z.pos, z.t1, z.t2 = (r2.get(T) for _ in range(5))
            z.tmp = r2.mat(2)
            return z

        zh = hybrid_places()
        DK = 128
        lastdim = lambda v, n: v.unsqueeze(len(v.shape)).to_broadcast(list(v.shape) + [n])

        def hybrid_pe():
            z = zh
            block_norm_pe(z.sq)
            TE.wait_ge(S["h_ready"], S.nth(TE, "h_ready"))
            fm_linear("gdn_qkv", h, DC, 1536, "act", "qkv_out")
            fm_linear("gdn_z", h, DC, 512, "act", "z_out")
            tm_linear("gdn_ba", h, DC, 8, "dve", "ba_out")
            norm_pe([[c] for c in range(8)], 8, C["ones"], z.sq)
            TE.wait_ge(S["gates_log"], S.nth(TE, "gates_log"))
            b = acquire("dve")
            for m_ in range(TM):
                mm(ps[:, b, 8 * m_:8 * m_ + 4], C["upto"], z.g[:, m_, :], start=True, stop=True)
                mm(ps[:, b, 8 * m_ + 4:8 * m_ + 8], C["later"], z.g[:, m_, :], start=True, stop=True)
            for c in range(NCH):
                r0 = GC * (c % 2)
                i = mm(ps[:, b, 16 + 4 * c:20 + 4 * c], C["blk"][:, r0:r0 + 1].to_broadcast([P, P]), z.g[:, c // 2, :],
                       start=True, stop=True)
            i.then_inc(S["tile_for_dve"], 1)
            frees(b, "gate_sums")
            TE.wait_ge(S["gate_masks"], S.nth(TE, "gate_masks"))
            for m_ in range(TM):
                b = acquire("dve")
                i = mm(ps[:, b, :], C["ones"], z.N[:, 4 * m_:4 * m_ + 4, :], start=True, stop=True)
                i.then_inc(S["tile_for_dve"], 1)
                frees(b, "gate_rows")
            TE.wait_ge(S["qk_normed"], S.nth(TE, "qk_normed"))
            for src, pool, name in ((z.k, "act", "k_turned"), (z.v, "dve", "v_turned")):
                for m_ in range(TM):
                    b = acquire(pool)
                    for g in range(GH):
                        i = TE.transpose(ps[:, b, g * P:(g + 1) * P], src[:, g, m_ * P:(m_ + 1) * P], C["ident"])
                    i.then_inc(S[filled[pool]], 1)
                    frees(b, name)
            for lhs, rhs, name in ((z.k, z.k, "kk_out"), (z.k, z.q, "kq_out")):
                for m_ in range(TM):
                    b = acquire("dve")
                    tok = slice(m_ * P, (m_ + 1) * P)
                    for g in range(GH):
                        i = mm(ps[:, b, g * P:(g + 1) * P], lhs[:, g, tok], rhs[:, g, tok], start=True, stop=True)
                    i.then_inc(S["tile_for_dve"], 1)
                    frees(b, name)
            TE.wait_ge(S["n_ready"], S.nth(TE, "n_ready"))
            for m_ in range(TM):
                b = acquire("act")
                for g in range(GH):
                    i = TE.transpose(ps[:, b, g * P:(g + 1) * P], z.N[:, 4 * m_ + g, :], C["ident"])
                i.then_inc(S["tile_for_act"], 1)
                frees(b, "powers")
            for r in range(5):
                TE.wait_ge(S["powers"], expected["powers"])
                for lhs, rhs in ((z.NT, z.N),) + (((z.N, z.NT),) if r < 4 else ()):
                    for m_ in range(TM):
                        b = acquire("act")
                        for g in range(4 * m_, 4 * m_ + 4):
                            i = mm(ps[:, b, (g % 4) * P:(g % 4 + 1) * P], lhs[:, g, :], rhs[:, g, :],
                                   start=True, stop=True)
                        i.then_inc(S["tile_for_act"], 1)
                        frees(b, "powers")
                TE.wait_ge(S["powers"], expected["powers"])
                TE.wait_ge(S["inverse"], S.nth(TE, "inverse"))
                for m_ in range(TM):
                    b = acquire("dve")
                    for g in range(4 * m_, 4 * m_ + 4):
                        i = mm(ps[:, b, (g % 4) * P:(g % 4 + 1) * P], z.N[:, g, :], z.inv[:, g, :],
                               start=True, stop=True)
                    i.then_inc(S["tile_for_dve"], 1)
                    frees(b, "inverse_part")
            TE.wait_ge(S["inverse"], S.nth(TE, "inverse"))
            TE.wait_ge(S["k_scaled"], S.nth(TE, "k_scaled"))
            for m_ in range(TM):
                b = acquire("act")
                for g in range(GH):
                    i = mm(ps[:, b, g * P:(g + 1) * P], z.inv[:, 4 * m_ + g, :], z.vb[:, m_, g, :], start=True, stop=True)
                i.then_inc(S["tile_for_act"], 1)
                frees(b, "uw_out")
            for m_ in range(TM):
                b = acquire("act")
                for g in range(GH):
                    i = mm(ps[:, b, g * P:(g + 1) * P], z.kbeg[:, m_, g, :], z.inv[:, 4 * m_ + g, :],
                           start=True, stop=True)
                i.then_inc(S["tile_for_act"], 1)
                frees(b, "uw_out")
            TE.wait_ge(S["uw_out"], expected["uw_out"])
            for c in range(NCH):
                m_, r0 = c // 2, GC * (c % 2)
                rows = slice(r0, r0 + GC)
                TE.wait_ge(S["state_ready"], S.nth(TE, "state_ready"))
                b = acquire("dve")
                for g in range(GH):
                    i = mm(ps[:, b, g * P:(g + 1) * P], z.wT[:, 4 * m_ + g, :], z.state[:, g, :], start=True, stop=True)
                i.then_inc(S["tile_for_dve"], 1)
                frees(b, "v_new")
                TE.wait_ge(S["v_new"], expected["v_new"])
                b = acquire("act")
                for g in range(GH):
                    mm(ps[:, b, g * GC:(g + 1) * GC], z.state[:, g, :], z.q[:, g, c * GC:(c + 1) * GC],
                       start=True, stop=False)
                    i = mm(ps[:, b, g * GC:(g + 1) * GC], z.vnew[rows, g, :], z.qk[rows, 4 * m_ + g, rows],
                           start=False, stop=True)
                i.then_inc(S["tile_for_act"], 1)
                frees(b, "delta_out")
                if c < NCH - 1:
                    b = acquire("dve")
                    for g in range(GH):
                        i = mm(ps[:, b, g * P:(g + 1) * P], z.kdec[rows, m_, g, :], z.vnew[rows, g, :],
                               start=True, stop=True)
                    i.then_inc(S["tile_for_dve"], 1)
                    frees(b, "state_grown")
            norm_pe([[c] for c in range(4)], 4, C["ones"], z.sq)
            TE.wait_ge(S["delta_through"], S.nth(TE, "delta_through"))
            fm_linear("moba_q", h, DC, 512, "act", "att_in")
            fm_linear("moba_k", h, DC, 512, "act", "att_in")
            tm_linear("moba_v", h, DC, 512, "act", "att_in")
            rotate_pe("att_in", z.aq, 4, C["rot128"])
            rotate_pe("att_in", z.ak, 4, C["rot128"])
            TE.wait_ge(S["k_rotated"], S.nth(TE, "k_rotated"))

            def scores(i, b):
                for t in range(TM):
                    m = mm(ps[:, b, t * T:(t + 1) * T], z.aq[:, i, t * P:(t + 1) * P], z.ak[:, i, :],
                           start=True, stop=True)
                return m

            def values(i, pt):
                b = acquire("dve")
                value_product(z.av, slice(i * P, (i + 1) * P), b, 0, pt).then_inc(S["tile_for_dve"], 1)
                frees(b, "o_out")
            attention_pe(4, scores, values, z.p, z.pt)
            TE.wait_ge(S["o_out"], expected["o_out"])
            fm_linear("hy_out", h, DC, D, "dve", "residual_in")

        def hybrid_act():
            z = zh
            block_norm_act(z.sq, z.rs)
            evict_act([z.pad[:, c:c + 2, 4:260] for c in range(0, 12, 2)], frees="qkv_out", n=6)
            evict_act(pairs(z.z), ACT.Silu, frees="z_out", n=2)
            SE.wait_ge(S["conv_done"], S.nth(SE, "conv_done"))
            SE.activation(z.conv, z.conv, ACT.Silu).then_inc(S["silu_done"], 1)
            SE.wait_ge(S["silu_done"], S.nth(SE, "silu_done"))
            norm_act(z.conv[:, 0:8, :], z.sq, z.rs, 8, 1.0)
            SE.wait_ge(S["ba_ready"], S.nth(SE, "ba_ready"))
            SE.activation(z.bb, z.bb, ACT.Exp, scale=-1.0).then_inc(S["act_step"], 1)
            SE.wait_ge(S["act_step"], S.nth(SE, "act_step"))
            SE.activation(z.al[:, 0:4], z.al[:, 0:4], ACT.Exp).then_inc(S["ba_exp"], 1)
            SE.wait_ge(S["ba_exp"], S.nth(SE, "ba_exp"))
            SE.activation(z.ba[:, :, 4:8], z.bb[:, :, 4:8], ACT.Ln, bias=1.0).then_inc(S["ba_ln"], 1)
            SE.wait_ge(S["ba_ln"], S.nth(SE, "ba_ln"))
            SE.wait_ge(S["decay_rows"], S.nth(SE, "decay_rows"))
            for g in range(8):
                m_, hh = g // 4, g % 4
                SE.activation(z.dec[:, g, :], z.dec[:, g, :], ACT.Exp,
                    bias=z.cum[:, 8 * m_ + hh:8 * m_ + hh + 1]).then_inc(S["act_step"], 1)
                SE.wait_ge(S["act_step"], S.nth(SE, "act_step"))
                SE.activation(z.decT[:, g, :], z.decT[:, g, :], ACT.Exp,
                    bias=z.ncum[:, m_, hh:hh + 1]).then_inc(S["act_step"], 1)
                SE.wait_ge(S["act_step"], S.nth(SE, "act_step"))
            SE.activation(z.R, z.R, ACT.Exp).then_inc(S["act_step"], 1)
            SE.wait_ge(S["act_step"], S.nth(SE, "act_step"))
            SE.activation(z.cum, z.cum, ACT.Exp).then_inc(S["decays"], 1)
            SE.wait_ge(S["decays"], S.nth(SE, "decays"))
            evict_act([z.ktm[:, m_] .rearrange("p h d -> p (h d)") for m_ in range(TM)], frees="k_turned", n=2)
            g4 = lambda v, m_: v[:, 4 * m_:4 * m_ + 4, :]
            evict_act([g4(z.NT, m_) for m_ in range(TM)], frees="powers", n=2)
            SE.wait_ge(S["inverse"], S.nth(SE, "inverse"))
            for r in range(5):
                k = 2 if r == 4 else 4
                got = [take("act") for _ in range(k)]
                for j, t in enumerate(got):
                    SE.activation(g4((z.N, z.NT)[j // 2], j % 2), t.rearrange("p (c n) -> p c n", c=4),
                        ACT.Copy).then_inc(S["powers"], 1)
                    SE.wait_ge(S["powers"], S.nth(SE, "powers"))
            evict_act([g4(z.u, 0), g4(z.u, 1)], frees="uw_out", n=2)
            evict_act([g4(z.wT, 0), g4(z.wT, 1)], frees="uw_out", n=2)
            for c in range(NCH):
                evict_act([z.o[:, :, c * GC:(c + 1) * GC]], frees="delta_out")
            norm_act(z.o, z.sq[:, 0:4, :], z.rs, 4, 128.0)
            SE.wait_ge(S["delta_through"], S.nth(SE, "delta_through"))
            evict_act(pairs(z.aq) + pairs(z.ak) + [z.av[:, 0, :], z.av[:, 1, :]], frees="att_in", n=6)
            rope_act(z.cos, z.sin)
            attention_act(4, z.p, z.pt, 128 ** -0.5, z.st)

        def hybrid_dve():
            z = zh
            block_norm_dve(z.rs, mod_cols(0, 1), mod_cols(0, 0))
            VE.memset(z.pad[:, :, 0:4], 0.0).then_inc(S["dve_step"], 1)
            VE.wait_ge(S["dve_step"], S.nth(VE, "dve_step"))
            VE.wait_ge(S["qkv_out"], S.nth(VE, "qkv_out", 6))
            w = V["gdn_conv"].rearrange("p (c j) -> p c j", j=4)
            for c in range(12):
                for j in range(4):
                    src = z.pad[:, c, 1 + j:1 + j + T]
                    if j == 0:
                        VE.tensor_scalar(z.conv[:, c, :], src, w[:, c, 0:1], None, ALU.mult).then_inc(S["dve_step"],
                            1)
                        VE.wait_ge(S["dve_step"], S.nth(VE, "dve_step"))
                    else:
                        signal = "conv_done" if (c, j) == (11, 3) else "dve_step"
                        VE.scalar_tensor_tensor(out=z.conv[:, c, :], in0=src, scalar=w[:, c, j:j + 1],
                            in1=z.conv[:, c, :], op0=ALU.mult, op1=ALU.add).then_inc(S[signal], 1)
                        VE.wait_ge(S[signal], S.nth(VE, signal))
            for m_ in range(TM):
                VE.tensor_copy(z.ba[:, m_, :], take("dve")[:, 0:8]).then_inc(S["ba_out"], 1)
                VE.wait_ge(S["ba_out"], S.nth(VE, "ba_out"))
            VE.tensor_copy(z.bb[:, :, 0:4], z.ba[:, :, 0:4]).then_inc(S["dve_step"], 1)
            VE.wait_ge(S["dve_step"], S.nth(VE, "dve_step"))
            VE.tensor_tensor(z.g, z.ba[:, :, 4:8], z.al[:, 4:8].unsqueeze(1).to_broadcast([P, TM, 4]),
                ALU.add).then_inc(S["dve_step"], 1)
            VE.wait_ge(S["dve_step"], S.nth(VE, "dve_step"))
            VE.scalar_tensor_tensor(out=z.bb[:, :, 4:8], in0=z.g, scalar=-1.0, in1=z.g, op0=ALU.mult,
                op1=ALU.max).then_inc(S["ba_ready"], 1)
            VE.wait_ge(S["ba_ready"], S.nth(VE, "ba_ready"))
            VE.wait_ge(S["ba_exp"], S.nth(VE, "ba_exp"))
            VE.tensor_scalar(z.beta, z.bb[:, :, 0:4], 1.0, None, ALU.add).then_inc(S["dve_step"], 1)
            VE.wait_ge(S["dve_step"], S.nth(VE, "dve_step"))
            VE.reciprocal(z.beta, z.beta).then_inc(S["dve_step"], 1)
            VE.wait_ge(S["dve_step"], S.nth(VE, "dve_step"))
            VE.tensor_scalar(z.nbeta, z.beta, -1.0, None, ALU.mult).then_inc(S["dve_step"], 1)
            VE.wait_ge(S["dve_step"], S.nth(VE, "dve_step"))
            VE.wait_ge(S["ba_ln"], S.nth(VE, "ba_ln"))
            VE.scalar_tensor_tensor(out=z.g, in0=z.g, scalar=0.0, in1=z.ba[:, :, 4:8], op0=ALU.max,
                op1=ALU.add).then_inc(S["dve_step"], 1)
            VE.wait_ge(S["dve_step"], S.nth(VE, "dve_step"))
            VE.tensor_scalar(z.g, z.g, -1.0, None, ALU.mult).then_inc(S["dve_step"], 1)
            VE.wait_ge(S["dve_step"], S.nth(VE, "dve_step"))
            VE.tensor_tensor(z.g, z.g, z.al[:, 0:4].unsqueeze(1).to_broadcast([P, TM, 4]),
                ALU.mult).then_inc(S["gates_log"], 1)
            VE.wait_ge(S["gates_log"], S.nth(VE, "gates_log"))
            for g in range(8):
                signal = "gate_masks" if g == 7 else "dve_step"
                VE.tensor_scalar(z.N[:, g, :], C["upto"], z.g[:, g // 4, g % 4:g % 4 + 1], None,
                    ALU.mult).then_inc(S[signal], 1)
                VE.wait_ge(S[signal], S.nth(VE, signal))
            norm_dve(z.rs, 8)
            VE.tensor_tensor(z.conv[:, 0:8, :], z.conv[:, 0:8, :], z.rs, ALU.mult).then_inc(S["dve_step"], 1)
            VE.wait_ge(S["dve_step"], S.nth(VE, "dve_step"))
            VE.tensor_scalar(z.q, z.q, float(DK) ** -0.5, None, ALU.mult).then_inc(S["qk_normed"], 1)
            VE.wait_ge(S["qk_normed"], S.nth(VE, "qk_normed"))
            VE.tensor_copy(z.cum, take("dve")[:, 0:32]).then_inc(S["gate_sums"], 1)
            VE.wait_ge(S["gate_sums"], S.nth(VE, "gate_sums"))
            gcv = z.cum[:, 0:16].rearrange("p (m n) -> p m n", m=TM)
            VE.tensor_scalar(z.ncum, gcv[:, :, 0:4], -1.0, None, ALU.mult).then_inc(S["dve_step"], 1)
            VE.wait_ge(S["dve_step"], S.nth(VE, "dve_step"))
            bc4 = lambda v: v.unsqueeze(1).to_broadcast([P, 4, P])
            for m_ in range(TM):
                t = take("dve").rearrange("p (c n) -> p c n", c=4)
                s4 = slice(4 * m_, 4 * m_ + 4)
                VE.scalar_tensor_tensor(out=z.dec[:, s4, :], in0=t, scalar=-1.0, in1=bc4(C["mlow"]), op0=ALU.mult,
                    op1=ALU.add).then_inc(S["dve_step"], 1)
                VE.wait_ge(S["dve_step"], S.nth(VE, "dve_step"))
                VE.tensor_tensor(z.decT[:, s4, :], t, bc4(C["mup"]), ALU.add).then_inc(S["dve_step"], 1)
                VE.wait_ge(S["dve_step"], S.nth(VE, "dve_step"))
                VE.tensor_copy(z.R[:, s4, :], t).then_inc(S["gate_rows"], 1)
                VE.wait_ge(S["gate_rows"], S.nth(VE, "gate_rows"))
            VE.memset(z.state, 0.0).then_inc(S["decay_rows"], 1)
            VE.wait_ge(S["decay_rows"], S.nth(VE, "decay_rows"))
            VE.wait_ge(S["decays"], S.nth(VE, "decays"))
            for m_ in range(TM):
                t = take("dve").rearrange("p (h d) -> p h d", h=GH)
                VE.tensor_tensor(z.vb[:, m_], t, lastdim(z.beta[:, m_, :], P), ALU.mult).then_inc(S["v_turned"], 1)
                VE.wait_ge(S["v_turned"], S.nth(VE, "v_turned"))
            VE.wait_ge(S["k_turned"], S.nth(VE, "k_turned", 2))
            for m_ in range(TM):
                VE.tensor_tensor(z.ncum[:, m_, :], z.beta[:, m_, :], gcv[:, m_, 0:4],
                    ALU.mult).then_inc(S["dve_step"], 1)
                VE.wait_ge(S["dve_step"], S.nth(VE, "dve_step"))
                VE.tensor_tensor(z.kbeg[:, m_], z.ktm[:, m_], lastdim(z.ncum[:, m_, :], P),
                    ALU.mult).then_inc(S["dve_step"], 1)
                VE.wait_ge(S["dve_step"], S.nth(VE, "dve_step"))
                VE.tensor_tensor(z.kdec[:, m_], z.ktm[:, m_], lastdim(gcv[:, m_, 4:8], P),
                    ALU.mult).then_inc(S["dve_step"], 1)
                VE.wait_ge(S["dve_step"], S.nth(VE, "dve_step"))
            for m_ in range(TM):
                t = take("dve").rearrange("p (c n) -> p c n", c=4)
                s4 = slice(4 * m_, 4 * m_ + 4)
                VE.tensor_tensor(z.N[:, s4, :], t, z.dec[:, s4, :], ALU.mult).then_inc(S["kk_out"], 1)
                VE.wait_ge(S["kk_out"], S.nth(VE, "kk_out"))
                for g in range(4 * m_, 4 * m_ + 4):
                    signal = "n_ready" if g == 7 else "dve_step"
                    VE.scalar_tensor_tensor(out=z.N[:, g, :], in0=z.N[:, g, :],
                        scalar=z.nbeta[:, m_,
                        g % 4:g % 4 + 1], in1=C["later"], op0=ALU.mult, op1=ALU.mult).then_inc(S[signal], 1)
                    VE.wait_ge(S[signal], S.nth(VE, signal))
            for m_ in range(TM):
                t = take("dve").rearrange("p (c n) -> p c n", c=4)
                s4 = slice(4 * m_, 4 * m_ + 4)
                VE.tensor_tensor(z.qk[:, s4, :], t, z.decT[:, s4, :], ALU.mult).then_inc(S["kq_out"], 1)
                VE.wait_ge(S["kq_out"], S.nth(VE, "kq_out"))
            qv = z.q.rearrange("p h (m t) -> p m h t", m=TM)
            VE.tensor_tensor(qv, qv, z.R.rearrange("p (m h) t -> p m h t", m=TM), ALU.mult).then_inc(S["k_scaled"], 1)
            VE.wait_ge(S["k_scaled"], S.nth(VE, "k_scaled"))
            VE.wait_ge(S["powers"], S.nth(VE, "powers", 2))
            for m_ in range(TM):
                signal = "inverse" if m_ else "dve_step"
                VE.tensor_tensor(z.inv[:, 4 * m_:4 * m_ + 4, :], z.NT[:, 4 * m_:4 * m_ + 4, :], bc4(C["ident"]),
                    ALU.add).then_inc(S[signal], 1)
                VE.wait_ge(S[signal], S.nth(VE, signal))
            for r in range(5):
                for m_ in range(TM):
                    t = take("dve").rearrange("p (c n) -> p c n", c=4)
                    s4 = slice(4 * m_, 4 * m_ + 4)
                    VE.tensor_tensor(z.inv[:, s4, :], z.inv[:, s4, :], t, ALU.add).then_inc(S["inverse_part"], 1)
                    VE.wait_ge(S["inverse_part"], S.nth(VE, "inverse_part"))
                VE.tensor_scalar(small[:, 2:3], small[:, 0:1], 1.0, None, ALU.mult).then_inc(S["inverse"], 1)
                VE.wait_ge(S["inverse"], S.nth(VE, "inverse"))
            VE.wait_ge(S["uw_out"], S.nth(VE, "uw_out", 4))
            VE.tensor_scalar(small[:, 2:3], small[:, 0:1], 1.0, None, ALU.mult).then_inc(S["state_ready"], 1)
            VE.wait_ge(S["state_ready"], S.nth(VE, "state_ready"))
            for c in range(NCH):
                m_, r0 = c // 2, GC * (c % 2)
                rows = slice(r0, r0 + GC)
                t = take("dve").rearrange("p (h d) -> p h d", h=GH)
                VE.tensor_tensor(z.vnew[rows], z.u[rows, 4 * m_:4 * m_ + 4, :], t[rows],
                    ALU.subtract).then_inc(S["v_new"], 1)
                VE.wait_ge(S["v_new"], S.nth(VE, "v_new"))
                if c < NCH - 1:
                    t = take("dve").rearrange("p (h d) -> p h d", h=GH)
                    VE.tensor_tensor(z.state, z.state, lastdim(z.cum[:, 16 + 4 * c:20 + 4 * c], P),
                        ALU.mult).then_inc(S["dve_step"], 1)
                    VE.wait_ge(S["dve_step"], S.nth(VE, "dve_step"))
                    VE.tensor_tensor(z.state, z.state, t, ALU.add).then_inc(S["state_grown"], 1)
                    VE.wait_ge(S["state_grown"], S.nth(VE, "state_grown"))
                    VE.tensor_scalar(small[:, 2:3], small[:, 0:1], 1.0, None, ALU.mult).then_inc(S["state_ready"], 1)
                    VE.wait_ge(S["state_ready"], S.nth(VE, "state_ready"))
            norm_dve(z.rs, 4)
            for g in range(GH):
                VE.scalar_tensor_tensor(out=z.o[:, g, :], in0=z.o[:, g, :], scalar=V["gdn_o_norm"][:, 0:1],
                    in1=z.rs[:, g, :], op0=ALU.mult, op1=ALU.mult).then_inc(S["dve_step"], 1)
                VE.wait_ge(S["dve_step"], S.nth(VE, "dve_step"))
            VE.tensor_tensor(z.keep, z.o, z.z, ALU.mult).then_inc(S["delta_through"], 1)
            VE.wait_ge(S["delta_through"], S.nth(VE, "delta_through"))
            rope_dve(0, z.cos, z.sin, z.pos, z.t1, z.t2)
            VE.wait_ge(S["att_in"], S.nth(VE, "att_in", 6))
            rotate_dve(z.aq, 4, z.cos, z.sin, z.tmp, "dve_step")
            rotate_dve(z.ak, 4, z.cos, z.sin, z.tmp, "k_rotated")
            VE.tensor_copy(h[:, 0:4, :], z.keep).then_inc(S["dve_step"], 1)
            VE.wait_ge(S["dve_step"], S.nth(VE, "dve_step"))

            def out(i):
                VE.tensor_copy(h[:, 4 + i, :], take("dve")[:, 0:T]).then_inc(S["o_out"], 1)
                VE.wait_ge(S["o_out"], S.nth(VE, "o_out"))
            attention_dve(4, z.p, causal, 128 ** -0.5, z.st, out)
            residual_dve(mod_cols(0, 2))

        def mla_places():
            z, r = Z(), Scratch(False)
            z.sq, z.rs = r.mat(8), r.mat(1)
            z.cq, z.ckv = r.mat(4), r.mat(2)
            z.kr, z.qr = r.mat(1), r.mat(4)
            z.cos, z.sin, z.pos, z.t1, z.t2 = (r.get(T) for _ in range(5))
            z.tmp = r.mat(2)
            z.qn, z.kn = r.mat(8), r.mat(8)
            z.v = r.get(2048).rearrange("p (m n) -> p m n", m=TM)
            z.p = [r.mat(2) for _ in range(2)]
            z.pt = [r.mat(2) for _ in range(2)]
            z.st = r.get(8)
            return z
        zm = mla_places()

        def mla_pe():
            z = zm
            block_norm_pe(z.sq)
            TE.wait_ge(S["h_ready"], S.nth(TE, "h_ready"))
            fm_linear("mla_cq", h, DC, 512, "act", "latent_in")
            fm_linear("mla_ckv", h, DC, 256, "act", "latent_in")
            fm_linear("mla_kr", h, DC, P, "act", "kr_in")
            norm_pe([[0, 1, 2, 3]], 4, C["ones"], z.sq)
            norm_pe([[0, 1]], 2, C["ones"], z.sq)
            rotate_pe("kr_in", z.kr, 1, C["rot64"])
            TE.wait_ge(S["latent_ready"], S.nth(TE, "latent_ready", 2))
            fm_linear("mla_qn", z.cq, 4, 1024, "act", "mla_up")
            fm_linear("mla_qr", z.cq, 4, 512, "act", "qr_in")
            fm_linear("mla_kn", z.ckv, 2, 1024, "act", "mla_up")
            tm_linear("mla_v", z.ckv, 2, 1024, "act", "mla_up")
            rotate_pe("qr_in", z.qr, 4, C["rot64"])
            TE.wait_ge(S["q_rotated"], S.nth(TE, "q_rotated"))
            TE.wait_ge(S["mla_up"], expected["mla_up"])

            def scores(i, b):
                r0 = 64 * (i % 2)
                for t in range(TM):
                    tok = slice(t * P, (t + 1) * P)
                    mm(ps[:, b, t * T:(t + 1) * T], z.qn[:, i, tok], z.kn[:, i, :], start=True, stop=False)
                    m = mm(ps[:, b, t * T:(t + 1) * T], z.qr[r0:r0 + 64, i // 2, tok], z.kr[r0:r0 + 64, 0, :],
                           start=False, stop=True)
                return m

            def values(i, pt):
                b = acquire("dve")
                value_product(z.v, slice(i * P, (i + 1) * P), b, 0, pt).then_inc(S["tile_for_dve"], 1)
                frees(b, "o_out")
            attention_pe(MLA_H, scores, values, z.p, z.pt)
            TE.wait_ge(S["o_out"], expected["o_out"])
            fm_linear("mla_out", h, DC, D, "dve", "residual_in")

        def mla_act():
            z = zm
            block_norm_act(z.sq, z.rs)
            evict_act(pairs(z.cq) + pairs(z.ckv), frees="latent_in", n=3)
            evict_act([z.kr], frees="kr_in")
            norm_act(z.cq, z.sq[:, 0:4, :], z.rs, 1, 512.0)
            SE.wait_ge(S["latent_ready"], S.nth(SE, "latent_ready"))
            norm_act(z.ckv, z.sq[:, 0:2, :], z.rs, 1, 256.0)
            evict_act(pairs(z.qn), frees="mla_up", n=4)
            evict_act(pairs(z.qr), frees="qr_in", n=2)
            evict_act(pairs(z.kn), frees="mla_up", n=4)
            evict_act([z.v[:, t, n:n + 512] for n in (0, 512) for t in range(TM)], frees="mla_up", n=4)
            rope_act(z.cos, z.sin)
            attention_act(MLA_H, z.p, z.pt, 192 ** -0.5, z.st)

        def mla_dve():
            z = zm
            block_norm_dve(z.rs, mod_cols(1, 1), mod_cols(1, 0))
            for lat, n, gain in ((z.cq, 4, "q_norm"), (z.ckv, 2, "kv_norm")):
                norm_dve(z.rs, 1)
                for c in range(n):
                    signal = "latent_ready" if c == n - 1 else "dve_step"
                    VE.scalar_tensor_tensor(out=lat[:, c, :], in0=lat[:, c, :], scalar=V[gain][:, c:c + 1],
                        in1=z.rs[:, 0, :], op0=ALU.mult, op1=ALU.mult).then_inc(S[signal], 1)
                    VE.wait_ge(S[signal], S.nth(VE, signal))
            rope_dve(1, z.cos, z.sin, z.pos, z.t1, z.t2)
            VE.wait_ge(S["kr_in"], S.nth(VE, "kr_in"))
            rotate_dve(z.kr, 1, z.cos, z.sin, z.tmp, "dve_step")
            VE.wait_ge(S["qr_in"], S.nth(VE, "qr_in", 2))
            rotate_dve(z.qr, 4, z.cos, z.sin, z.tmp, "q_rotated")

            def out(i):
                VE.tensor_copy(h[:, i, :], take("dve")[:, 0:T]).then_inc(S["o_out"], 1)
                VE.wait_ge(S["o_out"], S.nth(VE, "o_out"))
            attention_dve(MLA_H, z.p, causal, 192 ** -0.5, z.st, out)
            residual_dve(mod_cols(1, 2))

        def peer_places():
            z, r = Z(), Scratch(False)
            z.sq, z.rs = r.mat(8), r.mat(1)
            z.q = r.mat(HP)
            z.sc = r.get(TM * HP * NKEY).rearrange("p (m g n) -> p m g n", m=TM, g=HP)
            z.cand = r.get(PEER_H * T).rearrange("p (g n) -> p g n", g=PEER_H)
            g16 = lambda g: r.get(g * 16).rearrange("p (g k) -> p g k", k=16)
            z.s = g16(HP)
            z.i = g16(HP)
            z.iu = r.get(HP * 16).bitcast(U32).rearrange("p (g k) -> p g k", k=16)
            z.top, z.pa, z.pb, z.gate, z.e1, z.e2 = (g16(PEER_H) for _ in range(6))
            z.pu, z.pv = (r.get(PEER_H * 16).bitcast(U32).rearrange("p (g k) -> p g k", k=16) for _ in range(2))
            z.eq = r.get(PEER_H * T).rearrange("p (g k a) -> p g k a", g=PEER_H, a=16)
            z.sum = r.get(8)
            return z
        zp = peer_places()
        gates_all = big[:].rearrange("p (j t) -> p j t", t=T)
        by_token = sel[:].rearrange("p (w t) -> p w t", t=T)
        NG = T // GRP
        NI = NKEY // UV_RING
        hot1 = [hot[:, g * 2 * GRP * P:g * 2 * GRP * P + GRP * P].rearrange("p (t n) -> p t n", n=P) for g in range(2)]
        hot2 = [hot[:, (g * 2 + 1) * GRP * P:(g * 2 + 2) * GRP * P].rearrange("p (t n) -> p t n", n=P) for g in range(2)]
        gelu = [hot[:, g * T:(g + 1) * T] for g in range(2)]
        prod = [hot[:, (2 + g) * T:(3 + g) * T] for g in range(2)]

        def uv_slot(s):
            v = uvr[:, s * UV_W:(s + 1) * UV_W]
            return v[:, 0:D].rearrange("p (c e) -> p c e", c=DC), v[:, D:2 * D]

        CREDITS = {"gates_out": 4, "gelu_taken": 4, "gate_applied": 2, "experts_used": 2}

        def loop_count(L, name):
            per = {"gates_out": NG, "hot_ready": NG}.get(name, NKEY)
            return L * per + CREDITS.get(name, 0)

        def peer_pe(L):
            z = zp
            block_norm_pe(z.sq)
            TE.wait_ge(S["h_ready"], S.nth(TE, "h_ready"))
            fm_linear("peer_q", h, DC, HP * P, "act", "peer_q_in")
            i_, w = next_weight("sub_keys")
            TE.wait_ge(S["peer_q_in"], expected["peer_q_in"])
            for t in range(TM):
                for g0 in range(0, HP, 4):
                    b = acquire("act")
                    for g in range(g0, g0 + 4):
                        m = mm(ps[:, b, (g - g0) * P:(g - g0 + 1) * P], z.q[:, g, t * P:(t + 1) * P], w[:, g, :],
                               start=True, stop=True)
                    m.then_inc(S["tile_for_act"], 1)
                    frees(b, "key_scores")
            last_use(i_, ("key_scores", expected["key_scores"]))
            for t in range(TM):
                TE.wait_ge(S["chosen"], S.nth(TE, "chosen"))
                b = acquire("dve")
                for k, v in enumerate((z.e1, z.e2, z.gate)):
                    m = TE.transpose(ps[:, b, k * P:(k + 1) * P], v.rearrange("p g k -> p (g k)"), C["ident"])
                m.then_inc(S["tile_for_dve"], 1)
                frees(b, "chosen_turned")
            for b in range(4):
                TE.wait_ge(S[freed_by[b][0]], freed_by[b][1])
            base = acquired["act"]
            with TE.Fori(0, NG // 4) as it:
                for g in range(4):
                    b = (base + g) % 4
                    TE.wait_ge(S["hot_ready"], it * 4 + (loop_count(L, "hot_ready") + g + 1))
                    TE.wait_ge(S["gates_out"], it * 4 + (loop_count(L, "gates_out") + g + 1 - 4))
                    for t in range(GRP):
                        m = mm(ps[:, b, t * P:(t + 1) * P], hot1[g % 2][:, t, :], hot2[g % 2][:, t, :],
                               start=True, stop=True)
                    m.then_inc(S["tile_for_act"], 1)
            acquired["act"] += NG
            for b in range(4):
                TE.wait_ge(S["gates_out"], loop_count(L + 1, "gates_out"))
            TE.wait_ge(S["sums_cleared"], S.nth(TE, "sums_cleared"))
            base = acquired["act"]

            def activations(s, jj):
                u, _ = uv_slot(s)
                TE.wait_ge(S[f"experts_in_{s}"], jj[1] + 16)
                TE.wait_ge(S["gelu_taken"], jj[0] + (loop_count(L, "gelu_taken") + 1 - 4))
                b = (base + s) % 4
                for c in range(DC):
                    m = mm(ps[:, b, 0:T], u[:, c, :], h[:, c, :], start=(c == 0), stop=(c == DC - 1))
                m.then_inc(S["tile_for_act"], 1)

            def outputs(s, jj):
                _, v = uv_slot(s)
                TE.wait_ge(S["gate_applied"], jj[0] + (loop_count(L, "gate_applied") + 1))
                for c in range(DC):
                    m = mm(ps[:, 4 + c // 2, (c % 2) * T:(c % 2 + 1) * T], v[:, c * P:(c + 1) * P], prod[s % 2],
                           start=False, stop=False, skip_group_check=True)
                m.then_inc(S["experts_used"], 1)

            slot_in = 16 * NI * L
            activations(0, (0, slot_in))
            with TE.Fori(0, NI - 1) as it:
                for s in range(UV_RING):
                    nx = s + 1
                    if nx < UV_RING:
                        activations(nx, (it * UV_RING + nx, it * 16 + slot_in))
                    else:
                        activations(0, (it * UV_RING + nx, it * 16 + (slot_in + 16)))
                    outputs(s, (it * UV_RING + s,))
            last = (NI - 1) * UV_RING
            for s in range(UV_RING):
                if s + 1 < UV_RING:
                    activations(s + 1, (last + s + 1, slot_in + 16 * (NI - 1)))
                outputs(s, (last + s,))
            acquired["act"] += NKEY
            for b in range(4):
                freed_by[b] = ("gelu_taken", loop_count(L + 1, "gelu_taken"))
                freed_by[4 + b] = ("sums_read", L + 1)

        def peer_act(L):
            z = zp
            block_norm_act(z.sq, z.rs)
            evict_act(pairs(z.q), frees="peer_q_in", n=HP // 2)
            evict_act([z.sc[:, t, g:g + 4, :] for t in range(TM) for g in range(0, HP, 4)], frees="key_scores", n=8)
            for t in range(TM):
                SE.wait_ge(S["top_shifted"], S.nth(SE, "top_shifted"))
                SE.activation(z.gate, z.gate, ACT.Exp).then_inc(S["top_exp"], 1)
                SE.wait_ge(S["top_exp"], S.nth(SE, "top_exp"))
            base = taken["act"]
            with SE.Fori(0, NG // 4) as it:
                for g in range(4):
                    b = (base + g) % 4
                    SE.wait_ge(S["tile_for_act"], it * 4 + (base + g + 1))
                    dst = gates_all[:, :, bass.ds(it * (4 * GRP) + g * GRP, GRP)].rearrange("p j t -> p t j")
                    SE.activation(dst, ps[:, b, :].rearrange("p (t j) -> p t j", t=GRP), ACT.Copy)\
                        .then_inc(S["gates_out"], 1)
            taken["act"] += NG
            SE.wait_ge(S["gates_out"], loop_count(L + 1, "gates_out"))
            base = taken["act"]
            with SE.Fori(0, NI) as it:
                for s in range(UV_RING):
                    b = (base + s) % 4
                    j = it * UV_RING + s
                    SE.wait_ge(S["tile_for_act"], j + (base + 1))
                    SE.wait_ge(S["gate_applied"], j + (loop_count(L, "gate_applied") + 1 - 2))
                    SE.activation(gelu[s % 2], ps[:, b, 0:T], ACT.Gelu).then_inc(S["gelu_taken"], 1)
            taken["act"] += NKEY

        def top16(vals, val16, idx16, name_last="dve_step"):
            for r in range(2):
                o = slice(8 * r, 8 * r + 8)
                VE.max(val16[:, o], vals).then_inc(S["dve_step"], 1)
                VE.wait_ge(S["dve_step"], S.nth(VE, "dve_step"))
                VE.max_index(idx16[:, o], val16[:, o], vals).then_inc(S["dve_step"], 1)
                VE.wait_ge(S["dve_step"], S.nth(VE, "dve_step"))
                if r == 0:
                    VE.match_replace(vals, val16[:, o], vals, LOW).then_inc(S["dve_step"], 1)
                    VE.wait_ge(S["dve_step"], S.nth(VE, "dve_step"))

        def peer_dve(L):
            z = zp
            block_norm_dve(z.rs, mod_cols(L, 4), mod_cols(L, 3))
            VE.tensor_copy(small[:, 1:2], small[:, 0:1]).then_inc(S["expert_ring_free"], 1)
            VE.wait_ge(S["expert_ring_free"], S.nth(VE, "expert_ring_free"))
            VE.wait_ge(S["key_scores"], S.nth(VE, "key_scores", 8))
            iota16 = C["iota"][:, 0:16].unsqueeze(1).unsqueeze(1).to_broadcast([P, PEER_H, 16, 16])
            s2 = z.s.rearrange("p (g w) k -> p g w k", w=2)
            i2 = z.i.rearrange("p (g w) k -> p g w k", w=2)
            full = [P, PEER_H, 16, 16]
            for t in range(TM):
                for g in range(HP):
                    top16(z.sc[:, t, g, :], z.s[:, g, :], z.iu[:, g, :])
                VE.tensor_copy(z.i, z.iu).then_inc(S["dve_step"], 1)
                VE.wait_ge(S["dve_step"], S.nth(VE, "dve_step"))
                VE.tensor_tensor(z.cand.rearrange("p g (a b) -> p g a b", a=16),
                    s2[:, :, 0, :].unsqueeze(3).to_broadcast(full), s2[:, :, 1,
                    :].unsqueeze(2).to_broadcast(full), ALU.add).then_inc(S["dve_step"], 1)
                VE.wait_ge(S["dve_step"], S.nth(VE, "dve_step"))
                for g in range(PEER_H):
                    top16(z.cand[:, g, :], z.top[:, g, :], z.pu[:, g, :])
                VE.tensor_scalar(z.pv, z.pu, 4, None, ALU.logical_shift_right).then_inc(S["dve_step"], 1)
                VE.wait_ge(S["dve_step"], S.nth(VE, "dve_step"))
                VE.tensor_scalar(z.pu, z.pu, 15, None, ALU.bitwise_and).then_inc(S["dve_step"], 1)
                VE.wait_ge(S["dve_step"], S.nth(VE, "dve_step"))
                VE.tensor_copy(z.pa, z.pv).then_inc(S["dve_step"], 1)
                VE.wait_ge(S["dve_step"], S.nth(VE, "dve_step"))
                VE.tensor_copy(z.pb, z.pu).then_inc(S["dve_step"], 1)
                VE.wait_ge(S["dve_step"], S.nth(VE, "dve_step"))
                VE.tensor_tensor(z.gate, z.top, z.top[:, :, 0:1].to_broadcast([P, PEER_H, 16]),
                    ALU.subtract).then_inc(S["top_shifted"], 1)
                VE.wait_ge(S["top_shifted"], S.nth(VE, "top_shifted"))
                for which, pos, dst in ((0, z.pa, z.e1), (1, z.pb, z.e2)):
                    VE.tensor_tensor(z.eq, pos.unsqueeze(3).to_broadcast(full), iota16,
                        ALU.is_equal).then_inc(S["dve_step"], 1)
                    VE.wait_ge(S["dve_step"], S.nth(VE, "dve_step"))
                    VE.tensor_tensor(z.eq, z.eq, i2[:, :, which, :].unsqueeze(2).to_broadcast(full),
                        ALU.mult).then_inc(S["dve_step"], 1)
                    VE.wait_ge(S["dve_step"], S.nth(VE, "dve_step"))
                    VE.tensor_reduce(dst, z.eq, AX, ALU.add).then_inc(S["dve_step"], 1)
                    VE.wait_ge(S["dve_step"], S.nth(VE, "dve_step"))
                VE.wait_ge(S["top_exp"], S.nth(VE, "top_exp"))
                VE.tensor_reduce(z.sum, z.gate, AX, ALU.add).then_inc(S["dve_step"], 1)
                VE.wait_ge(S["dve_step"], S.nth(VE, "dve_step"))
                VE.reciprocal(z.sum, z.sum).then_inc(S["dve_step"], 1)
                VE.wait_ge(S["dve_step"], S.nth(VE, "dve_step"))
                VE.tensor_tensor(z.gate, z.gate, lastdim(z.sum, 16), ALU.mult).then_inc(S["chosen"], 1)
                VE.wait_ge(S["chosen"], S.nth(VE, "chosen"))
                v = take("dve")[:, 0:3 * P].rearrange("p (w t) -> p w t", w=3)
                VE.tensor_copy(by_token[:, :, t * P:(t + 1) * P], v).then_inc(S["chosen_turned"], 1)
                VE.wait_ge(S["chosen_turned"], S.nth(VE, "chosen_turned"))
            with VE.Fori(0, NG // 4) as it:
                for g in range(4):
                    VE.wait_ge(S["gates_out"], it * 4 + (loop_count(L, "gates_out") + g + 1 - 2))
                    for t in range(GRP):
                        col = it * (4 * GRP) + (g * GRP + t)
                        at = lambda w: sel[:, bass.ds(col + w * T, 1)]
                        VE.tensor_scalar(hot1[g % 2][:, t, :], C["iota"], at(0), None, ALU.is_equal)
                        m = VE.tensor_scalar(hot2[g % 2][:, t, :], C["iota"], at(1), at(2), ALU.is_equal, ALU.mult)
                    m.then_inc(S["hot_ready"], 1)
            VE.wait_ge(S["gates_out"], loop_count(L + 1, "gates_out"))
            for b in range(4):
                signal = "sums_cleared" if b == 3 else "dve_step"
                VE.memset(ps[:, 4 + b, :], 0.0).then_inc(S[signal], 1)
                VE.wait_ge(S[signal], S.nth(VE, signal))
            with VE.Fori(0, NI) as it:
                for s in range(UV_RING):
                    j = it * UV_RING + s
                    VE.wait_ge(S["gelu_taken"], j + (loop_count(L, "gelu_taken") + 1))
                    VE.wait_ge(S["experts_used"], j + (loop_count(L, "experts_used") + 1 - 2))
                    VE.tensor_tensor(prod[s % 2], gelu[s % 2], big[:, bass.ds(j * T, T)], ALU.mult)\
                        .then_inc(S["gate_applied"], 1)
            VE.wait_ge(S["experts_used"], loop_count(L + 1, "experts_used"))
            g2 = mod_cols(L, 5)
            for c in range(DC):
                signal = "sums_read" if c == DC - 1 else "dve_step"
                VE.scalar_tensor_tensor(out=x[:, c, :], in0=ps[:, 4 + c // 2, (c % 2) * T:(c % 2 + 1) * T],
                    scalar=g2[:, c:c + 1], in1=x[:, c, :], op0=ALU.mult, op1=ALU.add).then_inc(S[signal], 1)
                VE.wait_ge(S[signal], S.nth(VE, signal))
            VE.tensor_copy(small[:, 1:2], small[:, 0:1]).then_inc(S["x_new"], 1)
            VE.wait_ge(S["x_new"], S.nth(VE, "x_new"))

        def peer_sp(L):
            uv = a["peer_uv"][L].rearrange("j p n -> p j n")
            SP.wait_ge(S["expert_ring_free"], S.nth(SP, "expert_ring_free"))
            for s in range(UV_RING):
                SP.dma_start(uvr[:, s * UV_W:(s + 1) * UV_W], uv[:, s, :]).then_inc(S[f"experts_in_{s}"], 16)
            with SP.Fori(1, NI) as it:
                for s in range(UV_RING):
                    j = it * UV_RING + s
                    SP.wait_ge(S["experts_used"], j + (loop_count(L, "experts_used") + 1 - UV_RING))
                    SP.dma_start(uvr[:, s * UV_W:(s + 1) * UV_W], uv[:, bass.ds(j, 1), :].rearrange("p a n -> p (a n)"))\
                        .then_inc(S[f"experts_in_{s}"], 16)
            SP.wait_ge(S["gate_applied"], loop_count(L + 1, "gate_applied"))

        def close_pe():
            block_norm_pe(zm.sq)

        def close_act():
            block_norm_act(zm.sq, zm.rs)

        def close_dve():
            block_norm_dve(zm.rs, V["final_norm"], out=x, name="x_new")

        def tables_sp():
            SP.wait_ge(S["experts_used"], loop_count(DEPTH, "experts_used"))
            SP.dma_start(hyc, a["hyena_tables"]).then_inc(S["tables_in"], 16)

        hyc = uvr[:, 0:4096]
        h_fwd = hyc[:, 0:1024].rearrange("p (m n) -> p m n", m=TM)
        h_inv = hyc[:, 1024:2048].rearrange("p (k t) -> p k t", k=4)
        h_win = hyc[:, 2048:3072].rearrange("p (m n) -> p m n", m=TM)
        h_winb = hyc[:, 3072:4096].rearrange("p (m n) -> p m n", m=TM)

        def second_places():
            z, r = Z(), Scratch(True)
            r.more = 4096
            z.sq, z.rs6 = r.mat(8), r.mat(6)
            z.rs = z.rs6[:, 0:4, :]
            after_norm = (r.at, r.more)
            z.ya, z.yb, z.yc = r.mat(4), r.mat(4), r.mat(4)
            after_y = (r.at, r.more)
            z.F = r.get(4096).rearrange("p (o w k n) -> p o w k n", o=2, w=2, k=2)
            z.sinv = r.get(8)
            after_f = (r.at, r.more)
            back = lambda to: rewind(r, to)
            z.h1, z.h2, z.ang, z.turns = (r.get(T) for _ in range(4))
            z.P, z.Q, z.A = (r.get(2048).rearrange("p (m o n) -> p m o n", m=TM, o=2) for _ in range(3))
            z.f, z.b = r.get(512), r.get(512)
            back(after_f)
            z.q, z.k = r.mat(4), r.mat(2)
            z.v = r.get(256).rearrange("p (m n) -> p m n", m=TM)
            z.p = [r.mat(2) for _ in range(2)]
            z.pt = [r.mat(2) for _ in range(2)]
            z.st = r.get(8)
            z.tmp = r.mat(2)
            back(after_f)
            z.pad = r.get(12 * 258).rearrange("p (c n) -> p c n", n=258)
            z.u = r.mat(12)
            z.ut = r.get(1024).rearrange("p (m n) -> p m n", m=TM)
            z.U = r.get(2048).rearrange("p (w k n) -> p w k n", w=2, k=2)
            z.Y = r.get(2048).rearrange("p (w k n) -> p w k n", w=2, k=2)
            z.t1 = r.get(1024).rearrange("p (k n) -> p k n", k=2)
            back(after_f)
            z.gq = r.mat(4)
            z.gv = r.get(1024).rearrange("p (m n) -> p m n", m=TM)
            z.go = r.mat(4)
            z.lr = r.get(T)
            z.lg = r.get(1024).rearrange("p (m n) -> p m n", m=TM)
            z.eb, z.ei = ([r.mat(2) for _ in range(2)] for _ in range(2))
            z.kt = r.get(512).rearrange("p (m n) -> p m n", m=TM)
            z.kd = [r.get(512).rearrange("p (m n) -> p m n", m=TM) for _ in range(2)]
            z.dec = r.get(16).rearrange("p (d g c) -> p d g c", d=2, g=2)
            z.aT = [r.get(1024).rearrange("p (g n) -> p g n", g=8) for _ in range(2)]
            z.e = z.aT[0].rearrange("p (m g) n -> p m (g n)", m=TM)
            z.S = [r.get(1024).rearrange("p (g c n) -> p g c n", g=2, c=NCH) for _ in range(2)]
            back(after_y)
            z.gate, z.mix = r.mat(8), r.mat(8)
            z.t2 = r.mat(2)
            back(after_norm)
            z.mn, z.xk, z.xq = r.mat(8), r.mat(8), r.mat(8)
            z.xv = r.get(2048).rearrange("p (m n) -> p m n", m=TM)
            z.xp = [r.mat(2) for _ in range(2)]
            z.xpt = [r.mat(2) for _ in range(2)]
            z.xst = r.get(8)
            back(after_norm)
            z.act = r.mat(D_FF // P)
            return z

        def rewind(r, to):
            r.at, r.more = to

        z2 = second_places()

        def open_dve():
            VE.tensor_copy(small[:, 1:2], small[:, 0:1]).then_inc(S["places_free"], 1)
            VE.wait_ge(S["places_free"], S.nth(VE, "places_free"))

        def filter_pe(L):
            z = z2
            i_, w = next_weight("hyena_net")
            w = w[:, 0, :]
            if L == 0:
                TE.wait_ge(S["tables_in"], 16)
            b = acquire("dve")
            mm(ps[0:64, b, 0:T], w[0:33, FT:FT + 64], C["zpos"][0:33, :], start=True,
                stop=True).then_inc(S["tile_for_dve"], 1)
            frees(b, "net_out")
            TE.wait_ge(S["net_ready"], S.nth(TE, "net_ready"))
            b = acquire("dve")
            mm(ps[0:64, b, 0:T], w[0:64, FT + 64:FT + 128], z.h1[0:64, :], start=True,
                stop=True).then_inc(S["tile_for_dve"], 1)
            frees(b, "net_out")
            TE.wait_ge(S["net_ready"], S.nth(TE, "net_ready"))
            for t in range(TM):
                for n in range(4):
                    b = acquire("dve")
                    mm(ps[:, b, :], z.h2[0:65, t * P:(t + 1) * P], w[0:65, n * 512:(n + 1) * 512], start=True,
                        stop=True).then_inc(S["tile_for_dve"], 1)
                    frees(b, "filter_out")
            last_use(i_, ("filter_out", expected["filter_out"]))
            TE.wait_ge(S["filter_ready"], S.nth(TE, "filter_ready"))
            for o in range(2):
                for part, src in ((0, z.P), (1, z.Q)):
                    for k in range(2):
                        b = acquire("act")
                        for t in range(TM):
                            m = mm(ps[:, b, :], h_fwd[:, t, part * T + k * P:part * T + (k + 1) * P], src[:, t, o, :],
                                   start=(t == 0), stop=(t == TM - 1))
                        m.then_inc(S["tile_for_act"], 1)
                        frees(b, "spectra")
            b = acquire("dve")
            for o in range(2):
                for c in range(4):
                    for t in range(TM):
                        m = mm(ps[:, b, 4 * o + c:4 * o + c + 1], z.A[:, t, o, c * P:(c + 1) * P], C["ones"][:, 0:1],
                               start=(t == 0), stop=(t == TM - 1))
            m.then_inc(S["tile_for_dve"], 1)
            frees(b, "filter_sums")

        def filter_act(L):
            z = z2
            for v in (z.h1, z.h2):
                SE.wait_ge(S["net_angles"], S.nth(SE, "net_angles"))
                SE.activation(v[0:64, :], z.ang[0:64, :], ACT.Sin).then_inc(S["net_ready"], 1)
                SE.wait_ge(S["net_ready"], S.nth(SE, "net_ready"))
            evict_act([z.F[:, o, w, k, :] for o in range(2) for w in range(2) for k in range(2)], frees="spectra", n=8)

        def filter_dve(L):
            z = z2
            VE.memset(z.h2[64:65, :], 1.0).then_inc(S["dve_step"], 1)
            VE.wait_ge(S["dve_step"], S.nth(VE, "dve_step"))
            if L == 0:
                VE.wait_ge(S["tables_in"], 16)
            for i, bias in enumerate(("hy_b1", "hy_b2")):
                t = take("dve")[0:64, 0:T]
                VE.tensor_scalar(z.f[0:64, 0:T], t, V[bias][0:64, L:L + 1],
                    V["hy_freq"][0:64, 2 * L + i:2 * L + i + 1], ALU.add, ALU.mult).then_inc(S["net_out"], 1)
                VE.wait_ge(S["net_out"], S.nth(VE, "net_out"))
                reduced_dve(z.ang[0:64, :], z.f[0:64, 0:T], 0.0, z.turns[0:64, :], "net_angles")
                VE.wait_ge(S["net_ready"], S.nth(VE, "net_ready"))
            for t in range(TM):
                for o in range(2):
                    VE.tensor_tensor(z.f, take("dve"), h_win[:, t, :], ALU.mult).then_inc(S["filter_out"], 1)
                    VE.wait_ge(S["filter_out"], S.nth(VE, "filter_out"))
                    VE.tensor_tensor(z.b, take("dve"), h_winb[:, t, :], ALU.mult).then_inc(S["filter_out"], 1)
                    VE.wait_ge(S["filter_out"], S.nth(VE, "filter_out"))
                    VE.tensor_tensor(z.P[:, t, o, :], z.f, z.b, ALU.add).then_inc(S["dve_step"], 1)
                    VE.wait_ge(S["dve_step"], S.nth(VE, "dve_step"))
                    VE.tensor_tensor(z.Q[:, t, o, :], z.b, z.f, ALU.subtract).then_inc(S["dve_step"], 1)
                    VE.wait_ge(S["dve_step"], S.nth(VE, "dve_step"))
                    VE.scalar_tensor_tensor(out=z.f, in0=z.f, scalar=-1.0, in1=z.f, op0=ALU.mult,
                        op1=ALU.max).then_inc(S["dve_step"], 1)
                    VE.wait_ge(S["dve_step"], S.nth(VE, "dve_step"))
                    VE.scalar_tensor_tensor(out=z.b, in0=z.b, scalar=-1.0, in1=z.b, op0=ALU.mult,
                        op1=ALU.max).then_inc(S["dve_step"], 1)
                    VE.wait_ge(S["dve_step"], S.nth(VE, "dve_step"))
                    signal = "filter_ready" if (t, o) == (1, 1) else "dve_step"
                    VE.tensor_tensor(z.A[:, t, o, :], z.b, z.f, ALU.add).then_inc(S[signal], 1)
                    VE.wait_ge(S[signal], S.nth(VE, signal))
            VE.tensor_scalar(z.sinv, take("dve")[:, 0:8], EPS, None, ALU.add).then_inc(S["filter_sums"], 1)
            VE.wait_ge(S["filter_sums"], S.nth(VE, "filter_sums"))
            VE.reciprocal(z.sinv, z.sinv).then_inc(S["dve_step"], 1)
            VE.wait_ge(S["dve_step"], S.nth(VE, "dve_step"))
            VE.wait_ge(S["spectra"], S.nth(VE, "spectra", 8))

        def att_pe(L):
            z = z2
            fm_linear("att_q", h, DC, 512, "act", "gqa_in")
            fm_linear("att_k", h, DC, 256, "act", "gqa_in")
            tm_linear("att_v", h, DC, P, "act", "gqa_in")
            norm_pe([[c] for c in range(6)], 6, C["blk"], z.sq)
            TE.wait_ge(S["gqa_normed"], S.nth(TE, "gqa_normed"))
            rotate_pe("gqa_in", z.q, 4, C["rot32"])
            rotate_pe("gqa_in", z.k, 2, C["rot32"])
            TE.wait_ge(S["k_rotated"], S.nth(TE, "k_rotated"))

            def scores(i, b):
                r0 = 64 * (i % 2)
                for t in range(TM):
                    m = mm(ps[:, b, t * T:(t + 1) * T], z.q[r0:r0 + 64, i // 2, t * P:(t + 1) * P],
                           z.k[r0:r0 + 64, i // 4, :], start=True, stop=True)
                return m

            def values(i, pt):
                b = acquire("dve")
                value_product(z.v, slice(64 * (i // 4), 64 * (i // 4) + 64), b, 0, pt).then_inc(S["tile_for_dve"], 1)
                frees(b, "o_out")
            attention_pe(8, scores, values, z.p, z.pt)

        def att_act(L):
            z = z2
            SE.wait_ge(S["places_free"], S.nth(SE, "places_free"))
            evict_act(pairs(z.q) + pairs(z.k) + [z.v[:, t, :] for t in range(TM)], frees="gqa_in", n=5)
            SE.activation(z.sq[:, 0:4, :], z.q, ACT.Square).then_inc(S["act_step"], 1)
            SE.wait_ge(S["act_step"], S.nth(SE, "act_step"))
            SE.activation(z.sq[:, 4:6, :], z.k, ACT.Square).then_inc(S["squares"], 1)
            SE.wait_ge(S["squares"], S.nth(SE, "squares"))
            for n, dst in ((2, z.rs6[:, 0:2, :]), (2, z.rs6[:, 2:4, :]), (2, z.rs6[:, 4:6, :])):
                t = take("act")
                SE.activation(dst, t.rearrange("p (c n) -> p c n", n=T), ACT.Sqrt, scale=1.0 / 64,
                    bias=eps_col).then_inc(S["roots"], 1)
                SE.wait_ge(S["roots"], S.nth(SE, "roots"))
            attention_act(8, z.p, z.pt, 64 ** -0.5, z.st)

        def att_dve(L):
            z = z2
            open_dve()
            VE.wait_ge(S["roots"], S.nth(VE, "roots", 3))
            VE.reciprocal(z.rs6, z.rs6).then_inc(S["dve_step"], 1)
            VE.wait_ge(S["dve_step"], S.nth(VE, "dve_step"))
            VE.scalar_tensor_tensor(out=z.q, in0=z.q, scalar=V["att_qn"][:, L:L + 1], in1=z.rs6[:, 0:4, :],
                op0=ALU.mult, op1=ALU.mult).then_inc(S["dve_step"], 1)
            VE.wait_ge(S["dve_step"], S.nth(VE, "dve_step"))
            VE.scalar_tensor_tensor(out=z.k, in0=z.k, scalar=V["att_kn"][:, L:L + 1], in1=z.rs6[:, 4:6, :],
                op0=ALU.mult, op1=ALU.mult).then_inc(S["gqa_normed"], 1)
            VE.wait_ge(S["gqa_normed"], S.nth(VE, "gqa_normed"))
            rotate_dve(z.q, 4, C["axcos"], C["axsin"], z.tmp, "dve_step")
            rotate_dve(z.k, 2, C["axcos"], C["axsin"], z.tmp, "k_rotated")

            def out(i):
                VE.tensor_copy(z.ya[64 * (i % 2):64 * (i % 2) + 64, i // 2, :],
                    take("dve")[0:64, 0:T]).then_inc(S["o_out"], 1)
                VE.wait_ge(S["o_out"], S.nth(VE, "o_out"))
            attention_dve(8, z.p, None, 64 ** -0.5, z.st, out)

        def hyena_pe(L):
            z = z2
            fm_linear("hyena_in", h, DC, 1536, "act", "hyena_in")
            for o in range(2):
                TE.wait_ge(S["conv_in"], S.nth(TE, "conv_in"))
                src = z.u[:, 0:4, :]
                for t in range(TM):
                    b = acquire("act")
                    for c in range(4):
                        m = TE.transpose(ps[:, b, c * P:(c + 1) * P], src[:, c, t * P:(t + 1) * P], C["ident"])
                    m.then_inc(S["tile_for_act"], 1)
                    frees(b, "time_major")
                TE.wait_ge(S["time_major"], expected["time_major"])
                for part in range(2):
                    for k in range(2):
                        b = acquire("act")
                        for t in range(TM):
                            m = mm(ps[:, b, :], h_fwd[:, t, part * T + k * P:part * T + (k + 1) * P], z.ut[:, t, :],
                                   start=(t == 0), stop=(t == TM - 1))
                        m.then_inc(S["tile_for_act"], 1)
                        frees(b, "u_spectrum")
                TE.wait_ge(S["y_spectrum"], S.nth(TE, "y_spectrum"))
                for c0 in range(0, 4, 2):
                    b = acquire("dve")
                    for c in (c0, c0 + 1):
                        for k in range(4):
                            m = mm(ps[:, b, (c - c0) * T:(c - c0 + 1) * T], z.Y[:, k // 2, k % 2, c * P:(c + 1) * P],
                                   h_inv[:, k, :], start=(k == 0), stop=(k == 3))
                    m.then_inc(S["tile_for_dve"], 1)
                    frees(b, "convolved")

        def hyena_act(L):
            z = z2
            SE.wait_ge(S["places_free"], S.nth(SE, "places_free"))
            evict_act([z.pad[:, c:c + 2, 1:257] for c in range(0, 12, 2)], frees="hyena_in", n=6)
            for o in range(2):
                evict_act([z.ut[:, t, :] for t in range(TM)], frees="time_major", n=2)
                evict_act([z.U[:, w, k, :] for w in range(2) for k in range(2)], frees="u_spectrum", n=4)

        def hyena_dve(L):
            z = z2
            open_dve()
            VE.memset(z.pad[:, :, 0:1], 0.0).then_inc(S["dve_step"], 1)
            VE.wait_ge(S["dve_step"], S.nth(VE, "dve_step"))
            VE.memset(z.pad[:, :, 257:258], 0.0).then_inc(S["dve_step"], 1)
            VE.wait_ge(S["dve_step"], S.nth(VE, "dve_step"))
            VE.wait_ge(S["hyena_in"], S.nth(VE, "hyena_in", 6))
            w = V["hy_conv"][:, 36 * L:36 * L + 36].rearrange("p (c j) -> p c j", j=3)
            for c in list(range(4, 12)) + list(range(4)):
                for j in range(3):
                    src = z.pad[:, c, j:j + T]
                    if j == 0:
                        VE.tensor_scalar(z.u[:, c, :], src, w[:, c, 0:1], None, ALU.mult).then_inc(S["dve_step"], 1)
                        VE.wait_ge(S["dve_step"], S.nth(VE, "dve_step"))
                    else:
                        signal = "conv_in" if (c, j) == (3, 2) else "dve_step"
                        VE.scalar_tensor_tensor(out=z.u[:, c, :], in0=src, scalar=w[:, c, j:j + 1], in1=z.u[:, c, :],
                            op0=ALU.mult, op1=ALU.add).then_inc(S[signal], 1)
                        VE.wait_ge(S[signal], S.nth(VE, signal))
            for o in range(2):
                VE.wait_ge(S["u_spectrum"], S.nth(VE, "u_spectrum", 4))
                Ur, Us, Fr, Fi = z.U[:, 0], z.U[:, 1], z.F[:, o, 0], z.F[:, o, 1]
                VE.tensor_tensor(z.t1, Us, Fi, ALU.mult).then_inc(S["dve_step"], 1)
                VE.wait_ge(S["dve_step"], S.nth(VE, "dve_step"))
                VE.tensor_tensor(z.Y[:, 0], Ur, Fr, ALU.mult).then_inc(S["dve_step"], 1)
                VE.wait_ge(S["dve_step"], S.nth(VE, "dve_step"))
                VE.tensor_tensor(z.Y[:, 0], z.Y[:, 0], z.t1, ALU.add).then_inc(S["dve_step"], 1)
                VE.wait_ge(S["dve_step"], S.nth(VE, "dve_step"))
                VE.tensor_tensor(z.t1, Ur, Fi, ALU.mult).then_inc(S["dve_step"], 1)
                VE.wait_ge(S["dve_step"], S.nth(VE, "dve_step"))
                VE.tensor_tensor(z.Y[:, 1], Us, Fr, ALU.mult).then_inc(S["dve_step"], 1)
                VE.wait_ge(S["dve_step"], S.nth(VE, "dve_step"))
                VE.tensor_tensor(z.Y[:, 1], z.Y[:, 1], z.t1, ALU.subtract).then_inc(S["y_spectrum"], 1)
                VE.wait_ge(S["y_spectrum"], S.nth(VE, "y_spectrum"))
                skip = V["hy_skip"][:, 8 * L + 4 * o:8 * L + 4 * o + 4]
                for c0 in (0, 2):
                    t = take("dve")
                    for c in (c0, c0 + 1):
                        v = z.u[:, c, :]
                        VE.tensor_scalar(v, v, skip[:, c:c + 1], None, ALU.mult).then_inc(S["dve_step"], 1)
                        VE.wait_ge(S["dve_step"], S.nth(VE, "dve_step"))
                        signal = "convolved" if c > c0 else "dve_step"
                        VE.scalar_tensor_tensor(out=v, in0=t[:, (c - c0) * T:(c - c0 + 1) * T],
                            scalar=z.sinv[:,
                            4 * o + c:4 * o + c + 1], in1=v, op0=ALU.mult, op1=ALU.add).then_inc(S[signal], 1)
                        VE.wait_ge(S[signal], S.nth(VE, signal))
                if o == 0:
                    VE.tensor_tensor(z.u[:, 0:4, :], z.u[:, 4:8, :], z.u[:, 0:4, :], ALU.mult).then_inc(S["conv_in"],
                        1)
                    VE.wait_ge(S["conv_in"], S.nth(VE, "conv_in"))
                else:
                    VE.tensor_tensor(z.yb, z.u[:, 8:12, :], z.u[:, 0:4, :], ALU.mult).then_inc(S["dve_step"], 1)
                    VE.wait_ge(S["dve_step"], S.nth(VE, "dve_step"))

        def gla_pe(L):
            z = z2
            fm_linear("gla_qk", h, DC, 512, "act", "gla_qk_in")
            tm_linear("gla_v", h, DC, 512, "act", "gla_v_in")
            fm_linear("gla_o", h, DC, 512, "act", "gla_go_in")
            i_, w = next_weight("gla_lr")
            b = acquire("act")
            for k in range(DC):
                m = mm(ps[0:64, b, 0:T], w[:, k, 0:64], h[:, k, :], start=(k == 0), stop=(k == DC - 1))
            m.then_inc(S["tile_for_act"], 1)
            frees(b, "lr_in")
            last_use(i_, ("lr_in", expected["lr_in"]))
            i_, w = next_weight("gla_net")
            TE.wait_ge(S["lr_in"], expected["lr_in"])
            for d in range(2):
                b = acquire("dve")
                for t in range(TM):
                    m = mm(ps[:, b, t * T:(t + 1) * T], z.lr[32 * d:32 * d + 17, t * P:(t + 1) * P],
                           w[32 * d:32 * d + 17, 0, :], start=True, stop=True)
                m.then_inc(S["tile_for_dve"], 1)
                frees(b, "logits")
            last_use(i_, ("logits", expected["logits"]))
            TE.wait_ge(S["gla_qk_in"], expected["gla_qk_in"])
            b = acquire("act")
            for t in range(TM):
                for g in range(2):
                    m = TE.transpose(ps[:, b, t * T + g * P:t * T + (g + 1) * P], z.gq[:, 2 + g, t * P:(t + 1) * P],
                                     C["ident"])
            m.then_inc(S["tile_for_act"], 1)
            frees(b, "gla_kt")
            TE.wait_ge(S["g_ready"], S.nth(TE, "g_ready"))
            for d, mask in ((0, "upto"), (1, "since")):
                b = acquire("act")
                for g in range(2):
                    for t in range(TM):
                        m = mm(ps[:, b, g * T + t * P:g * T + (t + 1) * P],
                               z.lg[:, t, d * T + g * P:d * T + (g + 1) * P], C[mask], start=True, stop=True)
                m.then_inc(S["tile_for_act"], 1)
                frees(b, "cum_out")
            for d, mask in ((0, "later"), (1, "before")):
                b = acquire("act")
                for t in range(TM):
                    m = mm(ps[:, b, t * T:(t + 1) * T], C[mask], z.lg[:, t, d * T:(d + 1) * T], start=True, stop=True)
                m.then_inc(S["tile_for_act"], 1)
                frees(b, "rem_out")
            TE.wait_ge(S["gla_scaled"], S.nth(TE, "gla_scaled"))
            TE.wait_ge(S["gla_v_in"], expected["gla_v_in"])
            for d in range(2):
                for r0 in (0, 64):
                    b = acquire("dve")
                    for t in range(TM):
                        for g in range(2):
                            m = mm(ps[:, b, (2 * t + g) * P:(2 * t + g + 1) * P],
                                   z.ei[d][r0:r0 + 64, g, t * P:(t + 1) * P], z.eb[d][r0:r0 + 64, g, t * P:(t + 1) * P],
                                   start=True, stop=True)
                    m.then_inc(S["tile_for_dve"], 1)
                    frees(b, "intra")
            for d in range(2):
                for odd in ((1, 0) if d == 0 else (0, 1)):
                    b = acquire("dve")
                    rows = slice(64 * odd, 64 * odd + 64)
                    for g in range(2):
                        for t in range(TM):
                            for i in (2 * g, 2 * g + 1):
                                r0 = 64 * (i % 2)
                                m = mm(ps[r0:r0 + 64, b, (2 * g + t) * P:(2 * g + t + 1) * P],
                                       z.kd[d][rows, t, i * 64:(i + 1) * 64], z.gv[rows, t, i * P:(i + 1) * P],
                                       start=True, stop=True)
                    m.then_inc(S["tile_for_dve"], 1)
                    frees(b, "state_in")
            TE.wait_ge(S["gla_states"], S.nth(TE, "gla_states"))
            for i in range(GH):
                r0, g = 64 * (i % 2), i // 2
                b = acquire("act")
                for t in range(TM):
                    for d in range(2):
                        mm(ps[:, b, t * P:(t + 1) * P], z.gv[:, t, i * P:(i + 1) * P], z.aT[d][:, 4 * t + i, :],
                           start=(d == 0), stop=False)
                    for c in (2 * t, 2 * t + 1):
                        for d in range(2):
                            m = mm(ps[:, b, c * GC:(c + 1) * GC], z.S[d][r0:r0 + 64, g, c, :],
                                   z.eb[d][r0:r0 + 64, g, c * GC:(c + 1) * GC], start=False,
                                   stop=(c % 2 == 1 and d == 1))
                m.then_inc(S["tile_for_act"], 1)
                frees(b, "gla_out")
            norm_pe([[c] for c in range(4)], 4, C["ones"], z.sq)

        def gla_act(L):
            z = z2
            SE.wait_ge(S["places_free"], S.nth(SE, "places_free"))
            evict_act(pairs(z.gq), frees="gla_qk_in", n=2)
            evict_act([z.gv[:, t, :] for t in range(TM)], frees="gla_v_in", n=2)
            evict_act(pairs(z.go), ACT.Silu, frees="gla_go_in", n=2)
            SE.wait_ge(S["lr_ones"], S.nth(SE, "lr_ones"))
            t = take("act")
            SE.activation(z.lr[0:16, :], t[0:16, 0:T], ACT.Copy).then_inc(S["act_step"], 1)
            SE.wait_ge(S["act_step"], S.nth(SE, "act_step"))
            SE.activation(z.lr[32:48, :], t[32:48, 0:T], ACT.Copy).then_inc(S["lr_in"], 1)
            SE.wait_ge(S["lr_in"], S.nth(SE, "lr_in"))
            evict_act([z.kt.rearrange("p m n -> p (m n)")], frees="gla_kt")
            SE.wait_ge(S["logit_abs"], S.nth(SE, "logit_abs"))
            SE.activation(z.e, z.e, ACT.Exp, scale=-1.0).then_inc(S["act_step"], 1)
            SE.wait_ge(S["act_step"], S.nth(SE, "act_step"))
            SE.activation(z.e, z.e, ACT.Ln, bias=1.0).then_inc(S["logit_ln"], 1)
            SE.wait_ge(S["logit_ln"], S.nth(SE, "logit_ln"))
            for d in range(2):
                t = take("act").rearrange("p (g n) -> p g n", g=2)
                SE.activation(z.eb[d], t, ACT.Exp).then_inc(S["act_step"], 1)
                SE.wait_ge(S["act_step"], S.nth(SE, "act_step"))
                SE.activation(z.ei[d], t, ACT.Exp, scale=-1.0).then_inc(S["cum_out"], 1)
                SE.wait_ge(S["cum_out"], S.nth(SE, "cum_out"))
            evict_act([z.kd[d] for d in range(2)], ACT.Exp, frees="rem_out", n=2)
            evict_act([z.yc[:, i, :] for i in range(GH)], frees="gla_out", n=4)
            norm_act(z.yc, z.sq[:, 0:4, :], z.rs, 4, 128.0)

        def gla_dve(L):
            z = z2
            VE.memset(z.lr[0:64, :], 1.0).then_inc(S["lr_ones"], 1)
            VE.wait_ge(S["lr_ones"], S.nth(VE, "lr_ones"))
            open_dve()
            for d in range(2):
                VE.tensor_copy(z.e[:, :, d * T:(d + 1) * T],
                    take("dve").rearrange("p (m n) -> p m n", m=TM)).then_inc(S["logits"], 1)
                VE.wait_ge(S["logits"], S.nth(VE, "logits"))
            VE.tensor_scalar(z.lg, z.e, 0.0, None, ALU.min).then_inc(S["dve_step"], 1)
            VE.wait_ge(S["dve_step"], S.nth(VE, "dve_step"))
            VE.scalar_tensor_tensor(out=z.e, in0=z.e, scalar=-1.0, in1=z.e, op0=ALU.mult,
                op1=ALU.max).then_inc(S["dve_step"], 1)
            VE.wait_ge(S["dve_step"], S.nth(VE, "dve_step"))
            VE.tensor_scalar(small[:, 2:3], small[:, 0:1], 1.0, None, ALU.mult).then_inc(S["logit_abs"], 1)
            VE.wait_ge(S["logit_abs"], S.nth(VE, "logit_abs"))
            VE.wait_ge(S["logit_ln"], S.nth(VE, "logit_ln"))
            VE.tensor_tensor(z.lg, z.lg, z.e, ALU.subtract).then_inc(S["dve_step"], 1)
            VE.wait_ge(S["dve_step"], S.nth(VE, "dve_step"))
            VE.tensor_scalar(z.lg, z.lg, 1.0 / 16, None, ALU.mult).then_inc(S["g_ready"], 1)
            VE.wait_ge(S["g_ready"], S.nth(VE, "g_ready"))
            VE.wait_ge(S["cum_out"], S.nth(VE, "cum_out", 2))
            for d in range(2):
                v = z.eb[d].rearrange("p g (c n) -> p g c n", n=GC)
                VE.tensor_copy(z.dec[:, d].unsqueeze(3),
                    v[:, :, :, GC - 1:GC] if d == 0 else v[:, :, :, 0:1]).then_inc(S["dve_step"], 1)
                VE.wait_ge(S["dve_step"], S.nth(VE, "dve_step"))
                VE.scalar_tensor_tensor(out=z.eb[d], in0=z.gq[:, 0:2, :], scalar=64 ** -0.5, in1=z.eb[d],
                    op0=ALU.mult, op1=ALU.mult).then_inc(S["dve_step"], 1)
                VE.wait_ge(S["dve_step"], S.nth(VE, "dve_step"))
                VE.tensor_tensor(z.ei[d], z.ei[d], z.gq[:, 2:4, :], ALU.mult).then_inc(S["dve_step"], 1)
                VE.wait_ge(S["dve_step"], S.nth(VE, "dve_step"))
            VE.wait_ge(S["gla_kt"], S.nth(VE, "gla_kt"))
            VE.wait_ge(S["rem_out"], S.nth(VE, "rem_out", 2))
            for d in range(2):
                signal = "gla_scaled" if d else "dve_step"
                VE.tensor_tensor(z.kd[d], z.kd[d], z.kt, ALU.mult).then_inc(S[signal], 1)
                VE.wait_ge(S[signal], S.nth(VE, signal))
            for d in range(2):
                for w in range(2):
                    dst = z.aT[d].rearrange("p (t g w) n -> p w t g n", t=TM, w=2)[:, w]
                    VE.tensor_tensor(dst, take("dve").rearrange("p (t g n) -> p t g n", t=TM, g=2),
                        C["upto" if d == 0 else "later"].unsqueeze(1).unsqueeze(1).to_broadcast([P, TM, 2,
                        P]), ALU.mult).then_inc(S["intra"], 1)
                    VE.wait_ge(S["intra"], S.nth(VE, "intra"))
            for d in range(2):
                order = range(NCH) if d == 0 else range(NCH - 1, -1, -1)
                order = list(order)
                VE.memset(z.S[d][:, :, order[0], :], 0.0).then_inc(S["dve_step"], 1)
                VE.wait_ge(S["dve_step"], S.nth(VE, "dve_step"))
                v = {odd: take("dve") for odd in ((1, 0) if d == 0 else (0, 1))}
                for g in range(2):
                    for c, nx in zip(order, order[1:]):
                        o = (2 * g + c // 2) * P
                        signal = "state_in" if g == 1 and nx in order[-2:] else "dve_step"
                        VE.scalar_tensor_tensor(out=z.S[d][:, g, nx, :], in0=z.S[d][:, g, c, :],
                            scalar=z.dec[:, d, g, c:c + 1], in1=v[c % 2][:,
                            o:o + P], op0=ALU.mult, op1=ALU.add).then_inc(S[signal], 1)
                        VE.wait_ge(S[signal], S.nth(VE, signal))
            VE.tensor_scalar(small[:, 2:3], small[:, 0:1], 1.0, None, ALU.mult).then_inc(S["gla_states"], 1)
            VE.wait_ge(S["gla_states"], S.nth(VE, "gla_states"))
            norm_dve(z.rs, 4)
            VE.scalar_tensor_tensor(out=z.yc, in0=z.yc, scalar=V["gla_on"][:, L:L + 1], in1=z.rs, op0=ALU.mult,
                op1=ALU.mult).then_inc(S["dve_step"], 1)
            VE.wait_ge(S["dve_step"], S.nth(VE, "dve_step"))
            VE.tensor_tensor(z.yc, z.yc, z.go, ALU.mult).then_inc(S["dve_step"], 1)
            VE.wait_ge(S["dve_step"], S.nth(VE, "dve_step"))

        def mix_pe(L):
            z = z2
            for i, y in enumerate((z.ya, z.yb, z.yc)):
                fm_linear("gate", h, DC, D, "act", "gate_in")
                if i == 0:
                    TE.wait_ge(S["branches_ready"], S.nth(TE, "branches_ready"))
                fm_linear("branch", y, 4, D, "dve", "branch_in")
            TE.wait_ge(S["mixed"], S.nth(TE, "mixed"))
            fm_linear("mix_out", z.mix, DC, D, "dve", "residual_in")

        def mix_act(L):
            z = z2
            for i in range(3):
                SE.wait_ge(S["gate_place_free"], S.nth(SE, "gate_place_free"))
                evict_act(pairs(z.gate), ACT.Sigmoid, frees="gate_in", n=4)

        def mix_dve(L):
            z = z2
            VE.tensor_copy(small[:, 1:2], small[:, 0:1]).then_inc(S["branches_ready"], 1)
            VE.wait_ge(S["branches_ready"], S.nth(VE, "branches_ready"))
            for i in range(3):
                VE.tensor_copy(small[:, 1:2], small[:, 0:1]).then_inc(S["gate_place_free"], 1)
                VE.wait_ge(S["gate_place_free"], S.nth(VE, "gate_place_free"))
                for j in range(4):
                    VE.wait_ge(S["gate_in"], S.nth(VE, "gate_in"))
                    t = take("dve").rearrange("p (c n) -> p c n", c=2)
                    g, m = z.gate[:, 2 * j:2 * j + 2, :], z.mix[:, 2 * j:2 * j + 2, :]
                    if i == 0:
                        VE.tensor_tensor(m, t, g, ALU.mult).then_inc(S["branch_in"], 1)
                        VE.wait_ge(S["branch_in"], S.nth(VE, "branch_in"))
                    else:
                        VE.tensor_tensor(z.t2, t, g, ALU.mult).then_inc(S["branch_in"], 1)
                        VE.wait_ge(S["branch_in"], S.nth(VE, "branch_in"))
                        VE.tensor_tensor(m, m, z.t2, ALU.add).then_inc(S["dve_step"], 1)
                        VE.wait_ge(S["dve_step"], S.nth(VE, "dve_step"))
            VE.tensor_copy(small[:, 1:2], small[:, 0:1]).then_inc(S["mixed"], 1)
            VE.wait_ge(S["mixed"], S.nth(VE, "mixed"))
            residual_dve(None)

        def cross_pe(L):
            z = z2
            i_, mem = next_weight("mem")
            norm_pe([list(range(DC))], DC, C["ones"], z.sq)
            TE.wait_ge(S["mem_ready"], S.nth(TE, "mem_ready"))
            last_use(i_, ("mem_ready", L + 1))
            fm_linear("x_k", z.mn, DC, D, "act", "xk_in")
            tm_linear("x_v", z.mn, DC, D, "act", "xk_in")
            norm_pe([[2 * i, 2 * i + 1] for i in range(4)], 8, C["ones"], z.sq)
            block_norm_pe(z.sq)
            TE.wait_ge(S["h_ready"], S.nth(TE, "h_ready"))
            fm_linear("x_q", h, DC, D, "act", "xq_in")
            norm_pe([[2 * i, 2 * i + 1] for i in range(4)], 8, C["ones"], z.sq)
            TE.wait_ge(S["xq_ready"], S.nth(TE, "xq_ready"))

            def scores(i, b):
                for t in range(TM):
                    for k in range(2):
                        m = mm(ps[:, b, t * T:(t + 1) * T], z.xq[:, 2 * i + k, t * P:(t + 1) * P],
                               z.xk[:, 2 * i + k, :], start=(k == 0), stop=(k == 1))
                return m

            def values(i, pt):
                b = acquire("dve")
                for k in range(2):
                    m = value_product(z.xv, slice(i * T + k * P, i * T + (k + 1) * P), b, k, pt)
                m.then_inc(S["tile_for_dve"], 1)
                frees(b, "o_out")
            attention_pe(4, scores, values, z.xp, z.xpt)
            TE.wait_ge(S["o_out"], expected["o_out"])
            fm_linear("x_o", h, DC, D, "dve", "residual_in")

        def mem_tile(L):
            i = [i for i, w in enumerate(weights) if w[0] == "mem"][L]
            return i, ring_slot(i)[:, 0:DC * T].rearrange("p (c n) -> p c n", c=DC)

        def cross_act(L):
            z = z2
            i, mem = mem_tile(L)
            SE.wait_ge(S[f"weights_in_{i % RING}"], weights_in(i))
            SE.wait_ge(S["x_new"], S.nth(SE, "x_new"))
            norm_act(mem, z.sq, z.rs, 1, D)
            evict_act(pairs(z.xk) + [z.xv[:, t, n:n + 512] for n in (0, 512) for t in range(TM)], frees="xk_in", n=8)
            norm_act(z.xk, z.sq, z.rs, 4, 256.0)
            SE.wait_ge(S["xk_ready"], S.nth(SE, "xk_ready"))
            norm_act(x, z.sq, z.rs, 1, D)
            evict_act(pairs(z.xq), frees="xq_in", n=4)
            norm_act(z.xq, z.sq, z.rs, 4, 256.0)
            attention_act(4, z.xp, z.xpt, 256 ** -0.5, z.xst)

        def cross_dve(L):
            z = z2
            i, mem = mem_tile(L)
            norm_dve(z.rs, 1)
            for c in range(DC):
                signal = "mem_ready" if c == DC - 1 else "dve_step"
                VE.scalar_tensor_tensor(out=z.mn[:, c, :], in0=mem[:, c, :],
                    scalar=V["ln_mem"][:, 8 * L + c:8 * L + c + 1], in1=z.rs[:, 0,
                    :], op0=ALU.mult, op1=ALU.mult).then_inc(S[signal], 1)
                VE.wait_ge(S[signal], S.nth(VE, signal))
            for dst, gain, name in ((z.xk, "x_kn", "xk_ready"), (z.xq, "x_qn", "xq_ready")):
                if name == "xq_ready":
                    block_norm_dve(z.rs, V["ln_x"][:, 8 * L:8 * L + 8])
                norm_dve(z.rs, 4)
                for k in range(2):
                    d = dst.rearrange("p (i k) n -> p k i n", k=2)[:, k]
                    signal = name if k else "dve_step"
                    VE.scalar_tensor_tensor(out=d, in0=d, scalar=V[gain][:, 2 * L + k:2 * L + k + 1], in1=z.rs,
                        op0=ALU.mult, op1=ALU.mult).then_inc(S[signal], 1)
                    VE.wait_ge(S[signal], S.nth(VE, signal))

            def out(i):
                VE.tensor_copy(h[:, 2 * i:2 * i + 2, :],
                    take("dve").rearrange("p (c n) -> p c n", c=2)).then_inc(S["o_out"], 1)
                VE.wait_ge(S["o_out"], S.nth(VE, "o_out"))
            attention_dve(4, z.xp, None, 256 ** -0.5, z.xst, out)
            residual_dve(None)

        def mlp_pe(L):
            z = z2
            block_norm_pe(z.sq)
            TE.wait_ge(S["h_ready"], S.nth(TE, "h_ready"))
            fm_linear("mlp1", h, DC, D_FF, "act", "relu_out")
            TE.wait_ge(S["relu_out"], expected["relu_out"])
            fm_linear("mlp2", z.act, D_FF // P, D, "dve", "residual_in")

        def mlp_act(L):
            z = z2
            block_norm_act(z.sq, z.rs)
            for c in range(0, D_FF // P, 2):
                t = take("act").rearrange("p (c n) -> p c n", c=2)
                SE.activation(z.act[:, c:c + 2, :], t, ACT.Relu).then_inc(S["act_step"], 1)
                SE.wait_ge(S["act_step"], S.nth(SE, "act_step"))
                SE.activation(z.act[:, c:c + 2, :], z.act[:, c:c + 2, :], ACT.Square).then_inc(S["relu_out"], 1)
                SE.wait_ge(S["relu_out"], S.nth(SE, "relu_out"))

        def mlp_dve(L):
            block_norm_dve(z2.rs, V["ln_mlp"][:, 8 * L:8 * L + 8])
            residual_dve(None)

        def layer_pe(L):
            filter_pe(L)
            block_norm_pe(z2.sq)
            TE.wait_ge(S["h_ready"], S.nth(TE, "h_ready"))
            att_pe(L)
            hyena_pe(L)
            gla_pe(L)
            mix_pe(L)
            cross_pe(L)
            mlp_pe(L)

        def layer_act(L):
            SE.wait_ge(S["x_new"], S.nth(SE, "x_new"))
            filter_act(L)
            norm_act(x, z2.sq, z2.rs, 1, D)
            att_act(L)
            hyena_act(L)
            gla_act(L)
            mix_act(L)
            cross_act(L)
            mlp_act(L)

        def layer_dve(L):
            filter_dve(L)
            block_norm_dve(z2.rs, V["ln_mix"][:, 8 * L:8 * L + 8])
            att_dve(L)
            hyena_dve(L)
            gla_dve(L)
            mix_dve(L)
            cross_dve(L)
            mlp_dve(L)

        plan_mod(0)
        plan_hybrid()
        plan_peer(0)
        plan_mod(1)
        plan_mla()
        plan_peer(1)
        before.setdefault(len(weights), []).append(tables_sp)
        for L in range(DEPTH):
            plan_second(L)
        stage = lambda k: upto >= k

        block = ctx.enter_context(nc.Block())

        @block.tensor
        def _(pe):
            for name, n in CREDITS.items():
                pe.sem_inc(S[name], n)
            mod_pe(0)
            if stage(1):
                hybrid_pe()
            if stage(2):
                peer_pe(0)
            if stage(3):
                mod_pe(1)
                mla_pe()
            if stage(4):
                peer_pe(1)
            if stage(5):
                close_pe()
            for L in range(DEPTH):
                if stage(6 + L):
                    layer_pe(L)

        @block.scalar
        def _(act):
            mod_act(0)
            if stage(1):
                hybrid_act()
            if stage(2):
                peer_act(0)
            if stage(3):
                mla_act()
            if stage(4):
                peer_act(1)
            if stage(5):
                close_act()
            for L in range(DEPTH):
                if stage(6 + L):
                    layer_act(L)

        @block.vector
        def _(dve):
            dve.wait_ge(S["inputs_in"], 16 * 6)
            VE.memset(small[:, 0:2], EPS).then_inc(S["dve_step"], 1)
            VE.wait_ge(S["dve_step"], S.nth(VE, "dve_step"))
            VE.memset(small[:, 2:8], 0.0).then_inc(S["inputs_ready"], 1)
            VE.wait_ge(S["inputs_ready"], S.nth(VE, "inputs_ready"))
            mod_dve(0)
            VE.tensor_copy(small[:, 1:2], small[:, 0:1]).then_inc(S["x_new"], 1)
            VE.wait_ge(S["x_new"], S.nth(VE, "x_new"))
            if stage(1):
                hybrid_dve()
            if stage(2):
                peer_dve(0)
            if stage(3):
                mod_dve(1)
                mla_dve()
            if stage(4):
                peer_dve(1)
            if stage(5):
                close_dve()
            for L in range(DEPTH):
                if stage(6 + L):
                    layer_dve(L)
            VE.tensor_copy(small[:, 1:2], small[:, 0:1]).then_inc(S["x_final"], 1)
            VE.wait_ge(S["x_final"], S.nth(VE, "x_final"))

        @block.sync
        def _(sp):
            for dst, src in ((x, a["xT"].rearrange("(c p) n -> p c n", p=P)), (consts[:], a["consts"]),
                             (vecs[:], a["vecs"]), (pos_in, a["positions"].partition_broadcast(P)),
                             (zh.al[:, 0:4], a["gdn_a_log"].partition_broadcast(P)),
                             (zh.al[:, 4:8], a["gdn_dt_bias"].partition_broadcast(P))):
                sp.dma_start(dst, src).then_inc(S["inputs_in"], 16)
            for i, (name, src, kc, n, rows, pieces) in enumerate(weights):
                for f in before.get(i, []):
                    if (f is not tables_sp and i <= use[0]) or i < use[0]:
                        f()
                if i >= use[0]:
                    break
                if i - RING >= 0 and i - RING in weight_done:
                    sp.wait_ge(S[weight_done[i - RING][0]], weight_done[i - RING][1])
                if pieces is None:
                    dst = ring_slot(i)[:, 0:kc * n].rearrange("p (c n) -> p c n", c=kc)
                    sp.dma_start(dst, src).then_inc(S[f"weights_in_{i % RING}"], 16)
                else:
                    for r0, nr, c0, nc_, piece in pieces:
                        sp.dma_start(ring_slot(i)[r0:r0 + nr, c0:c0 + nc_], piece)\
                            .then_inc(S[f"weights_in_{i % RING}"], 16)
            sp.wait_ge(S["x_final"], 1)
            sp.dma_start(a["out"].rearrange("(c p) n -> p c n", p=P), x).then_inc(S["out_written"], 16)
            sp.wait_ge(S["out_written"], 16)


def laid_out(i):
    f = lambda n: np.asarray(i[n])
    col = lambda v: np.asarray(v).reshape(-1, P).T
    pad = lambda v: np.concatenate([np.asarray(v).reshape(-1, 64)] * 2, 1).T
    w_uq = f("mla_w_uq")[0].reshape(512, MLA_H, 192)
    w_ukv = f("mla_w_ukv")[0].reshape(256, MLA_H, 256)
    w_in = f("w_in_2")
    u = f("peer_u").reshape(DEPTH, NKEY, NKEY, DC, P).transpose(0, 2, 4, 3, 1).reshape(DEPTH, NKEY, P, D)
    v = f("peer_v").reshape(DEPTH, NKEY, NKEY, D).transpose(0, 2, 1, 3)
    vec = dict(
        cond=col(f("c")), norm_mix=col(f("norm_mix")), norm_ffn=col(f("norm_ffn")), mod_b=col(f("mod_b")),
        gdn_conv=f("gdn_conv")[0].reshape(4, 12, P).transpose(2, 1, 0).reshape(P, 48),
        gdn_o_norm=col(f("gdn_o_norm")), q_norm=col(f("mla_q_norm")), kv_norm=col(f("mla_kv_norm")),
        final_norm=col(f("final_norm")), ln_mix=col(f("ln_mix_2")), ln_x=col(f("ln_x_2")),
        ln_mem=col(f("ln_mem_2")), ln_mlp=col(f("ln_mlp_2")), att_qn=pad(f("attn_qnorm_2")),
        att_kn=pad(f("attn_knorm_2")), x_qn=col(f("x_qnorm_2")), x_kn=col(f("x_knorm_2")),
        hy_conv=f("hy_conv_2").reshape(DEPTH, 3, 12, P).transpose(3, 0, 2, 1).reshape(P, 72),
        hy_skip=col(f("hy_skip_2")), gla_on=col(f("gla_onorm_2")), hy_b1=pad(f("hy_b1_2")),
        hy_b2=pad(f("hy_b2_2")), hy_freq=pad(f("hy_freq_2")))
    consts, hyena = constant_tables()
    out = dict(
        xT=f("x")[0].T, memT=f("mem_2")[0].T, positions=f("positions")[0:1],
        vecs=np.concatenate([vec[k] for k in VEC_COLS], 1),
        consts=np.concatenate([consts[k] for k in CONST_COLS], 1), hyena_tables=hyena,
        gdn_a_log=f("gdn_a_log"), gdn_dt_bias=f("gdn_dt_bias"),
        peer_uv=np.concatenate([u, v], 3),
        sub_keys=f("peer_sub_keys").transpose(0, 1, 2, 4, 3).reshape(DEPTH, HP * P, NKEY),
        mla_kr=np.concatenate([f("mla_w_in")[0][:, 768:832]] * 2, 1),
        mla_uqn=w_uq[:, :, :128].reshape(512, -1), mla_uqr=w_uq[:, :, 128:].reshape(512, -1),
        mla_ukn=w_ukv[:, :, :128].reshape(256, -1), mla_uv=w_ukv[:, :, 128:].reshape(256, -1),
        att_kdup=np.concatenate([w_in[:, :, 512:576]] * 2 + [w_in[:, :, 576:640]] * 2, 2),
        gla_lrdup=np.concatenate([w_in[:, :, 3840:3856]] * 2 + [w_in[:, :, 3856:3872]] * 2, 2))
    for k in ("mod_w", "hy_w_in", "hy_w_out", "mla_w_in", "mla_w_out", "peer_w_q", "w_in_2", "hy_w1_2", "hy_w2_2",
              "hy_w3_2", "hy_b3_2", "gla_w_lr_2", "gla_b_lr_2", "w_br_attn_2", "w_br_hyena_2", "w_br_gla_2",
              "w_out_2", "x_wq_2", "x_wk_2", "x_wv_2", "x_wo_2", "mlp_w1_2", "mlp_w2_2"):
        out[k] = f(k)
    return {k: np.ascontiguousarray(v) for k, v in out.items()}


def kernel(**inputs):
    import concourse.bacc as bacc
    from concourse.bass_utils import run_bass_kernel_spmd

    nc = bacc.Bacc("TRN2", target_bir_lowering=False, num_devices=1)
    arrays = laid_out(inputs)
    aps = {k: nc.dram_tensor(k, v.shape, mybir.dt.from_np(v.dtype), kind="ExternalInput").ap()
           for k, v in arrays.items()}
    aps["out"] = nc.dram_tensor("out", (D, T), F32, kind="ExternalOutput").ap()
    two_blocks(nc, aps)
    r = run_bass_kernel_spmd(nc, [arrays], core_ids=[0])
    return np.ascontiguousarray(r.results[0]["out"].T).reshape(1, T, D)
```

```python
from contextlib import ExitStack

import concourse.bass as bass
from concourse import mybir
import numpy as np

F32 = mybir.dt.float32
F32R = mybir.dt.float32r
I32 = mybir.dt.int32
U32 = mybir.dt.uint32
ALU = mybir.AluOpType
ACT = mybir.ActivationFunctionType
AX = mybir.AxisListType.X

P = 128
T = 256
TM = T // P
D = 1024
DC = D // P
EPS = 1e-6
DEPTH = 2
NEG = -1e30
LOW = -3.0e38

GH, GC = 4, 64
NCH = T // GC
MLA_H = 8
PEER_H, PEER_K, NKEY = 8, 16, 128
HP = 2 * PEER_H
HYW, FT = 512, 2048
D_FF = 4096

RING, RING_W = 3, 4096
UV_RING, UV_W = 4, 2048
GRP = 4


def constant_tables():
    i = np.arange(P)
    s, t = i[:, None], i[None, :]
    same = (s // GC) == (t // GC)
    c = {}
    c["ident"] = np.eye(P)
    c["ones"] = np.ones((P, P))
    c["blk"] = same * 1.0
    c["upto"] = (same & (s <= t)) * 1.0
    c["since"] = (same & (s >= t)) * 1.0
    c["later"] = (same & (s > t)) * 1.0
    c["before"] = (same & (s < t)) * 1.0
    c["mlow"] = np.where(same & (t <= s), 0.0, NEG)
    c["mup"] = np.where(same & (s <= t), 0.0, NEG)

    def rotation(width):
        r = np.zeros((P, P))
        h = width // 2
        for m in range(P):
            if m % width < h:
                r[m + h, m] = -1.0
            else:
                r[m - h, m] = 1.0
        return r
    c["rot128"], c["rot64"], c["rot32"] = rotation(128), rotation(64), rotation(32)
    kv = np.arange(T)[None, None, :]
    q = np.arange(TM)[None, :, None] * P + i[:, None, None]
    c["causal"] = np.where(kv <= q, 0.0, NEG).reshape(P, TM * T)
    f16 = (np.float32(10000.0) ** (-np.arange(16, dtype=np.float32) / 16)).astype(np.float32)
    tok = np.arange(T)
    where = np.stack([tok // 64, tok % 64], 0).astype(np.float32)
    row = i % 64
    ang = (where[row // 32] * f16[row % 16][:, None]).astype(np.float32)
    c["axcos"], c["axsin"] = np.cos(ang), np.sin(ang)
    c["iota"] = np.broadcast_to(np.arange(P, dtype=np.float32), (P, P))
    inv = lambda n: (np.float32(10000.0) ** (-np.arange(0, n, 2, dtype=np.float32) / n)).astype(np.float32)
    c["invf"] = np.stack([inv(128)[i % 64], inv(64)[i % 32]], 1)
    th = 2 * np.pi * (np.arange(T)[None, :] + 0.5) * np.arange(T)[:, None] / (2 * T)
    fwd = np.concatenate([np.cos(th), np.sin(th)], 1).reshape(TM, P, 2 * T)
    inv_ = (np.concatenate([np.cos(th), np.sin(th)], 1).T / T).reshape(4, P, T)
    tn = np.arange(T, dtype=np.float32) / (T - 1)
    import math
    deltas = np.abs(np.linspace(math.log(1e-2) / 0.3, math.log(1e-2) / 1.5, HYW, dtype=np.float32))
    win = np.exp(-tn[:, None] * deltas).astype(np.float32)
    winb = win.copy()
    winb[0] = 0.0
    hy = [fwd.transpose(1, 0, 2).reshape(P, -1), inv_.transpose(1, 0, 2).reshape(P, -1),
          win.reshape(TM, P, HYW).transpose(1, 0, 2).reshape(P, -1),
          winb.reshape(TM, P, HYW).transpose(1, 0, 2).reshape(P, -1)]
    w = (2.0 * math.pi * np.arange(T, dtype=np.float32) / T).astype(np.float32)
    fr = np.linspace(1e-4, 15, 16, dtype=np.float32)
    fw = w[:, None] * fr
    z = np.concatenate([tn[:, None], np.cos(fw), -np.sin(fw)], -1).T
    zp = np.zeros((P, T))
    zp[:33] = z
    c["zpos"] = zp
    return ({k: np.ascontiguousarray(v, dtype=np.float32) for k, v in c.items()},
            np.ascontiguousarray(np.concatenate(hy, 1), dtype=np.float32))


CONST_COLS = dict(ident=P, ones=P, blk=P, upto=P, since=P, later=P, before=P, mlow=P, mup=P, rot128=P,
                  rot64=P, rot32=P, causal=TM * T, axcos=T, axsin=T, iota=P, invf=2, zpos=T)

VEC_COLS = dict(cond=8, norm_mix=16, norm_ffn=16, mod_b=96, gdn_conv=48, gdn_o_norm=1, q_norm=4, kv_norm=2,
                final_norm=8, ln_mix=16, ln_x=16, ln_mem=16, ln_mlp=16, att_qn=2, att_kn=2, x_qn=4, x_kn=4,
                hy_conv=72, hy_skip=16, gla_on=2, hy_b1=2, hy_b2=2, hy_freq=4)


class Signals:

    def __init__(self, nc, ctx):
        self.nc, self.ctx, self.sems, self.seen, self.sent = nc, ctx, {}, {}, {}

    def __getitem__(self, name):
        if name not in self.sems:
            self.sems[name] = self.ctx.enter_context(self.nc.semaphore(name))
        return self.sems[name]

    def nth(self, eng, name, n=1):
        k = (str(eng.engine), name)
        self.seen[k] = self.seen.get(k, 0) + n
        return self.seen[k]


def two_blocks(nc, a, upto=99):
    ctx = ExitStack()
    with ctx:
        S = Signals(nc, ctx)

        def sb(name, n, dt=F32):
            return ctx.enter_context(nc.sbuf_tensor(name, [P, n], dt))

        def two_views(name, n):
            with nc.sbuf_tensor(name, [P, n], F32) as plain:
                pass
            return plain, sb(name + "_split", n, F32R)

        ps = ctx.enter_context(nc.psum_tensor("ps", [P, 8, 512], F32))
        with nc.sbuf_tensor("big", [P, NKEY * T], F32) as big:
            pass
        ring_r = sb("ring_split", RING * RING_W, F32R)
        NORM_W = DC * T + 6 * T
        SPLIT_W = D_FF // P * T
        sb("norm_places", NORM_W)
        scr_r = [sb(f"scratch_split_{i}", SPLIT_W, F32R) for i in range(2)]
        sb("rest", NKEY * T - RING * RING_W - NORM_W - 2 * SPLIT_W)
        uvr, uvr_r = two_views("uvr", UV_RING * UV_W)
        xt, xt_r = two_views("xt", DC * T)
        ht, ht_r = two_views("ht", DC * T)
        high, high_r = two_views("high", 2 * D)
        sel = high[:, 0:3 * T]
        hot, hot_r = two_views("hot", 2 * 2 * GRP * P)
        consts, consts_r = two_views("consts_sb", sum(CONST_COLS.values()))
        vecs = sb("vecs_sb", sum(VEC_COLS.values()))
        modv = sb("modv", 2 * 48)
        small = sb("small", 256)
        pos_in = sb("pos_in", T, I32)[:]

        x = xt[:].rearrange("p (c t) -> p c t", t=T)
        h = ht[:].rearrange("p (c t) -> p c t", t=T)

        def named(tensor, cols):
            out, o = {}, 0
            for k, n in cols.items():
                out[k] = tensor[:, o:o + n]
                o += n
            return out
        C = named(consts, CONST_COLS)
        V = named(vecs, VEC_COLS)
        causal = C["causal"].rearrange("p (m k) -> p m k", m=TM)

        def ring_slot(i):
            return big[:, (i % RING) * RING_W:(i % RING + 1) * RING_W]
        SCR = RING * RING_W
        SCR_N = NKEY * T - SCR

        class Scratch:

            def __init__(self, expert_ring):
                self.at, self.more, self.end = 0, 0, UV_RING * UV_W if expert_ring else 0

            def get(self, n, dt=None):
                if self.at + n <= SCR_N:
                    v = big[:, SCR + self.at:SCR + self.at + n]
                    self.at += n
                else:
                    assert self.more + n <= self.end, (self.at, self.more, n)
                    v = uvr[:, self.more:self.more + n]
                    self.more += n
                return v

            def split(self, n):
                k, o = divmod(self.at - NORM_W, SPLIT_W)
                if o + n > SPLIT_W:
                    k, o = k + 1, 0
                self.at = NORM_W + k * SPLIT_W + o + n
                return scr_r[k][:, o:o + n]

            def mat(self, c, n=T):
                return self.get(c * n).rearrange("p (c n) -> p c n", n=n)

        TE, VE, SE, GE, SP = nc.tensor, nc.vector, nc.scalar, nc.gpsimd, nc.sync

        banks = {"act": [0, None], "dve": [4, None]}
        filled = {"act": "tile_for_act", "dve": "tile_for_dve"}
        acquired = {"act": 0, "dve": 0}
        taken = {"act": 0, "dve": 0}
        freed_by = {}
        expected = {}

        def acquire(pool):
            b = banks[pool][0] + acquired[pool] % 4
            acquired[pool] += 1
            if b in freed_by:
                name, n = freed_by[b]
                TE.wait_ge(S[name], n)
            return b

        def frees(b, name):
            expected[name] = expected.get(name, 0) + 1
            freed_by[b] = (name, expected[name])

        def take(pool):
            b = banks[pool][0] + taken[pool] % 4
            taken[pool] += 1
            (SE if pool == "act" else VE).wait_ge(S[filled[pool]], taken[pool])
            return ps[:, b, :]

        mm = TE.matmul

        before = {}
        weights = []
        use = [0]
        weight_done = {}

        def plan(name, src, kc, n, rows=P, pieces=None):
            weights.append((name, src, kc, n, rows, pieces))

        def weights_in(i):
            return 16 * sum(len(w[5] or [0]) for w in weights[i % RING:i + 1:RING])

        def next_weight(name):
            i = use[0]
            assert weights[i][0] == name, (weights[i][0], name)
            use[0] += 1
            TE.wait_ge(S[f"weights_in_{i % RING}"], weights_in(i))
            kc, n = weights[i][2:4]
            return i, ring_slot(i)[:, 0:kc * n].rearrange("p (c n) -> p c n", c=kc)

        def last_use(i, ins_freed):
            weight_done[i] = ins_freed

        def fm_linear(name, xin, kc, ncols, pool, reader, part=2, arriving=False):
            c, b, left = 0, None, ncols // P
            while c < left:
                i, w = next_weight(name)
                for n0 in range(0, weights[i][3], P):
                    if c % part == 0:
                        b = acquire(pool)
                    for k in range(kc):
                        if arriving and c == 0:
                            TE.wait_ge(S["h_ready"], S.nth(TE, "h_ready"))
                        m = mm(ps[:, b, (c % part) * T:(c % part + 1) * T], w[:, k, n0:n0 + P], xin[:, k, :],
                               start=(k == 0), stop=(k == kc - 1))
                    c += 1
                    if c % part == 0 or c == left:
                        m.then_inc(S[filled[pool]], 1)
                        frees(b, reader)
                last_use(i, (reader, expected[reader]) if c % part == 0 or c == left else None)
            for i in list(weight_done):
                if weight_done[i] is None:
                    weight_done[i] = next(weight_done[j] for j in range(i + 1, use[0]) if weight_done[j])

        pieces = []
        high_place = [high_r[:], hot_r[:]]
        split_at = {"high": 0, "low": 0}

        def piece(i, half, ring):
            kc, n = weights[i][2:4]
            w = ring[:, (i % RING) * RING_W:(i % RING) * RING_W + kc * n].rearrange("p (c n) -> p c n", c=kc)
            return w[:, :, half * (n // 2):(half + 1) * (n // 2)] if kc <= DC else w[:, half * (kc // 2):(half + 1) * (kc // 2), :]

        def high_part(p, like):
            return high_place[p % 2][:, 0:like.free_size()].rearrange("p (c n) -> p c n", c=like.shape[1])

        def split_linear(name, x_high, x_low, kc, ncols, pool, reader, first=None):
            c, b, left, ready = 0, None, ncols // P, 0
            while c < left:
                i = use[0]
                assert weights[i][0] == name, (weights[i][0], name)
                use[0] += 1
                by_chunks = kc > DC
                for half in range(2):
                    w_low = piece(i, half, ring_r)
                    w_high = high_part(len(pieces), w_low)
                    pieces.append((i, half))
                    TE.wait_ge(S["w_split"], len(pieces))
                    m = None
                    for n0 in range(0, w_low.shape[2], P):
                        if c % 2 == 0 and not (by_chunks and half):
                            b = acquire(pool)
                        for kk in range(w_low.shape[1]):
                            k = kk + half * (kc // 2) if by_chunks else kk
                            if first and c == 0 and k % 2 == 0:
                                TE.wait_ge(S[first], S.nth(TE, first))
                            out = ps[:, b, (c % 2) * T:(c % 2 + 1) * T]
                            st, en = k == 0, k == kc - 1
                            wh, wl = w_high[:, kk, n0:n0 + P], w_low[:, kk, n0:n0 + P]
                            o = mm(out, wh, x_high[:, k, :], start=st, stop=False)
                            if m is None:
                                o.then_inc(S["w_used"], 1)
                            mm(out, wh, x_low[:, k, :], start=False, stop=False)
                            m = mm(out, wl, x_high[:, k, :], start=False, stop=en)
                        if not by_chunks or half:
                            c += 1
                            if c % 2 == 0:
                                m.then_inc(S[filled[pool]], 1)
                                frees(b, reader)
                last_use(i, (reader, expected[reader]) if c == left else ("w_used", len(pieces) + 1))

        def split_high(idle=False):
            p = split_at["high"]
            split_at["high"] += 1
            i, half = pieces[p]
            SE.wait_ge(S[f"weights_in_{i % RING}"], weights_in(i))
            if not idle:
                SE.wait_ge(S["w_used"], p)
            w = piece(i, half, big)
            SE.activation(high_part(p, w), w, ACT.Copy).then_inc(S["w_high"], 1)

        def split_low():
            p = split_at["low"]
            split_at["low"] += 1
            i, half = pieces[p]
            VE.wait_ge(S["w_high"], p + 1)
            w = piece(i, half, big)
            VE.tensor_tensor(piece(i, half, ring_r), w, high_part(p, w).bitcast(F32), ALU.subtract)\
                .then_inc(S["w_split"], 1)

        def split_h_act(h_high, whole=False):
            for c in range(0, DC, 2):
                if not whole:
                    SE.wait_ge(S["h_part"], S.nth(SE, "h_part", 2))
                SE.activation(h_high[:, c:c + 2, :], h[:, c:c + 2, :], ACT.Copy).then_inc(S["x_high"], 1)

        def split_h_dve(h_high):
            for c in range(0, DC, 2):
                VE.wait_ge(S["x_high"], S.nth(VE, "x_high"))
                VE.tensor_tensor(h_low[:, c:c + 2, :], h[:, c:c + 2, :], h_high[:, c:c + 2, :].bitcast(F32),
                                 ALU.subtract).then_inc(S["x_split"], 1)
        h_low = ht_r[:].rearrange("p (c t) -> p c t", t=T)

        def tm_linear(name, xin, kc, ncols, pool, reader):
            c = 0
            while c < ncols:
                i, w = next_weight(name)
                n = weights[i][3]
                for n0 in range(0, n, 512):
                    nn = min(512, n - n0)
                    for t in range(TM):
                        b = acquire(pool)
                        for k in range(kc):
                            m = mm(ps[:, b, 0:nn], xin[:, k, t * P:(t + 1) * P], w[:, k, n0:n0 + nn],
                                   start=(k == 0), stop=(k == kc - 1))
                        m.then_inc(S[filled[pool]], 1)
                        frees(b, reader)
                c += n
                last_use(i, (reader, expected[reader]))

        def evict_act(dst, func=ACT.Copy, frees="act_freed", scale=1.0, n=1):
            for i in range(n):
                t = take("act")
                d = dst[i]
                t = t[:, 0:d.free_size()]
                if len(d.shape) == 3:
                    t = t.rearrange("p (c n) -> p c n", n=d.shape[2])
                SE.activation(d, t, func, scale=scale).then_inc(S[frees], 1)
                SE.wait_ge(S[frees], S.nth(SE, frees))

        def pairs(m, lo=0, hi=None):
            hi = hi or m.shape[1]
            return [m[:, c:min(c + 2, hi), :] for c in range(lo, hi, 2)]

        def norm_pe(groups, nchunk, lhs, sq):
            TE.wait_ge(S["squares"], S.nth(TE, "squares"))
            for g0 in range(0, len(groups), 2):
                b = acquire("act")
                for u, g in enumerate(groups[g0:g0 + 2]):
                    for j, c in enumerate(g):
                        m = mm(ps[:, b, u * T:(u + 1) * T], lhs, sq[:, c, :], start=(j == 0), stop=(j == len(g) - 1))
                m.then_inc(S["tile_for_act"], 1)
                frees(b, "roots")

        def norm_act(src, sq, rs, ngroups, mean):
            SE.activation(sq, src, ACT.Square).then_inc(S["squares"], 1)
            SE.wait_ge(S["squares"], S.nth(SE, "squares"))
            roots_act(rs, ngroups, mean)

        def roots_act(rs, ngroups, mean):
            for g0 in range(0, ngroups, 2):
                n = min(2, ngroups - g0)
                t = take("act")
                SE.activation(rs[:, g0:g0 + n, :], t[:, 0:n * T].rearrange("p (c n) -> p c n", n=T), ACT.Ln,
                    scale=1.0 / mean, bias=eps_col).then_inc(S["act_step"], 1)
                SE.wait_ge(S["act_step"], S.nth(SE, "act_step"))
                SE.activation(rs[:, g0:g0 + n, :], rs[:, g0:g0 + n, :], ACT.Exp, scale=-0.5).then_inc(S["roots"], 1)
                SE.wait_ge(S["roots"], S.nth(SE, "roots"))

        def norm_dve(rs, ngroups):
            VE.wait_ge(S["roots"], S.nth(VE, "roots", (ngroups + 1) // 2))

        eps_col = small[:, 0:1]

        all_groups = [list(range(DC))]

        def block_norm_pe(sq):
            b = acquire("act")
            for c in range(DC):
                if c % 2 == 0:
                    TE.wait_ge(S["squares"], S.nth(TE, "squares"))
                m = mm(ps[:, b, 0:T], C["ones"], sq[:, c, :], start=(c == 0), stop=(c == DC - 1))
            m.then_inc(S["tile_for_act"], 1)
            frees(b, "roots")

        def block_norm_act(sq, rs, parts=None):
            for c in range(0, DC, 2):
                if parts:
                    SE.wait_ge(S[parts], S.nth(SE, parts))
                SE.activation(sq[:, c:c + 2, :], x[:, c:c + 2, :], ACT.Square).then_inc(S["squares"], 1)
                SE.wait_ge(S["squares"], S.nth(SE, "squares"))
            if parts:
                SE.wait_ge(S["x_new"], S.nth(SE, "x_new"))
            roots_act(rs, 1, D)

        def block_norm_dve(rs, scale, shift=None, out=None, name="h_ready"):
            out = h if out is None else out
            norm_dve(rs, 1)
            if shift is None:
                for c in range(DC):
                    VE.scalar_tensor_tensor(out=out[:, c, :], in0=x[:, c, :], scalar=scale[:, c:c + 1], in1=rs[:, 0, :],
                                            op0=ALU.mult, op1=ALU.mult).then_inc(S[name], 1)
            else:
                for c in range(DC + 1):
                    if c < DC:
                        VE.scalar_tensor_tensor(out=out[:, c, :], in0=x[:, c, :], scalar=scale[:, c:c + 1],
                                                in1=rs[:, 0, :], op0=ALU.mult, op1=ALU.mult).then_inc(S["scaled"], 1)
                    if c >= 1:
                        VE.wait_ge(S["scaled"], S.nth(VE, "scaled"))
                        VE.tensor_scalar(out[:, c - 1, :], out[:, c - 1, :], shift[:, c - 1:c], None, ALU.add)\
                            .then_inc(S[name], 1)
            VE.wait_ge(S[name], S.nth(VE, name, DC))

        def residual_dve(gate, nbanks=DC // 2, name="x_new"):
            for b in range(nbanks):
                if gate is None:
                    residual_bank(b)
                    continue
                t = take("dve")
                for u in range(2):
                    c = 2 * b + u
                    last = "residual_in" if u else "dve_step"
                    VE.scalar_tensor_tensor(out=x[:, c, :], in0=t[:, u * T:(u + 1) * T], scalar=gate[:, c:c + 1],
                        in1=x[:, c, :], op0=ALU.mult, op1=ALU.add).then_inc(S[last], 1)
                    VE.wait_ge(S[last], S.nth(VE, last))
            x_complete(name)

        def residual_bank(b):
            VE.tensor_tensor(x[:, 2 * b:2 * b + 2, :], take("dve").rearrange("p (c n) -> p c n", c=2),
                x[:, 2 * b:2 * b + 2, :], ALU.add).then_inc(S["residual_in"], 1)
            VE.wait_ge(S["residual_in"], S.nth(VE, "residual_in"))

        def x_complete(name="x_new"):
            VE.tensor_copy(small[:, 1:2], small[:, 0:1]).then_inc(S[name], 1)
            VE.wait_ge(S[name], S.nth(VE, name))

        def attention_pe(H, scores, values, p, pt, dv_rows=P):
            for i in range(H + 2):
                if i < H:
                    b = acquire("dve")
                    m = scores(i, b)
                    m.then_inc(S["tile_for_dve"], 1)
                    frees(b, "scores_taken")
                if i >= 2:
                    TE.wait_ge(S["probs_turned"], expected["probs_turned"])
                    values(i - 2, pt[i % 2])
                if 1 <= i <= H:
                    TE.wait_ge(S["probs_ready"], S.nth(TE, "probs_ready"))
                    for j in range(TM):
                        b = acquire("act") if j == 0 else b
                        for t in range(TM):
                            m = TE.transpose(ps[:, b, j * T + t * P:j * T + (t + 1) * P],
                                             p[(i - 1) % 2][:, t, j * P:(j + 1) * P], C["ident"])
                    m.then_inc(S["tile_for_act"], 1)
                    frees(b, "probs_turned")

        def attention_act(H, p, pt, scale, st):
            for i in range(H + 1):
                if i >= 1:
                    evict_act([pt[(i + 1) % 2]], frees="probs_turned")
                if i < H:
                    SE.wait_ge(S["row_max"], S.nth(SE, "row_max"))
                    for t in range(TM):
                        signal = "exps" if t else "act_step"
                        SE.activation(p[i % 2][:, t, :], p[i % 2][:, t, :], ACT.Exp, scale=scale,
                            bias=st[:, 4 * (i % 2) + t:4 * (i % 2) + t + 1], accum_out=st[:,
                            4 * (i % 2) + 2 + t:4 * (i % 2) + 3 + t]).then_inc(S[signal], 1)
                        SE.wait_ge(S[signal], S.nth(SE, signal))

        def attention_dve(H, p, mask, scale, st, out):
            for i in range(H + 2):
                if 1 <= i <= H:
                    k = (i - 1) % 2
                    VE.wait_ge(S["exps"], S.nth(VE, "exps"))
                    VE.reciprocal(st[:, 4 * k + 2:4 * k + 4], st[:, 4 * k + 2:4 * k + 4]).then_inc(S["dve_step"], 1)
                    VE.wait_ge(S["dve_step"], S.nth(VE, "dve_step"))
                    for t in range(TM):
                        signal = "probs_ready" if t else "dve_step"
                        VE.tensor_scalar(p[k][:, t, :], p[k][:, t, :], st[:, 4 * k + 2 + t:4 * k + 3 + t], None,
                            ALU.mult).then_inc(S[signal], 1)
                        VE.wait_ge(S[signal], S.nth(VE, signal))
                if i < H:
                    t = take("dve").rearrange("p (m k) -> p m k", m=TM)
                    if mask is None:
                        VE.tensor_copy(p[i % 2], t).then_inc(S["scores_taken"], 1)
                        VE.wait_ge(S["scores_taken"], S.nth(VE, "scores_taken"))
                    else:
                        VE.tensor_tensor(p[i % 2], t, mask, ALU.add).then_inc(S["scores_taken"], 1)
                        VE.wait_ge(S["scores_taken"], S.nth(VE, "scores_taken"))
                    o = 4 * (i % 2)
                    VE.tensor_reduce(st[:, o:o + 2], p[i % 2], AX, ALU.max).then_inc(S["dve_step"], 1)
                    VE.wait_ge(S["dve_step"], S.nth(VE, "dve_step"))
                    VE.tensor_scalar(st[:, o:o + 2], st[:, o:o + 2], -scale, None, ALU.mult).then_inc(S["row_max"], 1)
                    VE.wait_ge(S["row_max"], S.nth(VE, "row_max"))
                if i >= 2:
                    out(i - 2)

        def value_product(v, cols, b, half, pt):
            for j in range(TM):
                m = mm(ps[0:cols.stop - cols.start, b, half * T:(half + 1) * T], v[:, j, cols], pt[:, j, :],
                       start=(j == 0), stop=(j == TM - 1))
            return m

        def plan_cols(name, w, lo, hi):
            K = w.shape[0]
            kc = K // P
            per = RING_W // kc
            v = w.rearrange("(c p) n -> p c n", p=P)
            for n0 in range(lo, hi, per):
                n = min(per, hi - n0)
                plan(name, v[:, :, n0:n0 + n], kc, n)

        def plan_mod(L, lo, hi):
            plan_cols(f"mod{L}", a["mod_w"][L], 512 * lo, 512 * hi)

        def plan_hybrid():
            w = a["hy_w_in"][0]
            plan_cols("gdn_qkv", w, 0, 1536)
            plan_cols("gdn_z", w, 1536, 2048)
            plan("gdn_ba", w.rearrange("(c p) n -> p c n", p=P)[:, :, 2048:2056], DC, 8)
            plan_mod(0, 4, 12)
            plan_cols("moba_q", w, 2056, 2568)
            plan_cols("moba_k", w, 2568, 3080)
            plan_cols("moba_v", w, 3080, 3592)
            plan_cols("hy_out", a["hy_w_out"][0], 0, D)

        def plan_mla():
            plan_cols("mla_cq", a["mla_w_in"][0], 0, 512)
            plan_cols("mla_ckv", a["mla_w_in"][0], 512, 768)
            plan_cols("mla_kr", a["mla_kr"], 0, P)
            plan_cols("mla_qn", a["mla_uqn"], 0, 1024)
            plan_cols("mla_qr", a["mla_uqr"], 0, 512)
            plan_cols("mla_kn", a["mla_ukn"], 0, 1024)
            plan_cols("mla_v", a["mla_uv"], 0, 1024)
            plan_cols("mla_out", a["mla_w_out"][0], 0, D)

        def plan_peer(L):
            plan_cols("peer_q", a["peer_w_q"][L], 0, HP * P)
            plan("sub_keys", a["sub_keys"][L].rearrange("(c p) n -> p c n", p=P), HP, NKEY)
            if L == 0:
                plan_mod(1, 0, 12)
            before.setdefault(len(weights), []).append(lambda: peer_sp(L))

        def plan_second(L):
            w = a["w_in_2"][L]
            plan("hyena_net", None, 1, FT + 128, P, hyena_pieces(L))
            plan_cols("att_q", w, 0, 512)
            plan_cols("att_k", a["att_kdup"][L], 0, 256)
            plan_cols("att_v", w, 640, 768)
            plan_cols("hyena_in", w, 768, 2304)
            plan_cols("gla_qk", w, 2304, 2816)
            plan_cols("gla_v", w, 2816, 3328)
            plan_cols("gla_o", w, 3328, 3840)
            plan_cols("gla_lr", a["gla_lrdup"][L], 0, 64)
            plan("gla_net", None, 1, 256, P, gla_pieces(L))
            for i, br in enumerate(("w_br_attn_2", "w_br_hyena_2", "w_br_gla_2")):
                plan_cols("gate", w, 3872 + i * D, 3872 + (i + 1) * D)
                plan_cols("branch", a[br][L], 0, D)
            plan_cols("mix_out", a["w_out_2"][L], 0, D)
            plan("mem", a["memT"].rearrange("(c p) n -> p c n", p=P), DC, T)
            plan_cols("x_k", a["x_wk_2"][L], 0, D)
            plan_cols("x_v", a["x_wv_2"][L], 0, D)
            plan_cols("x_q", a["x_wq_2"][L], 0, D)
            plan_cols("x_o", a["x_wo_2"][L], 0, D)
            plan_cols("mlp1", a["mlp_w1_2"][L], 0, D_FF)
            plan_cols("mlp2", a["mlp_w2_2"][L], 0, D)

        def hyena_pieces(L):
            row = lambda v: v.rearrange("(a n) -> a n", a=1)
            return [(0, 64, 0, FT, a["hy_w3_2"][L]), (64, 1, 0, FT, row(a["hy_b3_2"][L])),
                    (0, 33, FT, 64, a["hy_w1_2"][L]), (0, 64, FT + 64, 64, a["hy_w2_2"][L])]

        def gla_pieces(L):
            row = lambda v: v.rearrange("(a n) -> a n", a=1)
            return [(0, 16, 0, 256, a["gla_w_lr_2"][L, 0]), (16, 1, 0, 256, row(a["gla_b_lr_2"][L, 0])),
                    (32, 16, 0, 256, a["gla_w_lr_2"][L, 1]), (48, 1, 0, 256, row(a["gla_b_lr_2"][L, 1]))]

        condv = small[:, 8:16]
        mod_row = [hot[0:1, i * 512:(i + 1) * 512] for i in range(2)]

        def mod_row_pe(L):
            w_i, w = next_weight(f"mod{L}")
            b = acquire("act")
            for k in range(DC):
                m = mm(ps[0:1, b, :], condv[:, k:k + 1], w[:, k, :], start=(k == 0), stop=(k == DC - 1))
            m.then_inc(S["tile_for_act"], 1)
            frees(b, "mod_row")
            last_use(w_i, ("mod_row", expected["mod_row"]))

        def mod_cols_pe(i, rows_after):
            TE.wait_ge(S["mod_row"], expected["mod_row"] - rows_after)
            b = acquire("act")
            for j in range(4):
                m = mm(ps[:, b, j:j + 1], mod_row[i % 2][:, j * P:(j + 1) * P], C["ones"][0:1, 0:1],
                       start=True, stop=True)
            m.then_inc(S["tile_for_act"], 1)
            frees(b, "mod_part")

        def mod_pe(L, lo, hi):
            if (L, lo) == (0, 0):
                TE.wait_ge(S["cond_ready"], S.nth(TE, "cond_ready"))
            for i in range(lo, hi):
                mod_row_pe(L)
                if i > lo:
                    mod_cols_pe(i - 1, 1)
            mod_cols_pe(hi - 1, 0)

        def mod_act(L, lo, hi):
            if (L, lo) == (0, 0):
                SE.wait_ge(S["inputs_ready"], S.nth(SE, "inputs_ready"))
                SE.activation(condv, V["cond"], ACT.Silu).then_inc(S["cond_ready"], 1)
                SE.wait_ge(S["cond_ready"], S.nth(SE, "cond_ready"))
            for i in range(lo, hi + 1):
                if i < hi:
                    SE.activation(mod_row[i % 2], take("act")[0:1, :], ACT.Copy).then_inc(S["mod_row"], 1)
                    SE.wait_ge(S["mod_row"], S.nth(SE, "mod_row"))
                if i > lo:
                    o = 48 * L + 4 * (i - 1)
                    SE.activation(modv[:, o:o + 4], take("act")[:, 0:4], ACT.Copy).then_inc(S["mod_part"], 1)
                    SE.wait_ge(S["mod_part"], S.nth(SE, "mod_part"))

        def mod_dve(L, lo, hi):
            VE.wait_ge(S["mod_part"], S.nth(VE, "mod_part", hi - lo))
            m = modv[:, 48 * L:48 * L + 48]
            c = slice(4 * lo, 4 * hi)
            VE.tensor_tensor(m[:, c], m[:, c], V["mod_b"][:, 48 * L + 4 * lo:48 * L + 4 * hi],
                ALU.add).then_inc(S["dve_step"], 1)
            VE.wait_ge(S["dve_step"], S.nth(VE, "dve_step"))
            for which, norm in ((1, "norm_mix"), (4, "norm_ffn")):
                if 4 * lo <= 8 * which < 4 * hi:
                    col = m[:, 8 * which:8 * which + 8]
                    VE.scalar_tensor_tensor(out=col, in0=col, scalar=1.0, in1=V[norm][:, 8 * L:8 * L + 8],
                        op0=ALU.add, op1=ALU.mult).then_inc(S["dve_step"], 1)
                    VE.wait_ge(S["dve_step"], S.nth(VE, "dve_step"))

        def mod_cols(L, which):
            return modv[:, 48 * L + 8 * which:48 * L + 8 * which + 8]

        TWO_PI = 2 * np.pi
        C1 = 6.28125
        C2 = float(np.float32(np.round((TWO_PI - C1) * 2 ** 21) / 2 ** 21))
        C3 = float(TWO_PI - C1 - C2)
        MAGIC = 1.5 * 2 ** 23
        PI_IN = 3.1415925

        def reduced_dve(dst, ang, shift, turns, name):
            VE.tensor_scalar(turns, ang, 1 / TWO_PI, shift / TWO_PI, ALU.mult, ALU.add).then_inc(S["dve_step"], 1)
            VE.wait_ge(S["dve_step"], S.nth(VE, "dve_step"))
            VE.tensor_scalar(turns, turns, MAGIC, MAGIC, ALU.add, ALU.subtract).then_inc(S["dve_step"], 1)
            VE.wait_ge(S["dve_step"], S.nth(VE, "dve_step"))
            VE.scalar_tensor_tensor(out=dst, in0=turns, scalar=-C1, in1=ang, op0=ALU.mult,
                op1=ALU.add).then_inc(S["dve_step"], 1)
            VE.wait_ge(S["dve_step"], S.nth(VE, "dve_step"))
            VE.scalar_tensor_tensor(out=dst, in0=turns, scalar=-C2, in1=dst, op0=ALU.mult,
                op1=ALU.add).then_inc(S["dve_step"], 1)
            VE.wait_ge(S["dve_step"], S.nth(VE, "dve_step"))
            VE.scalar_tensor_tensor(out=dst, in0=turns, scalar=-C3, in1=dst, op0=ALU.mult,
                op1=ALU.add).then_inc(S["dve_step"], 1)
            VE.wait_ge(S["dve_step"], S.nth(VE, "dve_step"))
            if shift:
                VE.tensor_scalar(dst, dst, shift, None, ALU.add).then_inc(S["dve_step"], 1)
                VE.wait_ge(S["dve_step"], S.nth(VE, "dve_step"))
            VE.tensor_scalar(dst, dst, -PI_IN, PI_IN, ALU.max, ALU.min).then_inc(S[name], 1)
            VE.wait_ge(S[name], S.nth(VE, name))

        def rope_dve(which, cosv, sinv, posf, tmp, turns):
            VE.tensor_copy(posf, pos_in).then_inc(S["dve_step"], 1)
            VE.wait_ge(S["dve_step"], S.nth(VE, "dve_step"))
            VE.tensor_scalar(tmp, posf, C["invf"][:, which:which + 1], None, ALU.mult).then_inc(S["dve_step"], 1)
            VE.wait_ge(S["dve_step"], S.nth(VE, "dve_step"))
            reduced_dve(sinv, tmp, 0.0, turns, "angles")
            reduced_dve(cosv, tmp, float(np.pi / 2), turns, "angles")
            VE.wait_ge(S["tables"], S.nth(VE, "tables", 2))

        def rope_act(cosv, sinv):
            for v in (sinv, cosv):
                SE.wait_ge(S["angles"], S.nth(SE, "angles"))
                SE.activation(v, v, ACT.Sin).then_inc(S["tables"], 1)
                SE.wait_ge(S["tables"], S.nth(SE, "tables"))

        def rotate_pe(name, q, nchunk, rot, rows=P):
            TE.wait_ge(S[name], expected[name])
            for c0 in range(0, nchunk, 2):
                b = acquire("dve")
                for c in range(c0, min(c0 + 2, nchunk)):
                    m = mm(ps[:, b, (c - c0) * T:(c - c0 + 1) * T], rot, q[:, c, :], start=True, stop=True)
                m.then_inc(S["tile_for_dve"], 1)
                frees(b, "rotated")

        def rotate_dve(q, nchunk, cosv, sinv, tmp, name):
            for c0 in range(0, nchunk, 2):
                n = min(2, nchunk - c0)
                t = take("dve")[:, 0:n * T].rearrange("p (c n) -> p c n", n=T)
                bc = lambda v: v.unsqueeze(1).to_broadcast([P, n, T])
                VE.tensor_tensor(tmp[:, 0:n, :], t, bc(sinv), ALU.mult).then_inc(S["rotated"], 1)
                VE.wait_ge(S["rotated"], S.nth(VE, "rotated"))
                VE.tensor_tensor(q[:, c0:c0 + n, :], q[:, c0:c0 + n, :], bc(cosv), ALU.mult).then_inc(S["dve_step"],
                    1)
                VE.wait_ge(S["dve_step"], S.nth(VE, "dve_step"))
                signal = name if c0 + 2 >= nchunk else "dve_step"
                VE.tensor_tensor(q[:, c0:c0 + n, :], q[:, c0:c0 + n, :], tmp[:, 0:n, :], ALU.add).then_inc(S[signal],
                    1)
                VE.wait_ge(S[signal], S.nth(VE, signal))

        class Z:
            pass

        def hybrid_places():
            z, r = Z(), Scratch(True)
            z.pad = r.get(12 * 260).rearrange("p (c n) -> p c n", n=260)
            z.conv = r.mat(12)
            z.q, z.k, z.v = z.conv[:, 0:4, :], z.conv[:, 4:8, :], z.conv[:, 8:12, :]
            z.z = r.mat(4)
            z.sq = r.mat(8)
            z.rs = r.mat(8)
            z.ba = r.get(16).rearrange("p (m n) -> p m n", m=TM)
            z.bb = r.get(16).rearrange("p (m n) -> p m n", m=TM)
            z.g = r.get(8).rearrange("p (m n) -> p m n", m=TM)
            z.beta = r.get(8).rearrange("p (m n) -> p m n", m=TM)
            z.nbeta = r.get(8).rearrange("p (m n) -> p m n", m=TM)
            z.al = r.get(8)
            z.cum = r.get(32)
            z.ncum = r.get(8).rearrange("p (m n) -> p m n", m=TM)
            z.ktm = r.get(1024).rearrange("p (m h d) -> p m h d", m=TM, h=GH)
            z.kbeg = r.get(1024).rearrange("p (m h d) -> p m h d", m=TM, h=GH)
            z.kdec = z.ktm
            z.vb = r.get(1024).rearrange("p (m h d) -> p m h d", m=TM, h=GH)
            pairs8 = lambda: r.get(1024).rearrange("p (g n) -> p g n", g=8)
            z.dec, z.decT, z.R, z.N, z.NT, z.inv, z.qk = (pairs8() for _ in range(7))
            z.u = pairs8()
            z.wT = z.dec
            z.state = r.get(512).rearrange("p (h d) -> p h d", h=GH)
            z.vnew = r.get(512).rearrange("p (h d) -> p h d", h=GH)
            z.o = r.mat(4)
            z.keep = z.sq[:, 0:4, :]
            r2 = Scratch(True)
            z.aq, z.ak = r2.mat(4), r2.mat(4)
            z.av = r2.get(1024).rearrange("p (m n) -> p m n", m=TM)
            z.p = [r2.mat(2) for _ in range(2)]
            z.pt = [r2.mat(2) for _ in range(2)]
            z.st = r2.get(8)
            z.cos, z.sin, z.pos, z.t1, z.t2 = (r2.get(T) for _ in range(5))
            z.tmp = r2.mat(2)
            return z

        zh = hybrid_places()
        DK = 128
        lastdim = lambda v, n: v.unsqueeze(len(v.shape)).to_broadcast(list(v.shape) + [n])

        def hybrid_pe():
            z = zh
            block_norm_pe(z.sq)
            fm_linear("gdn_qkv", h, DC, 1536, "act", "qkv_out", arriving=True)
            fm_linear("gdn_z", h, DC, 512, "act", "z_out")
            tm_linear("gdn_ba", h, DC, 8, "dve", "ba_out")
            mod_pe(0, 4, 8)
            norm_pe([[c] for c in range(8)], 8, C["ones"], z.sq)
            TE.wait_ge(S["gates_log"], S.nth(TE, "gates_log"))
            b = acquire("dve")
            for m_ in range(TM):
                mm(ps[:, b, 8 * m_:8 * m_ + 4], C["upto"], z.g[:, m_, :], start=True, stop=True)
                mm(ps[:, b, 8 * m_ + 4:8 * m_ + 8], C["later"], z.g[:, m_, :], start=True, stop=True)
            for c in range(NCH):
                r0 = GC * (c % 2)
                i = mm(ps[:, b, 16 + 4 * c:20 + 4 * c], C["blk"][:, r0:r0 + 1].to_broadcast([P, P]), z.g[:, c // 2, :],
                       start=True, stop=True)
            i.then_inc(S["tile_for_dve"], 1)
            frees(b, "gate_sums")
            TE.wait_ge(S["gate_masks"], S.nth(TE, "gate_masks"))
            for m_ in range(TM):
                b = acquire("dve")
                i = mm(ps[:, b, :], C["ones"], z.N[:, 4 * m_:4 * m_ + 4, :], start=True, stop=True)
                i.then_inc(S["tile_for_dve"], 1)
                frees(b, "gate_rows")
            TE.wait_ge(S["qk_normed"], S.nth(TE, "qk_normed"))
            for src, pool, name in ((z.k, "act", "k_turned"), (z.v, "dve", "v_turned")):
                for m_ in range(TM):
                    b = acquire(pool)
                    for g in range(GH):
                        i = TE.transpose(ps[:, b, g * P:(g + 1) * P], src[:, g, m_ * P:(m_ + 1) * P], C["ident"])
                    i.then_inc(S[filled[pool]], 1)
                    frees(b, name)
            for lhs, rhs, name in ((z.k, z.k, "kk_out"), (z.k, z.q, "kq_out")):
                for m_ in range(TM):
                    b = acquire("dve")
                    tok = slice(m_ * P, (m_ + 1) * P)
                    for g in range(GH):
                        i = mm(ps[:, b, g * P:(g + 1) * P], lhs[:, g, tok], rhs[:, g, tok], start=True, stop=True)
                    i.then_inc(S["tile_for_dve"], 1)
                    frees(b, name)
            mod_pe(0, 8, 12)
            TE.wait_ge(S["n_ready"], S.nth(TE, "n_ready"))
            for m_ in range(TM):
                b = acquire("act")
                for g in range(GH):
                    i = TE.transpose(ps[:, b, g * P:(g + 1) * P], z.N[:, 4 * m_ + g, :], C["ident"])
                i.then_inc(S["tile_for_act"], 1)
                frees(b, "powers")
            for r in range(5):
                TE.wait_ge(S["powers"], expected["powers"])
                for lhs, rhs in ((z.NT, z.N),) + (((z.N, z.NT),) if r < 4 else ()):
                    for m_ in range(TM):
                        b = acquire("act")
                        for g in range(4 * m_, 4 * m_ + 4):
                            i = mm(ps[:, b, (g % 4) * P:(g % 4 + 1) * P], lhs[:, g, :], rhs[:, g, :],
                                   start=True, stop=True)
                        i.then_inc(S["tile_for_act"], 1)
                        frees(b, "powers")
                TE.wait_ge(S["powers"], expected["powers"])
                TE.wait_ge(S["inverse"], S.nth(TE, "inverse"))
                for m_ in range(TM):
                    b = acquire("dve")
                    for g in range(4 * m_, 4 * m_ + 4):
                        i = mm(ps[:, b, (g % 4) * P:(g % 4 + 1) * P], z.N[:, g, :], z.inv[:, g, :],
                               start=True, stop=True)
                    i.then_inc(S["tile_for_dve"], 1)
                    frees(b, "inverse_part")
            TE.wait_ge(S["inverse"], S.nth(TE, "inverse"))
            TE.wait_ge(S["k_scaled"], S.nth(TE, "k_scaled"))
            for m_ in range(TM):
                b = acquire("act")
                for g in range(GH):
                    i = mm(ps[:, b, g * P:(g + 1) * P], z.inv[:, 4 * m_ + g, :], z.vb[:, m_, g, :], start=True, stop=True)
                i.then_inc(S["tile_for_act"], 1)
                frees(b, "uw_out")
            for m_ in range(TM):
                b = acquire("act")
                for g in range(GH):
                    i = mm(ps[:, b, g * P:(g + 1) * P], z.kbeg[:, m_, g, :], z.inv[:, 4 * m_ + g, :],
                           start=True, stop=True)
                i.then_inc(S["tile_for_act"], 1)
                frees(b, "uw_out")
            TE.wait_ge(S["uw_out"], expected["uw_out"])
            for c in range(NCH):
                m_, r0 = c // 2, GC * (c % 2)
                rows = slice(r0, r0 + GC)
                TE.wait_ge(S["state_ready"], S.nth(TE, "state_ready"))
                b = acquire("dve")
                for g in range(GH):
                    i = mm(ps[:, b, g * P:(g + 1) * P], z.wT[:, 4 * m_ + g, :], z.state[:, g, :], start=True, stop=True)
                i.then_inc(S["tile_for_dve"], 1)
                frees(b, "v_new")
                TE.wait_ge(S["v_new"], expected["v_new"])
                b = acquire("act")
                for g in range(GH):
                    mm(ps[:, b, g * GC:(g + 1) * GC], z.state[:, g, :], z.q[:, g, c * GC:(c + 1) * GC],
                       start=True, stop=False)
                    i = mm(ps[:, b, g * GC:(g + 1) * GC], z.vnew[rows, g, :], z.qk[rows, 4 * m_ + g, rows],
                           start=False, stop=True)
                i.then_inc(S["tile_for_act"], 1)
                frees(b, "delta_out")
                if c < NCH - 1:
                    b = acquire("dve")
                    for g in range(GH):
                        i = mm(ps[:, b, g * P:(g + 1) * P], z.kdec[rows, m_, g, :], z.vnew[rows, g, :],
                               start=True, stop=True)
                    i.then_inc(S["tile_for_dve"], 1)
                    frees(b, "state_grown")
            norm_pe([[c] for c in range(4)], 4, C["ones"], z.sq)
            TE.wait_ge(S["delta_through"], S.nth(TE, "delta_through"))
            fm_linear("moba_q", h, DC, 512, "act", "att_in")
            fm_linear("moba_k", h, DC, 512, "act", "att_in")
            tm_linear("moba_v", h, DC, 512, "act", "att_in")
            rotate_pe("att_in", z.aq, 4, C["rot128"])
            rotate_pe("att_in", z.ak, 4, C["rot128"])
            TE.wait_ge(S["k_rotated"], S.nth(TE, "k_rotated"))

            def scores(i, b):
                for t in range(TM):
                    m = mm(ps[:, b, t * T:(t + 1) * T], z.aq[:, i, t * P:(t + 1) * P], z.ak[:, i, :],
                           start=True, stop=True)
                return m

            def values(i, pt):
                b = acquire("dve")
                value_product(z.av, slice(i * P, (i + 1) * P), b, 0, pt).then_inc(S["tile_for_dve"], 1)
                frees(b, "o_out")
            attention_pe(4, scores, values, z.p, z.pt)
            TE.wait_ge(S["o_out"], expected["o_out"])
            fm_linear("hy_out", h, DC, D, "dve", "residual_in")

        def hybrid_act():
            z = zh
            SE.wait_ge(S["x_new"], S.nth(SE, "x_new"))
            block_norm_act(z.sq, z.rs)
            evict_act([z.pad[:, c:c + 2, 4:260] for c in range(0, 12, 2)], frees="qkv_out", n=6)
            evict_act(pairs(z.z), ACT.Silu, frees="z_out", n=2)
            mod_act(0, 4, 8)
            SE.wait_ge(S["conv_done"], S.nth(SE, "conv_done"))
            SE.activation(z.conv, z.conv, ACT.Silu).then_inc(S["silu_done"], 1)
            SE.wait_ge(S["silu_done"], S.nth(SE, "silu_done"))
            norm_act(z.conv[:, 0:8, :], z.sq, z.rs, 8, 1.0)
            SE.wait_ge(S["ba_ready"], S.nth(SE, "ba_ready"))
            SE.activation(z.bb, z.bb, ACT.Exp, scale=-1.0).then_inc(S["act_step"], 1)
            SE.wait_ge(S["act_step"], S.nth(SE, "act_step"))
            SE.activation(z.al[:, 0:4], z.al[:, 0:4], ACT.Exp).then_inc(S["ba_exp"], 1)
            SE.wait_ge(S["ba_exp"], S.nth(SE, "ba_exp"))
            SE.activation(z.ba[:, :, 4:8], z.bb[:, :, 4:8], ACT.Ln, bias=1.0).then_inc(S["ba_ln"], 1)
            SE.wait_ge(S["ba_ln"], S.nth(SE, "ba_ln"))
            SE.wait_ge(S["decay_rows"], S.nth(SE, "decay_rows"))
            for g in range(8):
                m_, hh = g // 4, g % 4
                SE.activation(z.dec[:, g, :], z.dec[:, g, :], ACT.Exp, bias=z.cum[:, 8 * m_ + hh:8 * m_ + hh + 1])\
                    .then_inc(S["act_step"], 1)
                SE.activation(z.decT[:, g, :], z.decT[:, g, :], ACT.Exp, bias=z.ncum[:, m_, hh:hh + 1])\
                    .then_inc(S["act_step"], 1)
            SE.wait_ge(S["act_step"], S.nth(SE, "act_step", 16))
            SE.activation(z.R, z.R, ACT.Exp).then_inc(S["act_step"], 1)
            SE.wait_ge(S["act_step"], S.nth(SE, "act_step"))
            SE.activation(z.cum, z.cum, ACT.Exp).then_inc(S["decays"], 1)
            SE.wait_ge(S["decays"], S.nth(SE, "decays"))
            evict_act([z.ktm[:, m_] .rearrange("p h d -> p (h d)") for m_ in range(TM)], frees="k_turned", n=2)
            mod_act(0, 8, 12)
            g4 = lambda v, m_: v[:, 4 * m_:4 * m_ + 4, :]
            evict_act([g4(z.NT, m_) for m_ in range(TM)], frees="powers", n=2)
            SE.wait_ge(S["inverse"], S.nth(SE, "inverse"))
            for r in range(5):
                k = 2 if r == 4 else 4
                got = [take("act") for _ in range(k)]
                for j, t in enumerate(got):
                    SE.activation(g4((z.N, z.NT)[j // 2], j % 2), t.rearrange("p (c n) -> p c n", c=4),
                        ACT.Copy).then_inc(S["powers"], 1)
                    SE.wait_ge(S["powers"], S.nth(SE, "powers"))
            evict_act([g4(z.u, 0), g4(z.u, 1)], frees="uw_out", n=2)
            evict_act([g4(z.wT, 0), g4(z.wT, 1)], frees="uw_out", n=2)
            for c in range(NCH):
                evict_act([z.o[:, :, c * GC:(c + 1) * GC]], frees="delta_out")
            norm_act(z.o, z.sq[:, 0:4, :], z.rs, 4, 128.0)
            SE.wait_ge(S["delta_through"], S.nth(SE, "delta_through"))
            evict_act(pairs(z.aq) + pairs(z.ak) + [z.av[:, 0, :], z.av[:, 1, :]], frees="att_in", n=6)
            rope_act(z.cos, z.sin)
            attention_act(4, z.p, z.pt, 128 ** -0.5, z.st)

        def hybrid_dve():
            z = zh
            block_norm_dve(z.rs, mod_cols(0, 1), mod_cols(0, 0))
            VE.memset(z.pad[:, :, 0:4], 0.0).then_inc(S["dve_step"], 1)
            VE.wait_ge(S["dve_step"], S.nth(VE, "dve_step"))
            VE.wait_ge(S["qkv_out"], S.nth(VE, "qkv_out", 6))
            w = V["gdn_conv"].rearrange("p (c j) -> p c j", j=4)
            for j in range(4):
                for c in range(12):
                    src = z.pad[:, c, 1 + j:1 + j + T]
                    if j == 0:
                        VE.tensor_scalar(z.conv[:, c, :], src, w[:, c, 0:1], None, ALU.mult).then_inc(S["dve_step"], 1)
                    else:
                        VE.scalar_tensor_tensor(out=z.conv[:, c, :], in0=src, scalar=w[:, c, j:j + 1],
                                                in1=z.conv[:, c, :], op0=ALU.mult, op1=ALU.add).then_inc(S["dve_step"], 1)
                VE.wait_ge(S["dve_step"], S.nth(VE, "dve_step", 12))
            VE.tensor_copy(small[:, 1:2], small[:, 0:1]).then_inc(S["conv_done"], 1)
            VE.wait_ge(S["conv_done"], S.nth(VE, "conv_done"))
            for m_ in range(TM):
                VE.tensor_copy(z.ba[:, m_, :], take("dve")[:, 0:8]).then_inc(S["ba_out"], 1)
                VE.wait_ge(S["ba_out"], S.nth(VE, "ba_out"))
            VE.tensor_copy(z.bb[:, :, 0:4], z.ba[:, :, 0:4]).then_inc(S["dve_step"], 1)
            VE.wait_ge(S["dve_step"], S.nth(VE, "dve_step"))
            VE.tensor_tensor(z.g, z.ba[:, :, 4:8], z.al[:, 4:8].unsqueeze(1).to_broadcast([P, TM, 4]),
                ALU.add).then_inc(S["dve_step"], 1)
            VE.wait_ge(S["dve_step"], S.nth(VE, "dve_step"))
            VE.scalar_tensor_tensor(out=z.bb[:, :, 4:8], in0=z.g, scalar=-1.0, in1=z.g, op0=ALU.mult,
                op1=ALU.max).then_inc(S["ba_ready"], 1)
            VE.wait_ge(S["ba_ready"], S.nth(VE, "ba_ready"))
            VE.wait_ge(S["ba_exp"], S.nth(VE, "ba_exp"))
            VE.tensor_scalar(z.beta, z.bb[:, :, 0:4], 1.0, None, ALU.add).then_inc(S["dve_step"], 1)
            VE.wait_ge(S["dve_step"], S.nth(VE, "dve_step"))
            VE.reciprocal(z.beta, z.beta).then_inc(S["dve_step"], 1)
            VE.wait_ge(S["dve_step"], S.nth(VE, "dve_step"))
            VE.tensor_scalar(z.nbeta, z.beta, -1.0, None, ALU.mult).then_inc(S["dve_step"], 1)
            VE.wait_ge(S["dve_step"], S.nth(VE, "dve_step"))
            VE.wait_ge(S["ba_ln"], S.nth(VE, "ba_ln"))
            VE.scalar_tensor_tensor(out=z.g, in0=z.g, scalar=0.0, in1=z.ba[:, :, 4:8], op0=ALU.max,
                op1=ALU.add).then_inc(S["dve_step"], 1)
            VE.wait_ge(S["dve_step"], S.nth(VE, "dve_step"))
            VE.tensor_scalar(z.g, z.g, -1.0, None, ALU.mult).then_inc(S["dve_step"], 1)
            VE.wait_ge(S["dve_step"], S.nth(VE, "dve_step"))
            VE.tensor_tensor(z.g, z.g, z.al[:, 0:4].unsqueeze(1).to_broadcast([P, TM, 4]),
                ALU.mult).then_inc(S["gates_log"], 1)
            VE.wait_ge(S["gates_log"], S.nth(VE, "gates_log"))
            for g in range(8):
                signal = "gate_masks" if g == 7 else "dve_step"
                VE.tensor_scalar(z.N[:, g, :], C["upto"], z.g[:, g // 4, g % 4:g % 4 + 1], None,
                    ALU.mult).then_inc(S[signal], 1)
                VE.wait_ge(S[signal], S.nth(VE, signal))
            norm_dve(z.rs, 8)
            VE.tensor_tensor(z.conv[:, 0:8, :], z.conv[:, 0:8, :], z.rs, ALU.mult).then_inc(S["dve_step"], 1)
            VE.wait_ge(S["dve_step"], S.nth(VE, "dve_step"))
            VE.tensor_scalar(z.q, z.q, float(DK) ** -0.5, None, ALU.mult).then_inc(S["qk_normed"], 1)
            VE.wait_ge(S["qk_normed"], S.nth(VE, "qk_normed"))
            VE.tensor_copy(z.cum, take("dve")[:, 0:32]).then_inc(S["gate_sums"], 1)
            VE.wait_ge(S["gate_sums"], S.nth(VE, "gate_sums"))
            gcv = z.cum[:, 0:16].rearrange("p (m n) -> p m n", m=TM)
            VE.tensor_scalar(z.ncum, gcv[:, :, 0:4], -1.0, None, ALU.mult).then_inc(S["dve_step"], 1)
            VE.wait_ge(S["dve_step"], S.nth(VE, "dve_step"))
            bc4 = lambda v: v.unsqueeze(1).to_broadcast([P, 4, P])
            for m_ in range(TM):
                t = take("dve").rearrange("p (c n) -> p c n", c=4)
                s4 = slice(4 * m_, 4 * m_ + 4)
                VE.scalar_tensor_tensor(out=z.dec[:, s4, :], in0=t, scalar=-1.0, in1=bc4(C["mlow"]), op0=ALU.mult,
                    op1=ALU.add).then_inc(S["dve_step"], 1)
                VE.wait_ge(S["dve_step"], S.nth(VE, "dve_step"))
                VE.tensor_tensor(z.decT[:, s4, :], t, bc4(C["mup"]), ALU.add).then_inc(S["dve_step"], 1)
                VE.wait_ge(S["dve_step"], S.nth(VE, "dve_step"))
                VE.tensor_copy(z.R[:, s4, :], t).then_inc(S["gate_rows"], 1)
                VE.wait_ge(S["gate_rows"], S.nth(VE, "gate_rows"))
            VE.memset(z.state, 0.0).then_inc(S["decay_rows"], 1)
            VE.wait_ge(S["decay_rows"], S.nth(VE, "decay_rows"))
            VE.wait_ge(S["decays"], S.nth(VE, "decays"))
            for m_ in range(TM):
                t = take("dve").rearrange("p (h d) -> p h d", h=GH)
                VE.tensor_tensor(z.vb[:, m_], t, lastdim(z.beta[:, m_, :], P), ALU.mult).then_inc(S["v_turned"], 1)
                VE.wait_ge(S["v_turned"], S.nth(VE, "v_turned"))
            VE.wait_ge(S["k_turned"], S.nth(VE, "k_turned", 2))
            for m_ in range(TM):
                VE.tensor_tensor(z.ncum[:, m_, :], z.beta[:, m_, :], gcv[:, m_, 0:4],
                    ALU.mult).then_inc(S["dve_step"], 1)
                VE.wait_ge(S["dve_step"], S.nth(VE, "dve_step"))
                VE.tensor_tensor(z.kbeg[:, m_], z.ktm[:, m_], lastdim(z.ncum[:, m_, :], P),
                    ALU.mult).then_inc(S["dve_step"], 1)
                VE.wait_ge(S["dve_step"], S.nth(VE, "dve_step"))
                VE.tensor_tensor(z.kdec[:, m_], z.ktm[:, m_], lastdim(gcv[:, m_, 4:8], P),
                    ALU.mult).then_inc(S["dve_step"], 1)
                VE.wait_ge(S["dve_step"], S.nth(VE, "dve_step"))
            for m_ in range(TM):
                t = take("dve").rearrange("p (c n) -> p c n", c=4)
                s4 = slice(4 * m_, 4 * m_ + 4)
                VE.tensor_tensor(z.N[:, s4, :], t, z.dec[:, s4, :], ALU.mult).then_inc(S["kk_out"], 1)
                VE.wait_ge(S["kk_out"], S.nth(VE, "kk_out"))
                for g in range(4 * m_, 4 * m_ + 4):
                    signal = "n_ready" if g == 7 else "dve_step"
                    VE.scalar_tensor_tensor(out=z.N[:, g, :], in0=z.N[:, g, :],
                        scalar=z.nbeta[:, m_,
                        g % 4:g % 4 + 1], in1=C["later"], op0=ALU.mult, op1=ALU.mult).then_inc(S[signal], 1)
                    VE.wait_ge(S[signal], S.nth(VE, signal))
            for m_ in range(TM):
                t = take("dve").rearrange("p (c n) -> p c n", c=4)
                s4 = slice(4 * m_, 4 * m_ + 4)
                VE.tensor_tensor(z.qk[:, s4, :], t, z.decT[:, s4, :], ALU.mult).then_inc(S["kq_out"], 1)
                VE.wait_ge(S["kq_out"], S.nth(VE, "kq_out"))
            qv = z.q.rearrange("p h (m t) -> p m h t", m=TM)
            VE.tensor_tensor(qv, qv, z.R.rearrange("p (m h) t -> p m h t", m=TM), ALU.mult).then_inc(S["k_scaled"], 1)
            VE.wait_ge(S["k_scaled"], S.nth(VE, "k_scaled"))
            VE.wait_ge(S["powers"], S.nth(VE, "powers", 2))
            for m_ in range(TM):
                signal = "inverse" if m_ else "dve_step"
                VE.tensor_tensor(z.inv[:, 4 * m_:4 * m_ + 4, :], z.NT[:, 4 * m_:4 * m_ + 4, :], bc4(C["ident"]),
                    ALU.add).then_inc(S[signal], 1)
                VE.wait_ge(S[signal], S.nth(VE, signal))
            for r in range(5):
                for m_ in range(TM):
                    t = take("dve").rearrange("p (c n) -> p c n", c=4)
                    s4 = slice(4 * m_, 4 * m_ + 4)
                    VE.tensor_tensor(z.inv[:, s4, :], z.inv[:, s4, :], t, ALU.add).then_inc(S["inverse_part"], 1)
                    VE.wait_ge(S["inverse_part"], S.nth(VE, "inverse_part"))
                VE.tensor_scalar(small[:, 2:3], small[:, 0:1], 1.0, None, ALU.mult).then_inc(S["inverse"], 1)
                VE.wait_ge(S["inverse"], S.nth(VE, "inverse"))
            VE.wait_ge(S["uw_out"], S.nth(VE, "uw_out", 4))
            VE.tensor_scalar(small[:, 2:3], small[:, 0:1], 1.0, None, ALU.mult).then_inc(S["state_ready"], 1)
            VE.wait_ge(S["state_ready"], S.nth(VE, "state_ready"))
            for c in range(NCH):
                m_, r0 = c // 2, GC * (c % 2)
                rows = slice(r0, r0 + GC)
                t = take("dve").rearrange("p (h d) -> p h d", h=GH)
                VE.tensor_tensor(z.vnew[rows], z.u[rows, 4 * m_:4 * m_ + 4, :], t[rows],
                    ALU.subtract).then_inc(S["v_new"], 1)
                VE.wait_ge(S["v_new"], S.nth(VE, "v_new"))
                if c < NCH - 1:
                    t = take("dve").rearrange("p (h d) -> p h d", h=GH)
                    VE.tensor_tensor(z.state, z.state, lastdim(z.cum[:, 16 + 4 * c:20 + 4 * c], P),
                        ALU.mult).then_inc(S["dve_step"], 1)
                    VE.wait_ge(S["dve_step"], S.nth(VE, "dve_step"))
                    VE.tensor_tensor(z.state, z.state, t, ALU.add).then_inc(S["state_grown"], 1)
                    VE.wait_ge(S["state_grown"], S.nth(VE, "state_grown"))
                    VE.tensor_scalar(small[:, 2:3], small[:, 0:1], 1.0, None, ALU.mult).then_inc(S["state_ready"], 1)
                    VE.wait_ge(S["state_ready"], S.nth(VE, "state_ready"))
            norm_dve(z.rs, 4)
            for g in range(GH):
                VE.scalar_tensor_tensor(out=z.o[:, g, :], in0=z.o[:, g, :], scalar=V["gdn_o_norm"][:, 0:1],
                    in1=z.rs[:, g, :], op0=ALU.mult, op1=ALU.mult).then_inc(S["dve_step"], 1)
                VE.wait_ge(S["dve_step"], S.nth(VE, "dve_step"))
            VE.tensor_tensor(z.keep, z.o, z.z, ALU.mult).then_inc(S["delta_through"], 1)
            VE.wait_ge(S["delta_through"], S.nth(VE, "delta_through"))
            rope_dve(0, z.cos, z.sin, z.pos, z.t1, z.t2)
            VE.wait_ge(S["att_in"], S.nth(VE, "att_in", 6))
            rotate_dve(z.aq, 4, z.cos, z.sin, z.tmp, "dve_step")
            rotate_dve(z.ak, 4, z.cos, z.sin, z.tmp, "k_rotated")
            VE.tensor_copy(h[:, 0:4, :], z.keep).then_inc(S["dve_step"], 1)
            VE.wait_ge(S["dve_step"], S.nth(VE, "dve_step"))

            def out(i):
                VE.tensor_copy(h[:, 4 + i, :], take("dve")[:, 0:T]).then_inc(S["o_out"], 1)
                VE.wait_ge(S["o_out"], S.nth(VE, "o_out"))
            attention_dve(4, z.p, causal, 128 ** -0.5, z.st, out)
            mod_dve(0, 4, 12)
            residual_dve(mod_cols(0, 2))

        def mla_places():
            z, r = Z(), Scratch(False)
            z.sq, z.rs = r.mat(8), r.mat(1)
            z.cq, z.ckv = r.mat(4), r.mat(2)
            z.kr, z.qr = r.mat(1), r.mat(4)
            z.cos, z.sin, z.pos, z.t1, z.t2 = (r.get(T) for _ in range(5))
            z.tmp = r.mat(2)
            z.qn, z.kn = r.mat(8), r.mat(8)
            z.v = r.get(2048).rearrange("p (m n) -> p m n", m=TM)
            z.p = [r.mat(2) for _ in range(2)]
            z.pt = [r.mat(2) for _ in range(2)]
            z.st = r.get(8)
            return z
        zm = mla_places()

        def mla_pe():
            z = zm
            block_norm_pe(z.sq)
            fm_linear("mla_cq", h, DC, 512, "act", "latent_in", arriving=True)
            fm_linear("mla_ckv", h, DC, 256, "act", "latent_in")
            fm_linear("mla_kr", h, DC, P, "act", "kr_in")
            norm_pe([[0, 1, 2, 3]], 4, C["ones"], z.sq)
            norm_pe([[0, 1]], 2, C["ones"], z.sq)
            rotate_pe("kr_in", z.kr, 1, C["rot64"])
            TE.wait_ge(S["latent_ready"], S.nth(TE, "latent_ready", 2))
            fm_linear("mla_qn", z.cq, 4, 1024, "act", "mla_up")
            fm_linear("mla_qr", z.cq, 4, 512, "act", "qr_in")
            fm_linear("mla_kn", z.ckv, 2, 1024, "act", "mla_up")
            tm_linear("mla_v", z.ckv, 2, 1024, "act", "mla_up")
            rotate_pe("qr_in", z.qr, 4, C["rot64"])
            TE.wait_ge(S["q_rotated"], S.nth(TE, "q_rotated"))
            TE.wait_ge(S["mla_up"], expected["mla_up"])

            def scores(i, b):
                r0 = 64 * (i % 2)
                for t in range(TM):
                    tok = slice(t * P, (t + 1) * P)
                    mm(ps[:, b, t * T:(t + 1) * T], z.qn[:, i, tok], z.kn[:, i, :], start=True, stop=False)
                    m = mm(ps[:, b, t * T:(t + 1) * T], z.qr[r0:r0 + 64, i // 2, tok], z.kr[r0:r0 + 64, 0, :],
                           start=False, stop=True)
                return m

            def values(i, pt):
                b = acquire("dve")
                value_product(z.v, slice(i * P, (i + 1) * P), b, 0, pt).then_inc(S["tile_for_dve"], 1)
                frees(b, "o_out")
            attention_pe(MLA_H, scores, values, z.p, z.pt)
            TE.wait_ge(S["o_out"], expected["o_out"])
            fm_linear("mla_out", h, DC, D, "dve", "residual_in")

        def mla_act():
            z = zm
            block_norm_act(z.sq, z.rs, "sums_read")
            evict_act(pairs(z.cq) + pairs(z.ckv), frees="latent_in", n=3)
            evict_act([z.kr], frees="kr_in")
            norm_act(z.cq, z.sq[:, 0:4, :], z.rs, 1, 512.0)
            SE.wait_ge(S["latent_ready"], S.nth(SE, "latent_ready"))
            norm_act(z.ckv, z.sq[:, 0:2, :], z.rs, 1, 256.0)
            evict_act(pairs(z.qn), frees="mla_up", n=4)
            evict_act(pairs(z.qr), frees="qr_in", n=2)
            evict_act(pairs(z.kn), frees="mla_up", n=4)
            evict_act([z.v[:, t, n:n + 512] for n in (0, 512) for t in range(TM)], frees="mla_up", n=4)
            rope_act(z.cos, z.sin)
            attention_act(MLA_H, z.p, z.pt, 192 ** -0.5, z.st)

        def mla_dve():
            z = zm
            block_norm_dve(z.rs, mod_cols(1, 1), mod_cols(1, 0))
            for lat, n, gain in ((z.cq, 4, "q_norm"), (z.ckv, 2, "kv_norm")):
                norm_dve(z.rs, 1)
                for c in range(n):
                    signal = "latent_ready" if c == n - 1 else "dve_step"
                    VE.scalar_tensor_tensor(out=lat[:, c, :], in0=lat[:, c, :], scalar=V[gain][:, c:c + 1],
                        in1=z.rs[:, 0, :], op0=ALU.mult, op1=ALU.mult).then_inc(S[signal], 1)
                    VE.wait_ge(S[signal], S.nth(VE, signal))
            rope_dve(1, z.cos, z.sin, z.pos, z.t1, z.t2)
            VE.wait_ge(S["kr_in"], S.nth(VE, "kr_in"))
            rotate_dve(z.kr, 1, z.cos, z.sin, z.tmp, "dve_step")
            VE.wait_ge(S["qr_in"], S.nth(VE, "qr_in", 2))
            rotate_dve(z.qr, 4, z.cos, z.sin, z.tmp, "q_rotated")

            def out(i):
                VE.tensor_copy(h[:, i, :], take("dve")[:, 0:T]).then_inc(S["o_out"], 1)
                VE.wait_ge(S["o_out"], S.nth(VE, "o_out"))
            attention_dve(MLA_H, z.p, causal, 192 ** -0.5, z.st, out)
            residual_dve(mod_cols(1, 2))

        def peer_places():
            z, r = Z(), Scratch(False)
            z.sq, z.rs = r.mat(8), r.mat(1)
            z.q = r.mat(HP)
            z.sc = r.get(TM * HP * NKEY).rearrange("p (m g n) -> p m g n", m=TM, g=HP)
            z.cand = r.get(PEER_H * T).rearrange("p (g n) -> p g n", g=PEER_H)
            g16 = lambda g: r.get(g * 16).rearrange("p (g k) -> p g k", k=16)
            z.s = g16(HP)
            z.i = g16(HP)
            z.iu = r.get(HP * 16).bitcast(U32).rearrange("p (g k) -> p g k", k=16)
            z.top, z.pa, z.pb, z.gate, z.e1, z.e2 = (g16(PEER_H) for _ in range(6))
            z.pu, z.pv = (r.get(PEER_H * 16).bitcast(U32).rearrange("p (g k) -> p g k", k=16) for _ in range(2))
            z.eq = r.get(PEER_H * T).rearrange("p (g k a) -> p g k a", g=PEER_H, a=16)
            z.sum = r.get(8)
            return z
        zp = peer_places()
        gates_all = big[:].rearrange("p (j t) -> p j t", t=T)
        by_token = sel.rearrange("p (w t) -> p w t", t=T)
        NG = T // GRP
        NI = NKEY // UV_RING
        hot1 = [hot[:, g * 2 * GRP * P:g * 2 * GRP * P + GRP * P].rearrange("p (t n) -> p t n", n=P) for g in range(2)]
        hot2 = [hot[:, (g * 2 + 1) * GRP * P:(g * 2 + 2) * GRP * P].rearrange("p (t n) -> p t n", n=P) for g in range(2)]
        gelu = [hot[:, g * T:(g + 1) * T] for g in range(2)]
        prod_high = [hot_r[:, (2 + g) * T:(3 + g) * T] for g in range(2)]
        prod_low = [hot_r[:, (4 + g) * T:(5 + g) * T] for g in range(2)]
        h_high = consts_r[:, 0:DC * T]
        h_low_all = ht_r[:]
        experts_high = [high_r[:], xt_r[:]]

        def uv_slot(s):
            v = uvr[:, s * UV_W:(s + 1) * UV_W]
            return v[:, 0:D], v[:, D:2 * D]

        def uv_low(s):
            v = uvr_r[:, s * UV_W:(s + 1) * UV_W]
            return v[:, 0:D], v[:, D:2 * D]

        def three_passes(out, w_high, w_low, x_high, x_low, start, stop, **kw):
            mm(out, w_high, x_high, start=start, stop=False, **kw)
            mm(out, w_high, x_low, start=False, stop=False, **kw)
            return mm(out, w_low, x_high, start=False, stop=stop, **kw)

        CREDITS = {"gates_out": 4, "gelu_taken": 4, "gate_applied": 2, "experts_used": 2}

        def loop_count(L, name):
            per = {"gates_out": NG, "hot_ready": NG}.get(name, NKEY)
            return L * per + CREDITS.get(name, 0)

        def peer_pe(L):
            z = zp
            block_norm_pe(z.sq)
            fm_linear("peer_q", h, DC, HP * P, "act", "peer_q_in", arriving=True)
            i_, w = next_weight("sub_keys")
            TE.wait_ge(S["peer_q_in"], expected["peer_q_in"])
            for t in range(TM):
                for g0 in range(0, HP, 4):
                    b = acquire("act")
                    for g in range(g0, g0 + 4):
                        m = mm(ps[:, b, (g - g0) * P:(g - g0 + 1) * P], z.q[:, g, t * P:(t + 1) * P], w[:, g, :],
                               start=True, stop=True)
                    m.then_inc(S["tile_for_act"], 1)
                    frees(b, "key_scores")
            last_use(i_, ("key_scores", expected["key_scores"]))
            for t in range(TM):
                if L == 0:
                    mod_pe(1, 6 * t, 6 * t + 6)
                TE.wait_ge(S["chosen"], S.nth(TE, "chosen"))
                b = acquire("dve")
                for k, v in enumerate((z.e1, z.e2, z.gate)):
                    m = TE.transpose(ps[:, b, k * P:(k + 1) * P], v.rearrange("p g k -> p (g k)"), C["ident"])
                m.then_inc(S["tile_for_dve"], 1)
                frees(b, "chosen_turned")
            for b in range(4):
                TE.wait_ge(S[freed_by[b][0]], freed_by[b][1])
            base = acquired["act"]
            with TE.Fori(0, NG // 4) as it:
                for g in range(4):
                    b = (base + g) % 4
                    TE.wait_ge(S["hot_ready"], it * 4 + (loop_count(L, "hot_ready") + g + 1))
                    TE.wait_ge(S["gates_out"], it * 4 + (loop_count(L, "gates_out") + g + 1 - 4))
                    for t in range(GRP):
                        m = mm(ps[:, b, t * P:(t + 1) * P], hot1[g % 2][:, t, :], hot2[g % 2][:, t, :],
                               start=True, stop=True)
                    m.then_inc(S["tile_for_act"], 1)
            acquired["act"] += NG
            for b in range(4):
                TE.wait_ge(S["gates_out"], loop_count(L + 1, "gates_out"))
            TE.wait_ge(S["sums_cleared"], S.nth(TE, "sums_cleared"))
            base = acquired["act"]

            TE.wait_ge(S["h_split"], S.nth(TE, "h_split"))

            def activations(s, j):
                u_low, u_high = uv_low(s)[0], experts_high[s % 2][:, 0:D]
                TE.wait_ge(S["u_split"], j + (loop_count(L, "u_split") + 1))
                TE.wait_ge(S["gelu_taken"], j + (loop_count(L, "gelu_taken") + 1 - 4))
                b = (base + s) % 4
                for c in range(DC):
                    e, t = slice(c * P, (c + 1) * P), slice(c * T, (c + 1) * T)
                    m = three_passes(ps[:, b, 0:T], u_high[:, e], u_low[:, e], h_high[:, t], h_low_all[:, t],
                                     start=(c == 0), stop=(c == DC - 1))
                m.then_inc(S["tile_for_act"], 1)

            def outputs(s, j):
                v_low, v_high = uv_low(s)[1], experts_high[s % 2][:, D:2 * D]
                TE.wait_ge(S["v_split"], j + (loop_count(L, "v_split") + 1))
                TE.wait_ge(S["gate_applied"], j + (loop_count(L, "gate_applied") + 1))
                for c in range(DC):
                    f = slice(c * P, (c + 1) * P)
                    m = three_passes(ps[:, 4 + c // 2, (c % 2) * T:(c % 2 + 1) * T], v_high[:, f], v_low[:, f],
                                     prod_high[s % 2], prod_low[s % 2], start=False, stop=False,
                                     skip_group_check=True)
                m.then_inc(S["experts_used"], 1)

            activations(0, 0)
            with TE.Fori(0, NI - 1) as it:
                for s in range(UV_RING):
                    activations((s + 1) % UV_RING, it * UV_RING + (s + 1))
                    outputs(s, it * UV_RING + s)
            last = (NI - 1) * UV_RING
            for s in range(UV_RING):
                if s + 1 < UV_RING:
                    activations(s + 1, last + s + 1)
                outputs(s, last + s)
            acquired["act"] += NKEY
            for b in range(4):
                freed_by[b] = ("gelu_taken", loop_count(L + 1, "gelu_taken"))
                freed_by[4 + b] = ("sums_read", 4 * L + b + 1)

        def peer_act(L):
            z = zp
            block_norm_act(z.sq, z.rs, "residual_in")
            evict_act(pairs(z.q), frees="peer_q_in", n=HP // 2)
            evict_act([z.sc[:, t, g:g + 4, :] for t in range(TM) for g in range(0, HP, 4)], frees="key_scores", n=8)
            for t in range(TM):
                if L == 0:
                    mod_act(1, 6 * t, 6 * t + 6)
                SE.wait_ge(S["top_shifted"], S.nth(SE, "top_shifted"))
                SE.activation(z.gate, z.gate, ACT.Exp).then_inc(S["top_exp"], 1)
                SE.wait_ge(S["top_exp"], S.nth(SE, "top_exp"))
            base = taken["act"]
            with SE.Fori(0, NG // 4) as it:
                for g in range(4):
                    b = (base + g) % 4
                    SE.wait_ge(S["tile_for_act"], it * 4 + (base + g + 1))
                    dst = gates_all[:, :, bass.ds(it * (4 * GRP) + g * GRP, GRP)].rearrange("p j t -> p t j")
                    SE.activation(dst, ps[:, b, :].rearrange("p (t j) -> p t j", t=GRP), ACT.Copy)\
                        .then_inc(S["gates_out"], 1)
            taken["act"] += NG
            SE.wait_ge(S["gates_out"], loop_count(L + 1, "gates_out"))
            SE.activation(h_high, ht[:], ACT.Copy).then_inc(S["h_high"], 1)
            base = taken["act"]

            def u_high(s, it):
                SE.wait_ge(S[f"u_in_{s}"], it * 16 + (16 * NI * L + 16))
                SE.activation(experts_high[s % 2][:, 0:D], uv_slot(s)[0], ACT.Copy).then_inc(S["u_high"], 1)

            def v_high(s, it):
                SE.wait_ge(S[f"v_in_{s}"], it * 16 + (16 * NI * L + 16))
                SE.activation(experts_high[s % 2][:, D:2 * D], uv_slot(s)[1], ACT.Copy).then_inc(S["v_high"], 1)

            SE.wait_ge(S["x_kept"], 16 * (L + 1))
            u_high(0, 0)
            u_high(1, 0)
            v_high(0, 0)

            def chunk(s, it, ahead):
                j = it * UV_RING + s
                SE.wait_ge(S["tile_for_act"], j + (base + 1))
                SE.wait_ge(S["gate_applied"], j + (loop_count(L, "gate_applied") + 1 - 2))
                SE.activation(gelu[s % 2], ps[:, (base + s) % 4, 0:T], ACT.Gelu).then_inc(S["gelu_taken"], 1)
                if ahead >= 2:
                    u_high((s + 2) % UV_RING, it + (s + 2) // UV_RING)
                if ahead >= 1:
                    SE.wait_ge(S["experts_used"], j + loop_count(L, "experts_used"))
                    v_high((s + 1) % UV_RING, it + (s + 1) // UV_RING)
            with SE.Fori(0, NI - 1) as it:
                for s in range(UV_RING):
                    chunk(s, it, UV_RING)
            for s in range(UV_RING):
                chunk(s, NI - 1, UV_RING - 1 - s)
            taken["act"] += NKEY

        def top16(vals, val16, idx16, n):
            for r in range(2):
                o = slice(8 * r, 8 * r + 8)
                for g in range(n):
                    VE.max(val16[:, g, o], vals[:, g, :]).then_inc(S["dve_step"], 1)
                VE.wait_ge(S["dve_step"], S.nth(VE, "dve_step", n))
                for g in range(n):
                    VE.max_index(idx16[:, g, o], val16[:, g, o], vals[:, g, :]).then_inc(S["dve_step"], 1)
                VE.wait_ge(S["dve_step"], S.nth(VE, "dve_step", n))
                if r == 0:
                    for g in range(n):
                        VE.match_replace(vals[:, g, :], val16[:, g, o], vals[:, g, :], LOW).then_inc(S["dve_step"], 1)
                    VE.wait_ge(S["dve_step"], S.nth(VE, "dve_step", n))

        def peer_dve(L):
            z = zp
            block_norm_dve(z.rs, mod_cols(L, 4), mod_cols(L, 3))
            VE.tensor_copy(small[:, 1:2], small[:, 0:1]).then_inc(S["expert_ring_free"], 1)
            VE.wait_ge(S["expert_ring_free"], S.nth(VE, "expert_ring_free"))
            VE.wait_ge(S["key_scores"], S.nth(VE, "key_scores", 8))
            iota16 = C["iota"][:, 0:16].unsqueeze(1).unsqueeze(1).to_broadcast([P, PEER_H, 16, 16])
            s2 = z.s.rearrange("p (g w) k -> p g w k", w=2)
            i2 = z.i.rearrange("p (g w) k -> p g w k", w=2)
            full = [P, PEER_H, 16, 16]
            for t in range(TM):
                top16(z.sc[:, t], z.s, z.iu, HP)
                VE.tensor_copy(z.i, z.iu).then_inc(S["dve_step"], 1)
                VE.wait_ge(S["dve_step"], S.nth(VE, "dve_step"))
                VE.tensor_tensor(z.cand.rearrange("p g (a b) -> p g a b", a=16),
                    s2[:, :, 0, :].unsqueeze(3).to_broadcast(full), s2[:, :, 1,
                    :].unsqueeze(2).to_broadcast(full), ALU.add).then_inc(S["dve_step"], 1)
                VE.wait_ge(S["dve_step"], S.nth(VE, "dve_step"))
                top16(z.cand, z.top, z.pu, PEER_H)
                VE.tensor_scalar(z.pv, z.pu, 4, None, ALU.logical_shift_right).then_inc(S["dve_step"], 1)
                VE.wait_ge(S["dve_step"], S.nth(VE, "dve_step"))
                VE.tensor_scalar(z.pu, z.pu, 15, None, ALU.bitwise_and).then_inc(S["dve_step"], 1)
                VE.wait_ge(S["dve_step"], S.nth(VE, "dve_step"))
                VE.tensor_copy(z.pa, z.pv).then_inc(S["dve_step"], 1)
                VE.wait_ge(S["dve_step"], S.nth(VE, "dve_step"))
                VE.tensor_copy(z.pb, z.pu).then_inc(S["dve_step"], 1)
                VE.wait_ge(S["dve_step"], S.nth(VE, "dve_step"))
                VE.tensor_tensor(z.gate, z.top, z.top[:, :, 0:1].to_broadcast([P, PEER_H, 16]),
                    ALU.subtract).then_inc(S["top_shifted"], 1)
                VE.wait_ge(S["top_shifted"], S.nth(VE, "top_shifted"))
                for which, pos, dst in ((0, z.pa, z.e1), (1, z.pb, z.e2)):
                    VE.tensor_tensor(z.eq, pos.unsqueeze(3).to_broadcast(full), iota16,
                        ALU.is_equal).then_inc(S["dve_step"], 1)
                    VE.wait_ge(S["dve_step"], S.nth(VE, "dve_step"))
                    VE.tensor_tensor(z.eq, z.eq, i2[:, :, which, :].unsqueeze(2).to_broadcast(full),
                        ALU.mult).then_inc(S["dve_step"], 1)
                    VE.wait_ge(S["dve_step"], S.nth(VE, "dve_step"))
                    VE.tensor_reduce(dst, z.eq, AX, ALU.add).then_inc(S["dve_step"], 1)
                    VE.wait_ge(S["dve_step"], S.nth(VE, "dve_step"))
                VE.wait_ge(S["top_exp"], S.nth(VE, "top_exp"))
                VE.tensor_reduce(z.sum, z.gate, AX, ALU.add).then_inc(S["dve_step"], 1)
                VE.wait_ge(S["dve_step"], S.nth(VE, "dve_step"))
                VE.reciprocal(z.sum, z.sum).then_inc(S["dve_step"], 1)
                VE.wait_ge(S["dve_step"], S.nth(VE, "dve_step"))
                VE.tensor_tensor(z.gate, z.gate, lastdim(z.sum, 16), ALU.mult).then_inc(S["chosen"], 1)
                VE.wait_ge(S["chosen"], S.nth(VE, "chosen"))
                v = take("dve")[:, 0:3 * P].rearrange("p (w t) -> p w t", w=3)
                VE.tensor_copy(by_token[:, :, t * P:(t + 1) * P], v).then_inc(S["chosen_turned"], 1)
                VE.wait_ge(S["chosen_turned"], S.nth(VE, "chosen_turned"))
            with VE.Fori(0, NG // 4) as it:
                for g in range(4):
                    VE.wait_ge(S["gates_out"], it * 4 + (loop_count(L, "gates_out") + g + 1 - 2))
                    keys = sel[:, bass.ds(it * (4 * GRP) + g * GRP, GRP)]
                    VE.tensor_tensor(hot1[g % 2], C["iota"].unsqueeze(1).to_broadcast([P, GRP, P]),
                                     keys.unsqueeze(2).to_broadcast([P, GRP, P]), ALU.is_equal)
                    for t in range(GRP):
                        col = it * (4 * GRP) + (g * GRP + t)
                        at = lambda w: sel[:, bass.ds(col + w * T, 1)]
                        m = VE.tensor_scalar(hot2[g % 2][:, t, :], C["iota"], at(1), at(2), ALU.is_equal, ALU.mult)
                    m.then_inc(S["hot_ready"], 1)
            VE.wait_ge(S["gates_out"], loop_count(L + 1, "gates_out"))
            for b in range(4):
                signal = "sums_cleared" if b == 3 else "dve_step"
                VE.memset(ps[:, 4 + b, :], 0.0).then_inc(S[signal], 1)
                VE.wait_ge(S[signal], S.nth(VE, signal))
            VE.wait_ge(S["h_high"], S.nth(VE, "h_high"))
            VE.tensor_tensor(h_low_all, ht[:], h_high.bitcast(F32), ALU.subtract).then_inc(S["h_split"], 1)

            def u_low(s, j):
                VE.wait_ge(S["u_high"], j + (loop_count(L, "u_high") + 1))
                u = uv_slot(s)[0]
                VE.tensor_tensor(uv_low(s)[0], u, experts_high[s % 2][:, 0:D].bitcast(F32), ALU.subtract)\
                    .then_inc(S["u_split"], 1)

            def v_low(s, j):
                VE.wait_ge(S["v_high"], j + (loop_count(L, "v_high") + 1))
                v = uv_slot(s)[1]
                VE.tensor_tensor(uv_low(s)[1], v, experts_high[s % 2][:, D:2 * D].bitcast(F32), ALU.subtract)\
                    .then_inc(S["v_split"], 1)

            u_low(0, 0)
            u_low(1, 1)
            v_low(0, 0)

            def chunk(s, j, ahead):
                VE.wait_ge(S["gelu_taken"], j + (loop_count(L, "gelu_taken") + 1))
                VE.tensor_tensor(gelu[s % 2], gelu[s % 2], big[:, bass.ds(j * T, T)], ALU.mult)\
                    .then_inc(S["product_out"], 1)
                VE.wait_ge(S["experts_used"], j + (loop_count(L, "experts_used") + 1 - 2))
                VE.wait_ge(S["product_out"], j + (loop_count(L, "product_out") + 1))
                VE.tensor_copy(prod_high[s % 2], gelu[s % 2]).then_inc(S["product_high"], 1)
                VE.wait_ge(S["product_high"], j + (loop_count(L, "product_high") + 1))
                VE.tensor_tensor(prod_low[s % 2], gelu[s % 2], prod_high[s % 2].bitcast(F32), ALU.subtract)\
                    .then_inc(S["gate_applied"], 1)
                if ahead >= 2:
                    u_low((s + 2) % UV_RING, j + 2)
                if ahead >= 1:
                    v_low((s + 1) % UV_RING, j + 1)
            with VE.Fori(0, NI - 1) as it:
                for s in range(UV_RING):
                    chunk(s, it * UV_RING + s, UV_RING)
            for s in range(UV_RING):
                chunk(s, NKEY - UV_RING + s, UV_RING - 1 - s)
            VE.wait_ge(S["experts_used"], loop_count(L + 1, "experts_used"))
            VE.wait_ge(S["x_back"], 2 * 16 * (L + 1))
            g2 = mod_cols(L, 5)
            for c in range(DC):
                signal = "sums_read" if c % 2 else "dve_step"
                VE.scalar_tensor_tensor(out=x[:, c, :], in0=ps[:, 4 + c // 2, (c % 2) * T:(c % 2 + 1) * T],
                    scalar=g2[:, c:c + 1], in1=x[:, c, :], op0=ALU.mult, op1=ALU.add).then_inc(S[signal], 1)
                VE.wait_ge(S[signal], S.nth(VE, signal))
            VE.tensor_copy(small[:, 1:2], small[:, 0:1]).then_inc(S["x_new"], 1)
            VE.wait_ge(S["x_new"], S.nth(VE, "x_new"))

        def peer_sp(L):
            uv = a["peer_uv"][L].rearrange("j p n -> p j n")
            kept = a["out"].rearrange("(c p) n -> p c n", p=P)
            SP.wait_ge(S["expert_ring_free"], S.nth(SP, "expert_ring_free"))
            SP.dma_start(kept, x).then_inc(S["x_kept"], 16)
            for s in range(UV_RING):
                u, v = uv_slot(s)
                SP.dma_start(u, uv[:, s, 0:D]).then_inc(S[f"u_in_{s}"], 16)
                SP.dma_start(v, uv[:, s, D:2 * D]).then_inc(S[f"v_in_{s}"], 16)
            with SP.Fori(1, NI) as it:
                for s in range(UV_RING):
                    u, v = uv_slot(s)
                    j = it * UV_RING + s
                    SP.wait_ge(S["gelu_taken"], j + (loop_count(L, "gelu_taken") + 1 - UV_RING))
                    SP.dma_start(u, uv[:, bass.ds(j, 1), 0:D].rearrange("p a n -> p (a n)"))\
                        .then_inc(S[f"u_in_{s}"], 16)
                    SP.wait_ge(S["experts_used"], j + (loop_count(L, "experts_used") + 1 - UV_RING))
                    SP.dma_start(v, uv[:, bass.ds(j, 1), D:2 * D].rearrange("p a n -> p (a n)"))\
                        .then_inc(S[f"v_in_{s}"], 16)
            SP.wait_ge(S["x_kept"], 16 * (L + 1))
            SP.wait_ge(S["gelu_taken"], loop_count(L + 1, "gelu_taken"))
            SP.dma_start(consts[:], a["consts"]).then_inc(S["x_back"], 16)
            SP.wait_ge(S["experts_used"], loop_count(L + 1, "experts_used"))
            SP.dma_start(x, kept).then_inc(S["x_back"], 16)
            SP.wait_ge(S["gate_applied"], loop_count(L + 1, "gate_applied"))

        def close_pe():
            block_norm_pe(zm.sq)

        def close_act():
            block_norm_act(zm.sq, zm.rs, "sums_read")

        def close_dve():
            block_norm_dve(zm.rs, V["final_norm"], out=x, name="x_normed")
            VE.tensor_copy(small[:, 1:2], small[:, 0:1]).then_inc(S["x_new"], 1)
            VE.wait_ge(S["x_new"], S.nth(VE, "x_new"))

        def tables_sp():
            SP.wait_ge(S["experts_used"], loop_count(DEPTH, "experts_used"))
            SP.dma_start(hyc, a["hyena_tables"]).then_inc(S["tables_in"], 16)

        hyc = uvr[:, 0:4096]
        h_fwd = hyc[:, 0:1024].rearrange("p (m n) -> p m n", m=TM)
        h_inv = hyc[:, 1024:2048].rearrange("p (k t) -> p k t", k=4)
        h_win = hyc[:, 2048:3072].rearrange("p (m n) -> p m n", m=TM)
        h_winb = hyc[:, 3072:4096].rearrange("p (m n) -> p m n", m=TM)

        def second_places():
            z, r = Z(), Scratch(True)
            r.more = 4096
            z.sq, z.rs6 = r.mat(8), r.mat(6)
            z.rs = z.rs6[:, 0:4, :]
            after_norm = (r.at, r.more)
            z.ya, z.yb, z.yc = r.mat(4), r.mat(4), r.mat(4)
            after_y = (r.at, r.more)
            z.F = r.get(4096).rearrange("p (o w k n) -> p o w k n", o=2, w=2, k=2)
            z.sinv = r.get(8)
            after_f = (r.at, r.more)
            back = lambda to: rewind(r, to)
            z.h1, z.h2, z.ang, z.turns = (r.get(T) for _ in range(4))
            z.P, z.Q, z.A = (r.get(2048).rearrange("p (m o n) -> p m o n", m=TM, o=2) for _ in range(3))
            z.f, z.b = r.get(512), r.get(512)
            back(after_f)
            z.q, z.k = r.mat(4), r.mat(2)
            z.v = r.get(256).rearrange("p (m n) -> p m n", m=TM)
            z.p = [r.mat(2) for _ in range(2)]
            z.pt = [r.mat(2) for _ in range(2)]
            z.st = r.get(8)
            z.tmp = r.mat(2)
            back(after_f)
            z.pad = r.get(12 * 258).rearrange("p (c n) -> p c n", n=258)
            z.u = r.mat(12)
            z.ut = r.get(1024).rearrange("p (m n) -> p m n", m=TM)
            z.U = r.get(2048).rearrange("p (w k n) -> p w k n", w=2, k=2)
            z.Y = r.get(2048).rearrange("p (w k n) -> p w k n", w=2, k=2)
            z.t1 = r.get(1024).rearrange("p (k n) -> p k n", k=2)
            back(after_f)
            z.gq = r.mat(4)
            z.gv = r.get(1024).rearrange("p (m n) -> p m n", m=TM)
            z.go = r.mat(4)
            z.lr = r.get(T)
            z.lg = r.get(1024).rearrange("p (m n) -> p m n", m=TM)
            z.eb, z.ei = ([r.mat(2) for _ in range(2)] for _ in range(2))
            z.kt = r.get(512).rearrange("p (m n) -> p m n", m=TM)
            z.kd = [r.get(512).rearrange("p (m n) -> p m n", m=TM) for _ in range(2)]
            z.dec = r.get(16).rearrange("p (d g c) -> p d g c", d=2, g=2)
            z.aT = [r.get(1024).rearrange("p (g n) -> p g n", g=8) for _ in range(2)]
            z.e = z.aT[0].rearrange("p (m g) n -> p m (g n)", m=TM)
            z.S = [r.get(1024).rearrange("p (g c n) -> p g c n", g=2, c=NCH) for _ in range(2)]
            back(after_y)
            z.gate, z.mix = r.mat(8), r.mat(8)
            z.t2 = r.mat(2)
            z.mix_high, z.mix_low = (r.split(DC * T).rearrange("p (c n) -> p c n", n=T) for _ in range(2))
            back(after_norm)
            z.mn, z.xk, z.xq = r.mat(8), r.mat(8), r.mat(8)
            z.xv = r.get(2048).rearrange("p (m n) -> p m n", m=TM)
            z.xp = [r.mat(2) for _ in range(2)]
            z.xpt = [r.mat(2) for _ in range(2)]
            z.xst = r.get(8)
            back(after_norm)
            parts = lambda v: v.rearrange("p (c n) -> p c n", n=T)
            z.act_high, z.act_low = parts(r.split(D_FF // P * T)), parts(r.split(D_FF // P * T))
            z.h_high = parts(uvr_r[:, 4096:4096 + DC * T])
            z.relu = [parts(uvr[:, 6144 + i * 512:6144 + (i + 1) * 512]) for i in range(2)]
            z.act = [parts(uvr[:, 7168 + i * 512:7168 + (i + 1) * 512]) for i in range(2)]
            return z

        def rewind(r, to):
            r.at, r.more = to

        z2 = second_places()

        def open_dve():
            VE.tensor_copy(small[:, 1:2], small[:, 0:1]).then_inc(S["places_free"], 1)
            VE.wait_ge(S["places_free"], S.nth(VE, "places_free"))

        def filter_pe(L):
            z = z2
            i_, w = next_weight("hyena_net")
            w = w[:, 0, :]
            if L == 0:
                TE.wait_ge(S["tables_in"], 16)
            b = acquire("dve")
            mm(ps[0:64, b, 0:T], w[0:33, FT:FT + 64], C["zpos"][0:33, :], start=True,
                stop=True).then_inc(S["tile_for_dve"], 1)
            frees(b, "net_out")
            TE.wait_ge(S["net_ready"], S.nth(TE, "net_ready"))
            b = acquire("dve")
            mm(ps[0:64, b, 0:T], w[0:64, FT + 64:FT + 128], z.h1[0:64, :], start=True,
                stop=True).then_inc(S["tile_for_dve"], 1)
            frees(b, "net_out")
            TE.wait_ge(S["net_ready"], S.nth(TE, "net_ready"))
            for t in range(TM):
                for n in range(4):
                    b = acquire("dve")
                    mm(ps[:, b, :], z.h2[0:65, t * P:(t + 1) * P], w[0:65, n * 512:(n + 1) * 512], start=True,
                        stop=True).then_inc(S["tile_for_dve"], 1)
                    frees(b, "filter_out")
            last_use(i_, ("filter_out", expected["filter_out"]))
            TE.wait_ge(S["filter_ready"], S.nth(TE, "filter_ready"))
            for o in range(2):
                for part, src in ((0, z.P), (1, z.Q)):
                    for k in range(2):
                        b = acquire("act")
                        for t in range(TM):
                            m = mm(ps[:, b, :], h_fwd[:, t, part * T + k * P:part * T + (k + 1) * P], src[:, t, o, :],
                                   start=(t == 0), stop=(t == TM - 1))
                        m.then_inc(S["tile_for_act"], 1)
                        frees(b, "spectra")
            b = acquire("dve")
            for o in range(2):
                for c in range(4):
                    for t in range(TM):
                        m = mm(ps[:, b, 4 * o + c:4 * o + c + 1], z.A[:, t, o, c * P:(c + 1) * P], C["ones"][:, 0:1],
                               start=(t == 0), stop=(t == TM - 1))
            m.then_inc(S["tile_for_dve"], 1)
            frees(b, "filter_sums")

        def filter_act(L):
            z = z2
            for v in (z.h1, z.h2):
                SE.wait_ge(S["net_angles"], S.nth(SE, "net_angles"))
                SE.activation(v[0:64, :], z.ang[0:64, :], ACT.Sin).then_inc(S["net_ready"], 1)
                SE.wait_ge(S["net_ready"], S.nth(SE, "net_ready"))
            evict_act([z.F[:, o, w, k, :] for o in range(2) for w in range(2) for k in range(2)], frees="spectra", n=8)

        def filter_dve(L):
            z = z2
            VE.memset(z.h2[64:65, :], 1.0).then_inc(S["dve_step"], 1)
            VE.wait_ge(S["dve_step"], S.nth(VE, "dve_step"))
            if L == 0:
                VE.wait_ge(S["tables_in"], 16)
            for i, bias in enumerate(("hy_b1", "hy_b2")):
                t = take("dve")[0:64, 0:T]
                VE.tensor_scalar(z.f[0:64, 0:T], t, V[bias][0:64, L:L + 1],
                    V["hy_freq"][0:64, 2 * L + i:2 * L + i + 1], ALU.add, ALU.mult).then_inc(S["net_out"], 1)
                VE.wait_ge(S["net_out"], S.nth(VE, "net_out"))
                reduced_dve(z.ang[0:64, :], z.f[0:64, 0:T], 0.0, z.turns[0:64, :], "net_angles")
                VE.wait_ge(S["net_ready"], S.nth(VE, "net_ready"))
            for t in range(TM):
                for o in range(2):
                    VE.tensor_tensor(z.f, take("dve"), h_win[:, t, :], ALU.mult).then_inc(S["filter_out"], 1)
                    VE.wait_ge(S["filter_out"], S.nth(VE, "filter_out"))
                    VE.tensor_tensor(z.b, take("dve"), h_winb[:, t, :], ALU.mult).then_inc(S["filter_out"], 1)
                    VE.wait_ge(S["filter_out"], S.nth(VE, "filter_out"))
                    VE.tensor_tensor(z.P[:, t, o, :], z.f, z.b, ALU.add).then_inc(S["dve_step"], 1)
                    VE.wait_ge(S["dve_step"], S.nth(VE, "dve_step"))
                    VE.tensor_tensor(z.Q[:, t, o, :], z.b, z.f, ALU.subtract).then_inc(S["dve_step"], 1)
                    VE.wait_ge(S["dve_step"], S.nth(VE, "dve_step"))
                    VE.scalar_tensor_tensor(out=z.f, in0=z.f, scalar=-1.0, in1=z.f, op0=ALU.mult,
                        op1=ALU.max).then_inc(S["dve_step"], 1)
                    VE.wait_ge(S["dve_step"], S.nth(VE, "dve_step"))
                    VE.scalar_tensor_tensor(out=z.b, in0=z.b, scalar=-1.0, in1=z.b, op0=ALU.mult,
                        op1=ALU.max).then_inc(S["dve_step"], 1)
                    VE.wait_ge(S["dve_step"], S.nth(VE, "dve_step"))
                    signal = "filter_ready" if (t, o) == (1, 1) else "dve_step"
                    VE.tensor_tensor(z.A[:, t, o, :], z.b, z.f, ALU.add).then_inc(S[signal], 1)
                    VE.wait_ge(S[signal], S.nth(VE, signal))
            VE.tensor_scalar(z.sinv, take("dve")[:, 0:8], EPS, None, ALU.add).then_inc(S["filter_sums"], 1)
            VE.wait_ge(S["filter_sums"], S.nth(VE, "filter_sums"))
            VE.reciprocal(z.sinv, z.sinv).then_inc(S["dve_step"], 1)
            VE.wait_ge(S["dve_step"], S.nth(VE, "dve_step"))
            VE.wait_ge(S["spectra"], S.nth(VE, "spectra", 8))

        def att_pe(L):
            z = z2
            fm_linear("att_q", h, DC, 512, "act", "gqa_in", arriving=True)
            fm_linear("att_k", h, DC, 256, "act", "gqa_in")
            tm_linear("att_v", h, DC, P, "act", "gqa_in")
            norm_pe([[c] for c in range(6)], 6, C["blk"], z.sq)
            TE.wait_ge(S["gqa_normed"], S.nth(TE, "gqa_normed"))
            rotate_pe("gqa_in", z.q, 4, C["rot32"])
            rotate_pe("gqa_in", z.k, 2, C["rot32"])
            TE.wait_ge(S["k_rotated"], S.nth(TE, "k_rotated"))

            def scores(i, b):
                r0 = 64 * (i % 2)
                for t in range(TM):
                    m = mm(ps[:, b, t * T:(t + 1) * T], z.q[r0:r0 + 64, i // 2, t * P:(t + 1) * P],
                           z.k[r0:r0 + 64, i // 4, :], start=True, stop=True)
                return m

            def values(i, pt):
                b = acquire("dve")
                value_product(z.v, slice(64 * (i // 4), 64 * (i // 4) + 64), b, 0, pt).then_inc(S["tile_for_dve"], 1)
                frees(b, "o_out")
            attention_pe(8, scores, values, z.p, z.pt)

        def att_act(L):
            z = z2
            SE.wait_ge(S["places_free"], S.nth(SE, "places_free"))
            evict_act(pairs(z.q) + pairs(z.k) + [z.v[:, t, :] for t in range(TM)], frees="gqa_in", n=5)
            SE.activation(z.sq[:, 0:4, :], z.q, ACT.Square).then_inc(S["act_step"], 1)
            SE.wait_ge(S["act_step"], S.nth(SE, "act_step"))
            SE.activation(z.sq[:, 4:6, :], z.k, ACT.Square).then_inc(S["squares"], 1)
            SE.wait_ge(S["squares"], S.nth(SE, "squares"))
            for n, dst in ((2, z.rs6[:, 0:2, :]), (2, z.rs6[:, 2:4, :]), (2, z.rs6[:, 4:6, :])):
                t = take("act")
                SE.activation(dst, t.rearrange("p (c n) -> p c n", n=T), ACT.Ln, scale=1.0 / 64,
                    bias=eps_col).then_inc(S["act_step"], 1)
                SE.wait_ge(S["act_step"], S.nth(SE, "act_step"))
                SE.activation(dst, dst, ACT.Exp, scale=-0.5).then_inc(S["roots"], 1)
                SE.wait_ge(S["roots"], S.nth(SE, "roots"))
            attention_act(8, z.p, z.pt, 64 ** -0.5, z.st)

        def att_dve(L):
            z = z2
            open_dve()
            VE.wait_ge(S["roots"], S.nth(VE, "roots", 3))
            VE.scalar_tensor_tensor(out=z.q, in0=z.q, scalar=V["att_qn"][:, L:L + 1], in1=z.rs6[:, 0:4, :],
                op0=ALU.mult, op1=ALU.mult).then_inc(S["dve_step"], 1)
            VE.wait_ge(S["dve_step"], S.nth(VE, "dve_step"))
            VE.scalar_tensor_tensor(out=z.k, in0=z.k, scalar=V["att_kn"][:, L:L + 1], in1=z.rs6[:, 4:6, :],
                op0=ALU.mult, op1=ALU.mult).then_inc(S["gqa_normed"], 1)
            VE.wait_ge(S["gqa_normed"], S.nth(VE, "gqa_normed"))
            rotate_dve(z.q, 4, C["axcos"], C["axsin"], z.tmp, "dve_step")
            rotate_dve(z.k, 2, C["axcos"], C["axsin"], z.tmp, "k_rotated")

            def out(i):
                VE.tensor_copy(z.ya[64 * (i % 2):64 * (i % 2) + 64, i // 2, :],
                    take("dve")[0:64, 0:T]).then_inc(S["o_out"], 1)
                VE.wait_ge(S["o_out"], S.nth(VE, "o_out"))
            attention_dve(8, z.p, None, 64 ** -0.5, z.st, out)

        def hyena_pe(L):
            z = z2
            fm_linear("hyena_in", h, DC, 1536, "act", "hyena_in")
            for o in range(2):
                TE.wait_ge(S["conv_in"], S.nth(TE, "conv_in"))
                src = z.u[:, 0:4, :]
                for t in range(TM):
                    b = acquire("act")
                    for c in range(4):
                        m = TE.transpose(ps[:, b, c * P:(c + 1) * P], src[:, c, t * P:(t + 1) * P], C["ident"])
                    m.then_inc(S["tile_for_act"], 1)
                    frees(b, "time_major")
                TE.wait_ge(S["time_major"], expected["time_major"])
                for part in range(2):
                    for k in range(2):
                        b = acquire("act")
                        for t in range(TM):
                            m = mm(ps[:, b, :], h_fwd[:, t, part * T + k * P:part * T + (k + 1) * P], z.ut[:, t, :],
                                   start=(t == 0), stop=(t == TM - 1))
                        m.then_inc(S["tile_for_act"], 1)
                        frees(b, "u_spectrum")
                TE.wait_ge(S["y_spectrum"], S.nth(TE, "y_spectrum"))
                for c0 in range(0, 4, 2):
                    b = acquire("dve")
                    for c in (c0, c0 + 1):
                        for k in range(4):
                            m = mm(ps[:, b, (c - c0) * T:(c - c0 + 1) * T], z.Y[:, k // 2, k % 2, c * P:(c + 1) * P],
                                   h_inv[:, k, :], start=(k == 0), stop=(k == 3))
                    m.then_inc(S["tile_for_dve"], 1)
                    frees(b, "convolved")

        def hyena_act(L):
            z = z2
            SE.wait_ge(S["places_free"], S.nth(SE, "places_free"))
            evict_act([z.pad[:, c:c + 2, 1:257] for c in range(0, 12, 2)], frees="hyena_in", n=6)
            for o in range(2):
                evict_act([z.ut[:, t, :] for t in range(TM)], frees="time_major", n=2)
                evict_act([z.U[:, w, k, :] for w in range(2) for k in range(2)], frees="u_spectrum", n=4)

        def hyena_dve(L):
            z = z2
            open_dve()
            VE.memset(z.pad[:, :, 0:1], 0.0).then_inc(S["dve_step"], 1)
            VE.wait_ge(S["dve_step"], S.nth(VE, "dve_step"))
            VE.memset(z.pad[:, :, 257:258], 0.0).then_inc(S["dve_step"], 1)
            VE.wait_ge(S["dve_step"], S.nth(VE, "dve_step"))
            VE.wait_ge(S["hyena_in"], S.nth(VE, "hyena_in", 6))
            w = V["hy_conv"][:, 36 * L:36 * L + 36].rearrange("p (c j) -> p c j", j=3)
            for lo, hi in ((0, 4), (4, 12)):
                for j in range(3):
                    for c in range(lo, hi):
                        src = z.pad[:, c, j:j + T]
                        if j == 0:
                            VE.tensor_scalar(z.u[:, c, :], src, w[:, c, 0:1], None, ALU.mult).then_inc(S["dve_step"], 1)
                        else:
                            VE.scalar_tensor_tensor(out=z.u[:, c, :], in0=src, scalar=w[:, c, j:j + 1],
                                                    in1=z.u[:, c, :], op0=ALU.mult, op1=ALU.add)\
                                .then_inc(S["dve_step"], 1)
                    VE.wait_ge(S["dve_step"], S.nth(VE, "dve_step", hi - lo))
                if lo == 0:
                    VE.tensor_copy(small[:, 1:2], small[:, 0:1]).then_inc(S["conv_in"], 1)
                    VE.wait_ge(S["conv_in"], S.nth(VE, "conv_in"))
            for o in range(2):
                VE.wait_ge(S["u_spectrum"], S.nth(VE, "u_spectrum", 4))
                Ur, Us, Fr, Fi = z.U[:, 0], z.U[:, 1], z.F[:, o, 0], z.F[:, o, 1]
                VE.tensor_tensor(z.t1, Us, Fi, ALU.mult).then_inc(S["dve_step"], 1)
                VE.wait_ge(S["dve_step"], S.nth(VE, "dve_step"))
                VE.tensor_tensor(z.Y[:, 0], Ur, Fr, ALU.mult).then_inc(S["dve_step"], 1)
                VE.wait_ge(S["dve_step"], S.nth(VE, "dve_step"))
                VE.tensor_tensor(z.Y[:, 0], z.Y[:, 0], z.t1, ALU.add).then_inc(S["dve_step"], 1)
                VE.wait_ge(S["dve_step"], S.nth(VE, "dve_step"))
                VE.tensor_tensor(z.t1, Ur, Fi, ALU.mult).then_inc(S["dve_step"], 1)
                VE.wait_ge(S["dve_step"], S.nth(VE, "dve_step"))
                VE.tensor_tensor(z.Y[:, 1], Us, Fr, ALU.mult).then_inc(S["dve_step"], 1)
                VE.wait_ge(S["dve_step"], S.nth(VE, "dve_step"))
                VE.tensor_tensor(z.Y[:, 1], z.Y[:, 1], z.t1, ALU.subtract).then_inc(S["y_spectrum"], 1)
                VE.wait_ge(S["y_spectrum"], S.nth(VE, "y_spectrum"))
                skip = V["hy_skip"][:, 8 * L + 4 * o:8 * L + 4 * o + 4]
                for c0 in (0, 2):
                    t = take("dve")
                    for c in (c0, c0 + 1):
                        v = z.u[:, c, :]
                        VE.tensor_scalar(v, v, skip[:, c:c + 1], None, ALU.mult).then_inc(S["dve_step"], 1)
                        VE.wait_ge(S["dve_step"], S.nth(VE, "dve_step"))
                        signal = "convolved" if c > c0 else "dve_step"
                        VE.scalar_tensor_tensor(out=v, in0=t[:, (c - c0) * T:(c - c0 + 1) * T],
                            scalar=z.sinv[:,
                            4 * o + c:4 * o + c + 1], in1=v, op0=ALU.mult, op1=ALU.add).then_inc(S[signal], 1)
                        VE.wait_ge(S[signal], S.nth(VE, signal))
                if o == 0:
                    VE.tensor_tensor(z.u[:, 0:4, :], z.u[:, 4:8, :], z.u[:, 0:4, :], ALU.mult).then_inc(S["conv_in"],
                        1)
                    VE.wait_ge(S["conv_in"], S.nth(VE, "conv_in"))
                else:
                    VE.tensor_tensor(z.yb, z.u[:, 8:12, :], z.u[:, 0:4, :], ALU.mult).then_inc(S["dve_step"], 1)
                    VE.wait_ge(S["dve_step"], S.nth(VE, "dve_step"))

        def gla_pe(L):
            z = z2
            fm_linear("gla_qk", h, DC, 512, "act", "gla_qk_in")
            tm_linear("gla_v", h, DC, 512, "act", "gla_v_in")
            fm_linear("gla_o", h, DC, 512, "act", "gla_go_in")
            i_, w = next_weight("gla_lr")
            b = acquire("act")
            for k in range(DC):
                m = mm(ps[0:64, b, 0:T], w[:, k, 0:64], h[:, k, :], start=(k == 0), stop=(k == DC - 1))
            m.then_inc(S["tile_for_act"], 1)
            frees(b, "lr_in")
            last_use(i_, ("lr_in", expected["lr_in"]))
            i_, w = next_weight("gla_net")
            TE.wait_ge(S["lr_in"], expected["lr_in"])
            for d in range(2):
                b = acquire("dve")
                for t in range(TM):
                    m = mm(ps[:, b, t * T:(t + 1) * T], z.lr[32 * d:32 * d + 17, t * P:(t + 1) * P],
                           w[32 * d:32 * d + 17, 0, :], start=True, stop=True)
                m.then_inc(S["tile_for_dve"], 1)
                frees(b, "logits")
            last_use(i_, ("logits", expected["logits"]))
            TE.wait_ge(S["gla_qk_in"], expected["gla_qk_in"])
            b = acquire("act")
            for t in range(TM):
                for g in range(2):
                    m = TE.transpose(ps[:, b, t * T + g * P:t * T + (g + 1) * P], z.gq[:, 2 + g, t * P:(t + 1) * P],
                                     C["ident"])
            m.then_inc(S["tile_for_act"], 1)
            frees(b, "gla_kt")
            TE.wait_ge(S["g_ready"], S.nth(TE, "g_ready"))
            for d, mask in ((0, "upto"), (1, "since")):
                b = acquire("act")
                for g in range(2):
                    for t in range(TM):
                        m = mm(ps[:, b, g * T + t * P:g * T + (t + 1) * P],
                               z.lg[:, t, d * T + g * P:d * T + (g + 1) * P], C[mask], start=True, stop=True)
                m.then_inc(S["tile_for_act"], 1)
                frees(b, "cum_out")
            for d, mask in ((0, "later"), (1, "before")):
                b = acquire("act")
                for t in range(TM):
                    m = mm(ps[:, b, t * T:(t + 1) * T], C[mask], z.lg[:, t, d * T:(d + 1) * T], start=True, stop=True)
                m.then_inc(S["tile_for_act"], 1)
                frees(b, "rem_out")
            TE.wait_ge(S["gla_scaled"], S.nth(TE, "gla_scaled"))
            TE.wait_ge(S["gla_v_in"], expected["gla_v_in"])
            for d in range(2):
                for r0 in (0, 64):
                    b = acquire("dve")
                    for t in range(TM):
                        for g in range(2):
                            m = mm(ps[:, b, (2 * t + g) * P:(2 * t + g + 1) * P],
                                   z.ei[d][r0:r0 + 64, g, t * P:(t + 1) * P], z.eb[d][r0:r0 + 64, g, t * P:(t + 1) * P],
                                   start=True, stop=True)
                    m.then_inc(S["tile_for_dve"], 1)
                    frees(b, "intra")
            for d in range(2):
                for odd in ((1, 0) if d == 0 else (0, 1)):
                    b = acquire("dve")
                    rows = slice(64 * odd, 64 * odd + 64)
                    for g in range(2):
                        for t in range(TM):
                            for i in (2 * g, 2 * g + 1):
                                r0 = 64 * (i % 2)
                                m = mm(ps[r0:r0 + 64, b, (2 * g + t) * P:(2 * g + t + 1) * P],
                                       z.kd[d][rows, t, i * 64:(i + 1) * 64], z.gv[rows, t, i * P:(i + 1) * P],
                                       start=True, stop=True)
                    m.then_inc(S["tile_for_dve"], 1)
                    frees(b, "state_in")
            TE.wait_ge(S["gla_states"], S.nth(TE, "gla_states"))
            for i in range(GH):
                r0, g = 64 * (i % 2), i // 2
                b = acquire("act")
                for t in range(TM):
                    for d in range(2):
                        mm(ps[:, b, t * P:(t + 1) * P], z.gv[:, t, i * P:(i + 1) * P], z.aT[d][:, 4 * t + i, :],
                           start=(d == 0), stop=False)
                    for c in (2 * t, 2 * t + 1):
                        for d in range(2):
                            m = mm(ps[:, b, c * GC:(c + 1) * GC], z.S[d][r0:r0 + 64, g, c, :],
                                   z.eb[d][r0:r0 + 64, g, c * GC:(c + 1) * GC], start=False,
                                   stop=(c % 2 == 1 and d == 1))
                m.then_inc(S["tile_for_act"], 1)
                frees(b, "gla_out")
            norm_pe([[c] for c in range(4)], 4, C["ones"], z.sq)

        def gla_act(L):
            z = z2
            SE.wait_ge(S["places_free"], S.nth(SE, "places_free"))
            evict_act(pairs(z.gq), frees="gla_qk_in", n=2)
            evict_act([z.gv[:, t, :] for t in range(TM)], frees="gla_v_in", n=2)
            evict_act(pairs(z.go), ACT.Silu, frees="gla_go_in", n=2)
            SE.wait_ge(S["lr_ones"], S.nth(SE, "lr_ones"))
            t = take("act")
            SE.activation(z.lr[0:16, :], t[0:16, 0:T], ACT.Copy).then_inc(S["act_step"], 1)
            SE.wait_ge(S["act_step"], S.nth(SE, "act_step"))
            SE.activation(z.lr[32:48, :], t[32:48, 0:T], ACT.Copy).then_inc(S["lr_in"], 1)
            SE.wait_ge(S["lr_in"], S.nth(SE, "lr_in"))
            evict_act([z.kt.rearrange("p m n -> p (m n)")], frees="gla_kt")
            SE.wait_ge(S["logit_abs"], S.nth(SE, "logit_abs"))
            SE.activation(z.e, z.e, ACT.Exp, scale=-1.0).then_inc(S["act_step"], 1)
            SE.wait_ge(S["act_step"], S.nth(SE, "act_step"))
            SE.activation(z.e, z.e, ACT.Ln, bias=1.0).then_inc(S["logit_ln"], 1)
            SE.wait_ge(S["logit_ln"], S.nth(SE, "logit_ln"))
            for d in range(2):
                t = take("act").rearrange("p (g n) -> p g n", g=2)
                SE.activation(z.eb[d], t, ACT.Exp).then_inc(S["act_step"], 1)
                SE.wait_ge(S["act_step"], S.nth(SE, "act_step"))
                SE.activation(z.ei[d], t, ACT.Exp, scale=-1.0).then_inc(S["cum_out"], 1)
                SE.wait_ge(S["cum_out"], S.nth(SE, "cum_out"))
            evict_act([z.kd[d] for d in range(2)], ACT.Exp, frees="rem_out", n=2)
            evict_act([z.yc[:, i, :] for i in range(GH)], frees="gla_out", n=4)
            norm_act(z.yc, z.sq[:, 0:4, :], z.rs, 4, 128.0)

        def gla_dve(L):
            z = z2
            VE.memset(z.lr[0:64, :], 1.0).then_inc(S["lr_ones"], 1)
            VE.wait_ge(S["lr_ones"], S.nth(VE, "lr_ones"))
            open_dve()
            for d in range(2):
                VE.tensor_copy(z.e[:, :, d * T:(d + 1) * T],
                    take("dve").rearrange("p (m n) -> p m n", m=TM)).then_inc(S["logits"], 1)
                VE.wait_ge(S["logits"], S.nth(VE, "logits"))
            VE.tensor_scalar(z.lg, z.e, 0.0, None, ALU.min).then_inc(S["dve_step"], 1)
            VE.wait_ge(S["dve_step"], S.nth(VE, "dve_step"))
            VE.scalar_tensor_tensor(out=z.e, in0=z.e, scalar=-1.0, in1=z.e, op0=ALU.mult,
                op1=ALU.max).then_inc(S["dve_step"], 1)
            VE.wait_ge(S["dve_step"], S.nth(VE, "dve_step"))
            VE.tensor_scalar(small[:, 2:3], small[:, 0:1], 1.0, None, ALU.mult).then_inc(S["logit_abs"], 1)
            VE.wait_ge(S["logit_abs"], S.nth(VE, "logit_abs"))
            VE.wait_ge(S["logit_ln"], S.nth(VE, "logit_ln"))
            VE.tensor_tensor(z.lg, z.lg, z.e, ALU.subtract).then_inc(S["dve_step"], 1)
            VE.wait_ge(S["dve_step"], S.nth(VE, "dve_step"))
            VE.tensor_scalar(z.lg, z.lg, 1.0 / 16, None, ALU.mult).then_inc(S["g_ready"], 1)
            VE.wait_ge(S["g_ready"], S.nth(VE, "g_ready"))
            VE.wait_ge(S["cum_out"], S.nth(VE, "cum_out", 2))
            for d in range(2):
                v = z.eb[d].rearrange("p g (c n) -> p g c n", n=GC)
                VE.tensor_copy(z.dec[:, d].unsqueeze(3),
                    v[:, :, :, GC - 1:GC] if d == 0 else v[:, :, :, 0:1]).then_inc(S["dve_step"], 1)
                VE.wait_ge(S["dve_step"], S.nth(VE, "dve_step"))
                VE.scalar_tensor_tensor(out=z.eb[d], in0=z.gq[:, 0:2, :], scalar=64 ** -0.5, in1=z.eb[d],
                    op0=ALU.mult, op1=ALU.mult).then_inc(S["dve_step"], 1)
                VE.wait_ge(S["dve_step"], S.nth(VE, "dve_step"))
                VE.tensor_tensor(z.ei[d], z.ei[d], z.gq[:, 2:4, :], ALU.mult).then_inc(S["dve_step"], 1)
                VE.wait_ge(S["dve_step"], S.nth(VE, "dve_step"))
            VE.wait_ge(S["gla_kt"], S.nth(VE, "gla_kt"))
            VE.wait_ge(S["rem_out"], S.nth(VE, "rem_out", 2))
            for d in range(2):
                signal = "gla_scaled" if d else "dve_step"
                VE.tensor_tensor(z.kd[d], z.kd[d], z.kt, ALU.mult).then_inc(S[signal], 1)
                VE.wait_ge(S[signal], S.nth(VE, signal))
            for d in range(2):
                for w in range(2):
                    dst = z.aT[d].rearrange("p (t g w) n -> p w t g n", t=TM, w=2)[:, w]
                    VE.tensor_tensor(dst, take("dve").rearrange("p (t g n) -> p t g n", t=TM, g=2),
                        C["upto" if d == 0 else "later"].unsqueeze(1).unsqueeze(1).to_broadcast([P, TM, 2,
                        P]), ALU.mult).then_inc(S["intra"], 1)
                    VE.wait_ge(S["intra"], S.nth(VE, "intra"))
            for d in range(2):
                order = range(NCH) if d == 0 else range(NCH - 1, -1, -1)
                order = list(order)
                VE.memset(z.S[d][:, :, order[0], :], 0.0).then_inc(S["dve_step"], 1)
                VE.wait_ge(S["dve_step"], S.nth(VE, "dve_step"))
                v = {odd: take("dve") for odd in ((1, 0) if d == 0 else (0, 1))}
                for g in range(2):
                    for c, nx in zip(order, order[1:]):
                        o = (2 * g + c // 2) * P
                        signal = "state_in" if g == 1 and nx in order[-2:] else "dve_step"
                        VE.scalar_tensor_tensor(out=z.S[d][:, g, nx, :], in0=z.S[d][:, g, c, :],
                            scalar=z.dec[:, d, g, c:c + 1], in1=v[c % 2][:,
                            o:o + P], op0=ALU.mult, op1=ALU.add).then_inc(S[signal], 1)
                        VE.wait_ge(S[signal], S.nth(VE, signal))
            VE.tensor_scalar(small[:, 2:3], small[:, 0:1], 1.0, None, ALU.mult).then_inc(S["gla_states"], 1)
            VE.wait_ge(S["gla_states"], S.nth(VE, "gla_states"))
            norm_dve(z.rs, 4)
            VE.scalar_tensor_tensor(out=z.yc, in0=z.yc, scalar=V["gla_on"][:, L:L + 1], in1=z.rs, op0=ALU.mult,
                op1=ALU.mult).then_inc(S["dve_step"], 1)
            VE.wait_ge(S["dve_step"], S.nth(VE, "dve_step"))
            VE.tensor_tensor(z.yc, z.yc, z.go, ALU.mult).then_inc(S["dve_step"], 1)
            VE.wait_ge(S["dve_step"], S.nth(VE, "dve_step"))

        def mix_pe(L):
            z = z2
            for i, y in enumerate((z.ya, z.yb, z.yc)):
                split_linear("gate", z.h_high, h_low, DC, D, "act", "gate_in", first="x_split" if i == 0 else None)
                if i == 0:
                    TE.wait_ge(S["branches_ready"], S.nth(TE, "branches_ready"))
                fm_linear("branch", y, 4, D, "dve", "branch_in")
            split_linear("mix_out", z.mix_high, z.mix_low, DC, D, "dve", "residual_in", first="mix_split")

        def mix_act(L):
            z = z2
            SE.wait_ge(S["h_over"], S.nth(SE, "h_over"))
            split_high(idle=True)
            split_high(idle=True)
            split_h_act(z.h_high, whole=True)
            for q in range(12):
                if q % 4 == 0:
                    SE.wait_ge(S["gate_place_free"], S.nth(SE, "gate_place_free"))
                evict_act([z.gate[:, 2 * (q % 4):2 * (q % 4) + 2, :]], ACT.Sigmoid, frees="gate_in")
                if q < 11:
                    split_high()
            for j in range(4):
                SE.wait_ge(S["mixed"], S.nth(SE, "mixed"))
                pair = slice(2 * j, 2 * j + 2)
                SE.activation(z.mix_high[:, pair, :], z.mix[:, pair, :], ACT.Copy).then_inc(S["mix_high"], 1)
                SE.wait_ge(S["mix_high"], S.nth(SE, "mix_high"))
            for _ in range(3):
                split_high()

        def mix_dve(L):
            z = z2
            VE.tensor_copy(small[:, 1:2], small[:, 0:1]).then_inc(S["branches_ready"], 1)
            VE.wait_ge(S["branches_ready"], S.nth(VE, "branches_ready"))
            VE.tensor_copy(small[:, 1:2], small[:, 0:1]).then_inc(S["h_over"], 1)
            VE.wait_ge(S["h_over"], S.nth(VE, "h_over"))
            split_low()
            split_low()
            split_h_dve(z.h_high)
            for i in range(3):
                VE.tensor_copy(small[:, 1:2], small[:, 0:1]).then_inc(S["gate_place_free"], 1)
                VE.wait_ge(S["gate_place_free"], S.nth(VE, "gate_place_free"))
                for _ in range(4 if i < 2 else 3):
                    split_low()
                for j in range(4):
                    VE.wait_ge(S["gate_in"], S.nth(VE, "gate_in"))
                    t = take("dve").rearrange("p (c n) -> p c n", c=2)
                    g, m = z.gate[:, 2 * j:2 * j + 2, :], z.mix[:, 2 * j:2 * j + 2, :]
                    if i == 0:
                        VE.tensor_tensor(m, t, g, ALU.mult).then_inc(S["branch_in"], 1)
                        VE.wait_ge(S["branch_in"], S.nth(VE, "branch_in"))
                    else:
                        VE.tensor_tensor(z.t2, t, g, ALU.mult).then_inc(S["branch_in"], 1)
                        VE.wait_ge(S["branch_in"], S.nth(VE, "branch_in"))
                        signal = "mixed" if i == 2 else "dve_step"
                        VE.tensor_tensor(m, m, z.t2, ALU.add).then_inc(S[signal], 1)
                        VE.wait_ge(S[signal], S.nth(VE, signal))
            for j in range(4):
                VE.wait_ge(S["mix_high"], S.nth(VE, "mix_high"))
                pair = slice(2 * j, 2 * j + 2)
                VE.tensor_tensor(z.mix_low[:, pair, :], z.mix[:, pair, :], z.mix_high[:, pair, :].bitcast(F32),
                                 ALU.subtract).then_inc(S["mix_split"], 1)
            for _ in range(3):
                split_low()
            residual_dve(None)

        def cross_pe(L):
            z = z2
            i_, mem = next_weight("mem")
            norm_pe([list(range(DC))], DC, C["ones"], z.sq)
            TE.wait_ge(S["mem_ready"], S.nth(TE, "mem_ready"))
            last_use(i_, ("mem_ready", L + 1))
            fm_linear("x_k", z.mn, DC, D, "act", "xk_in")
            tm_linear("x_v", z.mn, DC, D, "act", "xk_in")
            norm_pe([[2 * i, 2 * i + 1] for i in range(4)], 8, C["ones"], z.sq)
            block_norm_pe(z.sq)
            fm_linear("x_q", h, DC, D, "act", "xq_in", arriving=True)
            norm_pe([[2 * i, 2 * i + 1] for i in range(4)], 8, C["ones"], z.sq)
            TE.wait_ge(S["xq_ready"], S.nth(TE, "xq_ready"))

            def scores(i, b):
                for t in range(TM):
                    for k in range(2):
                        m = mm(ps[:, b, t * T:(t + 1) * T], z.xq[:, 2 * i + k, t * P:(t + 1) * P],
                               z.xk[:, 2 * i + k, :], start=(k == 0), stop=(k == 1))
                return m

            def values(i, pt):
                b = acquire("dve")
                for k in range(2):
                    m = value_product(z.xv, slice(i * T + k * P, i * T + (k + 1) * P), b, k, pt)
                m.then_inc(S["tile_for_dve"], 1)
                frees(b, "o_out")
            attention_pe(4, scores, values, z.xp, z.xpt)
            TE.wait_ge(S["o_out"], expected["o_out"])
            fm_linear("x_o", h, DC, D, "dve", "residual_in")

        def mem_tile(L):
            i = [i for i, w in enumerate(weights) if w[0] == "mem"][L]
            return i, ring_slot(i)[:, 0:DC * T].rearrange("p (c n) -> p c n", c=DC)

        def cross_act(L):
            z = z2
            i, mem = mem_tile(L)
            SE.wait_ge(S[f"weights_in_{i % RING}"], weights_in(i))
            SE.wait_ge(S["x_new"], S.nth(SE, "x_new"))
            SE.wait_ge(S["residual_in"], S.nth(SE, "residual_in", 4))
            norm_act(mem, z.sq, z.rs, 1, D)
            evict_act(pairs(z.xk) + [z.xv[:, t, n:n + 512] for n in (0, 512) for t in range(TM)], frees="xk_in", n=8)
            norm_act(z.xk, z.sq, z.rs, 4, 256.0)
            SE.wait_ge(S["xk_ready"], S.nth(SE, "xk_ready"))
            block_norm_act(z.sq, z.rs)
            evict_act(pairs(z.xq), frees="xq_in", n=4)
            norm_act(z.xq, z.sq, z.rs, 4, 256.0)
            attention_act(4, z.xp, z.xpt, 256 ** -0.5, z.xst)

        def cross_dve(L):
            z = z2
            i, mem = mem_tile(L)
            norm_dve(z.rs, 1)
            for c in range(DC):
                signal = "mem_ready" if c == DC - 1 else "dve_step"
                VE.scalar_tensor_tensor(out=z.mn[:, c, :], in0=mem[:, c, :],
                    scalar=V["ln_mem"][:, 8 * L + c:8 * L + c + 1], in1=z.rs[:, 0,
                    :], op0=ALU.mult, op1=ALU.mult).then_inc(S[signal], 1)
                VE.wait_ge(S[signal], S.nth(VE, signal))
            for dst, gain, name in ((z.xk, "x_kn", "xk_ready"), (z.xq, "x_qn", "xq_ready")):
                if name == "xq_ready":
                    block_norm_dve(z.rs, V["ln_x"][:, 8 * L:8 * L + 8])
                norm_dve(z.rs, 4)
                for k in range(2):
                    d = dst.rearrange("p (i k) n -> p k i n", k=2)[:, k]
                    signal = name if k else "dve_step"
                    VE.scalar_tensor_tensor(out=d, in0=d, scalar=V[gain][:, 2 * L + k:2 * L + k + 1], in1=z.rs,
                        op0=ALU.mult, op1=ALU.mult).then_inc(S[signal], 1)
                    VE.wait_ge(S[signal], S.nth(VE, signal))

            def out(i):
                VE.tensor_copy(h[:, 2 * i:2 * i + 2, :],
                    take("dve").rearrange("p (c n) -> p c n", c=2)).then_inc(S["o_out"], 1)
                VE.wait_ge(S["o_out"], S.nth(VE, "o_out"))
            attention_dve(4, z.xp, None, 256 ** -0.5, z.xst, out)
            residual_dve(None)

        NF = D_FF // P // 2

        def mlp_pe(L):
            z = z2
            block_norm_pe(z.sq)
            split_linear("mlp1", z.h_high, h_low, DC, D_FF, "act", "relu_out", first="x_split")
            split_linear("mlp2", z.act_high, z.act_low, D_FF // P, D, "dve", "residual_in", first="act_split")

        def mlp_act(L):
            z = z2
            split_high(idle=True)
            split_high(idle=True)
            block_norm_act(z.sq, z.rs, "residual_in")
            split_h_act(z.h_high)
            for p in range(2, 2 * NF + 2):
                if p < 2 * NF:
                    split_high()
                if p - 2 < NF:
                    i = p - 2
                    SE.activation(z.relu[i % 2], take("act").rearrange("p (c n) -> p c n", c=2),
                        ACT.Relu).then_inc(S["relu_out"], 1)
                    SE.wait_ge(S["relu_out"], S.nth(SE, "relu_out"))
                    if i >= 2:
                        SE.wait_ge(S["act_split"], NF * L + i - 1)
                    SE.activation(z.act[i % 2], z.relu[i % 2], ACT.Square).then_inc(S["act_step"], 1)
                    SE.wait_ge(S["act_step"], S.nth(SE, "act_step"))
                    SE.activation(z.act_high[:, 2 * i:2 * i + 2, :], z.act[i % 2], ACT.Copy).then_inc(S["act_high"],
                        1)
                    SE.wait_ge(S["act_high"], S.nth(SE, "act_high"))

        def mlp_dve(L):
            z = z2
            split_low()
            split_low()
            block_norm_dve(z.rs, V["ln_mlp"][:, 8 * L:8 * L + 8], name="h_part")
            split_h_dve(z.h_high)
            for p in range(2, 2 * NF + 3):
                if p < 2 * NF:
                    split_low()
                if p - 2 < NF:
                    i = p - 2
                    VE.wait_ge(S["act_high"], S.nth(VE, "act_high"))
                    VE.tensor_tensor(z.act_low[:, 2 * i:2 * i + 2, :], z.act[i % 2],
                                     z.act_high[:, 2 * i:2 * i + 2, :].bitcast(F32), ALU.subtract)\
                        .then_inc(S["act_split"], 1)
                elif p - NF >= 6 and (p - NF) % 4 == 2:
                    residual_bank((p - NF) // 4 - 1)
            x_complete()

        def layer_pe(L):
            filter_pe(L)
            block_norm_pe(z2.sq)
            att_pe(L)
            hyena_pe(L)
            gla_pe(L)
            mix_pe(L)
            cross_pe(L)
            mlp_pe(L)

        def layer_act(L):
            SE.wait_ge(S["x_new"], S.nth(SE, "x_new"))
            if L > 0:
                SE.wait_ge(S["residual_in"], S.nth(SE, "residual_in", 4))
            filter_act(L)
            block_norm_act(z2.sq, z2.rs)
            att_act(L)
            hyena_act(L)
            gla_act(L)
            mix_act(L)
            cross_act(L)
            mlp_act(L)

        def layer_dve(L):
            filter_dve(L)
            block_norm_dve(z2.rs, V["ln_mix"][:, 8 * L:8 * L + 8])
            att_dve(L)
            hyena_dve(L)
            gla_dve(L)
            mix_dve(L)
            cross_dve(L)
            mlp_dve(L)

        plan_mod(0, 0, 4)
        plan_hybrid()
        plan_peer(0)
        plan_mla()
        plan_peer(1)
        before.setdefault(len(weights), []).append(tables_sp)
        for L in range(DEPTH):
            plan_second(L)
        stage = lambda k: upto >= k

        block = ctx.enter_context(nc.Block())

        @block.tensor
        def _(pe):
            for name, n in CREDITS.items():
                pe.sem_inc(S[name], n)
            mod_pe(0, 0, 4)
            if stage(1):
                hybrid_pe()
            if stage(2):
                peer_pe(0)
            if stage(3):
                mla_pe()
            if stage(4):
                peer_pe(1)
            if stage(5):
                close_pe()
            for L in range(DEPTH):
                if stage(6 + L):
                    layer_pe(L)

        @block.scalar
        def _(act):
            mod_act(0, 0, 4)
            if stage(1):
                hybrid_act()
            if stage(2):
                peer_act(0)
            if stage(3):
                mla_act()
            if stage(4):
                peer_act(1)
            if stage(5):
                close_act()
            for L in range(DEPTH):
                if stage(6 + L):
                    layer_act(L)

        @block.vector
        def _(dve):
            dve.wait_ge(S["inputs_in"], 16 * 6)
            VE.memset(small[:, 0:2], EPS).then_inc(S["dve_step"], 1)
            VE.wait_ge(S["dve_step"], S.nth(VE, "dve_step"))
            VE.memset(small[:, 2:8], 0.0).then_inc(S["inputs_ready"], 1)
            VE.wait_ge(S["inputs_ready"], S.nth(VE, "inputs_ready"))
            mod_dve(0, 0, 4)
            VE.tensor_copy(small[:, 1:2], small[:, 0:1]).then_inc(S["x_new"], 1)
            VE.wait_ge(S["x_new"], S.nth(VE, "x_new"))
            if stage(1):
                hybrid_dve()
            if stage(2):
                peer_dve(0)
            if stage(3):
                mod_dve(1, 0, 12)
                mla_dve()
            if stage(4):
                peer_dve(1)
            if stage(5):
                close_dve()
            for L in range(DEPTH):
                if stage(6 + L):
                    layer_dve(L)
            VE.tensor_copy(small[:, 1:2], small[:, 0:1]).then_inc(S["x_final"], 1)
            VE.wait_ge(S["x_final"], S.nth(VE, "x_final"))

        @block.sync
        def _(sp):
            for dst, src in ((x, a["xT"].rearrange("(c p) n -> p c n", p=P)), (consts[:], a["consts"]),
                             (vecs[:], a["vecs"]), (pos_in, a["positions"].partition_broadcast(P)),
                             (zh.al[:, 0:4], a["gdn_a_log"].partition_broadcast(P)),
                             (zh.al[:, 4:8], a["gdn_dt_bias"].partition_broadcast(P))):
                sp.dma_start(dst, src).then_inc(S["inputs_in"], 16)
            for i, (name, src, kc, n, rows, pieces) in enumerate(weights):
                for f in before.get(i, []):
                    if (f is not tables_sp and i <= use[0]) or i < use[0]:
                        f()
                if i >= use[0]:
                    break
                if i - RING >= 0 and i - RING in weight_done:
                    sp.wait_ge(S[weight_done[i - RING][0]], weight_done[i - RING][1])
                if pieces is None:
                    dst = ring_slot(i)[:, 0:kc * n].rearrange("p (c n) -> p c n", c=kc)
                    sp.dma_start(dst, src).then_inc(S[f"weights_in_{i % RING}"], 16)
                else:
                    for r0, nr, c0, nc_, piece in pieces:
                        sp.dma_start(ring_slot(i)[r0:r0 + nr, c0:c0 + nc_], piece)\
                            .then_inc(S[f"weights_in_{i % RING}"], 16)
            sp.wait_ge(S["x_final"], 1)
            sp.dma_start(a["out"].rearrange("(c p) n -> p c n", p=P), x).then_inc(S["out_written"], 16)
            sp.wait_ge(S["out_written"], 16)


def laid_out(i):
    f = lambda n: np.asarray(i[n])
    col = lambda v: np.asarray(v).reshape(-1, P).T
    pad = lambda v: np.concatenate([np.asarray(v).reshape(-1, 64)] * 2, 1).T
    w_uq = f("mla_w_uq")[0].reshape(512, MLA_H, 192)
    w_ukv = f("mla_w_ukv")[0].reshape(256, MLA_H, 256)
    w_in = f("w_in_2")
    u = f("peer_u").reshape(DEPTH, NKEY, NKEY, DC, P).transpose(0, 2, 4, 3, 1).reshape(DEPTH, NKEY, P, D)
    v = f("peer_v").reshape(DEPTH, NKEY, NKEY, D).transpose(0, 2, 1, 3)
    vec = dict(
        cond=col(f("c")), norm_mix=col(f("norm_mix")), norm_ffn=col(f("norm_ffn")), mod_b=col(f("mod_b")),
        gdn_conv=f("gdn_conv")[0].reshape(4, 12, P).transpose(2, 1, 0).reshape(P, 48),
        gdn_o_norm=col(f("gdn_o_norm")), q_norm=col(f("mla_q_norm")), kv_norm=col(f("mla_kv_norm")),
        final_norm=col(f("final_norm")), ln_mix=col(f("ln_mix_2")), ln_x=col(f("ln_x_2")),
        ln_mem=col(f("ln_mem_2")), ln_mlp=col(f("ln_mlp_2")), att_qn=pad(f("attn_qnorm_2")),
        att_kn=pad(f("attn_knorm_2")), x_qn=col(f("x_qnorm_2")), x_kn=col(f("x_knorm_2")),
        hy_conv=f("hy_conv_2").reshape(DEPTH, 3, 12, P).transpose(3, 0, 2, 1).reshape(P, 72),
        hy_skip=col(f("hy_skip_2")), gla_on=col(f("gla_onorm_2")), hy_b1=pad(f("hy_b1_2")),
        hy_b2=pad(f("hy_b2_2")), hy_freq=pad(f("hy_freq_2")))
    consts, hyena = constant_tables()
    out = dict(
        xT=f("x")[0].T, memT=f("mem_2")[0].T, positions=f("positions")[0:1],
        vecs=np.concatenate([vec[k] for k in VEC_COLS], 1),
        consts=np.concatenate([consts[k] for k in CONST_COLS], 1), hyena_tables=hyena,
        gdn_a_log=f("gdn_a_log"), gdn_dt_bias=f("gdn_dt_bias"),
        peer_uv=np.concatenate([u, v], 3),
        sub_keys=f("peer_sub_keys").transpose(0, 1, 2, 4, 3).reshape(DEPTH, HP * P, NKEY),
        mla_kr=np.concatenate([f("mla_w_in")[0][:, 768:832]] * 2, 1),
        mla_uqn=w_uq[:, :, :128].reshape(512, -1), mla_uqr=w_uq[:, :, 128:].reshape(512, -1),
        mla_ukn=w_ukv[:, :, :128].reshape(256, -1), mla_uv=w_ukv[:, :, 128:].reshape(256, -1),
        att_kdup=np.concatenate([w_in[:, :, 512:576]] * 2 + [w_in[:, :, 576:640]] * 2, 2),
        gla_lrdup=np.concatenate([w_in[:, :, 3840:3856]] * 2 + [w_in[:, :, 3856:3872]] * 2, 2))
    for k in ("mod_w", "hy_w_in", "hy_w_out", "mla_w_in", "mla_w_out", "peer_w_q", "w_in_2", "hy_w1_2", "hy_w2_2",
              "hy_w3_2", "hy_b3_2", "gla_w_lr_2", "gla_b_lr_2", "w_br_attn_2", "w_br_hyena_2", "w_br_gla_2",
              "w_out_2", "x_wq_2", "x_wk_2", "x_wv_2", "x_wo_2", "mlp_w1_2", "mlp_w2_2"):
        out[k] = f(k)
    return {k: np.ascontiguousarray(v) for k, v in out.items()}


def kernel(**inputs):
    import concourse.bacc as bacc
    from concourse.bass_utils import run_bass_kernel_spmd

    nc = bacc.Bacc("TRN2", target_bir_lowering=False, num_devices=1)
    arrays = laid_out(inputs)
    aps = {k: nc.dram_tensor(k, v.shape, mybir.dt.from_np(v.dtype), kind="ExternalInput").ap()
           for k, v in arrays.items()}
    aps["out"] = nc.dram_tensor("out", (D, T), F32, kind="ExternalOutput").ap()
    two_blocks(nc, aps)
    r = run_bass_kernel_spmd(nc, [arrays], core_ids=[0])
    return np.ascontiguousarray(r.results[0]["out"].T).reshape(1, T, D)
```
